# Optimizing a Trainium2 kernel written in Bass

```python
import jax, jax.numpy as jnp
from jax import lax
import numpy as np

D_MODEL = 2048
BATCH = 1
SEQ = 256
DEPTH = 1

MEM_LEN = 256
HEAD_DIM = 64
RWKV_WIDTH = D_MODEL // 2
RWKV_HEADS = RWKV_WIDTH // HEAD_DIM
DECAY_LORA = max(32, int(round(1.8 * RWKV_WIDTH ** 0.5 / 32)) * 32)
AAA_LORA = max(32, int(round(1.8 * RWKV_WIDTH ** 0.5 / 32)) * 32)
GATE_LORA = max(32, int(round(0.6 * RWKV_WIDTH ** 0.8 / 32)) * 32)
GN_EPS = 64e-5
SWA_WIDTH = D_MODEL - RWKV_WIDTH
SWA_Q_HEADS = SWA_WIDTH // HEAD_DIM
SWA_KV_HEADS = max(1, SWA_Q_HEADS // 8)
SWA_GROUP = SWA_Q_HEADS // SWA_KV_HEADS
WINDOW = 128
BLOCK = 128
ROPE_THETA = 10000.0
SHIFT_COLS = 3 * RWKV_WIDTH + DECAY_LORA + AAA_LORA + GATE_LORA
SWA_COLS = SWA_WIDTH + 2 * SWA_KV_HEADS * HEAD_DIM
IN_COLS = SHIFT_COLS + SWA_COLS
XATTN_HEADS = 4
XATTN_HEAD_DIM = D_MODEL // XATTN_HEADS
D_FF = ((8 * D_MODEL // 3 + 255) // 256) * 256
RMS_EPS = 1e-6
NEG_INF = -1e30

kernel_name = 'hymba_rwkv7_swa_sink_macaron_layer'

def _rmsnorm(x, g):
    xf = x.astype(jnp.float32)
    y = xf * lax.rsqrt(jnp.mean(xf * xf, axis=-1, keepdims=True) + RMS_EPS)
    return (y * g.astype(jnp.float32)).astype(x.dtype)

def _swiglu(h, w_gate, w_up, w_down):
    return (jax.nn.silu(h @ w_gate) * (h @ w_up)) @ w_down

def _rope(t, pos):
    hd = t.shape[-1]
    inv_freq = ROPE_THETA ** (-jnp.arange(0, hd, 2, dtype=jnp.float32) / hd)
    ang = pos[:, None] * inv_freq[None, :]
    cos = jnp.cos(ang)[None, :, None, :]
    sin = jnp.sin(ang)[None, :, None, :]
    tf = t.astype(jnp.float32)
    t1, t2 = tf[..., : hd // 2], tf[..., hd // 2:]
    return jnp.concatenate([t1 * cos - t2 * sin, t2 * cos + t1 * sin], axis=-1).astype(t.dtype)

def _rwkv7_time_mix(z, w0, decay_up, a0, aaa_up, gate_up, k_k, k_a, r_k, lnx_w, lnx_b):
    out_dtype = z.dtype
    f32 = jnp.float32
    z = z.astype(f32)
    B, T, _ = z.shape
    C, H, N = RWKV_WIDTH, RWKV_HEADS, HEAD_DIM
    cuts = [C, 2 * C, 3 * C, 3 * C + DECAY_LORA, 3 * C + DECAY_LORA + AAA_LORA]
    r, k, v, wd, ad, gd = jnp.split(z, cuts, axis=-1)
    w = -jax.nn.softplus(-(w0.astype(f32) + jnp.tanh(wd) @ decay_up.astype(f32))) - 0.5
    a = jax.nn.sigmoid(a0.astype(f32) + ad @ aaa_up.astype(f32))
    g = jax.nn.sigmoid(gd) @ gate_up.astype(f32)
    kk = (k * k_k.astype(f32)).reshape(B, T, H, N)
    kk = kk / jnp.maximum(jnp.sqrt(jnp.sum(kk * kk, axis=-1, keepdims=True)), 1e-12)
    k = k * (1.0 + (a - 1.0) * k_a.astype(f32))
    heads = lambda t: t.reshape(B, T, H, N)
    r_h, k_h, v_h, a_h = heads(r), heads(k), heads(v), heads(a)
    decay = jnp.exp(-jnp.exp(heads(w)))
    tm = lambda t: jnp.swapaxes(t, 0, 1)
    seq_in = (tm(r_h), tm(decay), tm(k_h), tm(v_h), tm(-kk), tm(kk * a_h))

    def step(S, inp):
        r_t, w_t, k_t, v_t, a_t, b_t = inp
        sa = jnp.einsum('bhij,bhj->bhi', S, a_t)
        S = S * w_t[:, :, None, :] + sa[..., None] * b_t[:, :, None, :] + v_t[..., None] * k_t[:, :, None, :]
        return S, jnp.einsum('bhij,bhj->bhi', S, r_t)

    S0 = jnp.zeros((B, H, N, N), f32)
    _, y = lax.scan(step, S0, seq_in)
    y = tm(y)
    mu = jnp.mean(y, axis=-1, keepdims=True)
    var = jnp.mean(jnp.square(y - mu), axis=-1, keepdims=True)
    y = (y - mu) * lax.rsqrt(var + GN_EPS) * lnx_w.astype(f32).reshape(H, N) + lnx_b.astype(f32).reshape(H, N)
    y = y + jnp.sum(r_h * k_h * r_k.astype(f32), axis=-1, keepdims=True) * v_h
    return (y.reshape(B, T, C) * g).astype(out_dtype)

def _swa_gqa_sinks(q, k, v, sinks):
    B, T, _, hd = q.shape
    nb = T // BLOCK
    qb = q.reshape(B, nb, BLOCK, SWA_KV_HEADS, SWA_GROUP, hd)

    def band(t):
        tb = t.reshape(B, nb, BLOCK, SWA_KV_HEADS, hd)
        prev = jnp.pad(tb[:, :-1], ((0, 0), (1, 0), (0, 0), (0, 0), (0, 0)))
        return jnp.concatenate([prev, tb], axis=2)

    kb, vb = band(k), band(v)
    s = jnp.einsum('bnqhgd,bnkhd->bnhgqk', qb, kb).astype(jnp.float32) * (hd ** -0.5)
    blk = jnp.arange(nb)[:, None]
    qpos = blk * BLOCK + jnp.arange(BLOCK)[None, :]
    kpos = (blk - 1) * BLOCK + jnp.arange(2 * BLOCK)[None, :]
    diff = qpos[:, :, None] - kpos[:, None, :]
    valid = (diff >= 0) & (diff < WINDOW) & (kpos[:, None, :] >= 0)
    s = jnp.where(valid[None, :, None, None], s, NEG_INF)
    sink = jnp.broadcast_to(sinks.astype(jnp.float32).reshape(SWA_KV_HEADS, SWA_GROUP)[None, None, :, :, None, None],
                            s.shape[:-1] + (1,))
    p = jax.nn.softmax(jnp.concatenate([s, sink], axis=-1), axis=-1)[..., :-1]
    o = jnp.einsum('bnhgqk,bnkhd->bnqhgd', p.astype(v.dtype), vb)
    return o.reshape(B, T, SWA_Q_HEADS * hd)

def _memory_cross_attn(h, mem_n, w_xq, w_xkv, w_xo):
    B, T, _ = h.shape
    M = mem_n.shape[1]
    q = (h @ w_xq).reshape(B, T, XATTN_HEADS, XATTN_HEAD_DIM)
    k, v = jnp.split(mem_n @ w_xkv, 2, axis=-1)
    k = k.reshape(B, M, XATTN_HEADS, XATTN_HEAD_DIM)
    v = v.reshape(B, M, XATTN_HEADS, XATTN_HEAD_DIM)
    s = jnp.einsum('bthd,bmhd->bhtm', q, k).astype(jnp.float32) * (XATTN_HEAD_DIM ** -0.5)
    p = jax.nn.softmax(s, axis=-1).astype(v.dtype)
    o = jnp.einsum('bhtm,bmhd->bthd', p, v).reshape(B, T, D_MODEL)
    return o @ w_xo

def setup_inputs(seed: int = 0) -> dict:
    key = jax.random.key(seed)
    ks = iter(jax.random.split(key, 40))
    f32 = jnp.float32
    L, D, C = DEPTH, D_MODEL, RWKV_WIDTH
    nrm = lambda shape, scale: jax.random.normal(next(ks), shape, f32) * scale
    uni = lambda shape, lo, hi: jax.random.uniform(next(ks), shape, f32, lo, hi)
    gain = lambda shape: 1.0 + nrm(shape, 0.02)
    return {
        'x': nrm((BATCH, SEQ, D), 1.0),
        'mem': nrm((BATCH, MEM_LEN, D), 1.0),
        'f1_norm': gain((L, D)),
        'f1_gate': nrm((L, D, D_FF), D ** -0.5),
        'f1_up': nrm((L, D, D_FF), D ** -0.5),
        'f1_down': nrm((L, D_FF, D), D_FF ** -0.5),
        'mix_norm': gain((L, D)),
        'w_in': nrm((L, D, IN_COLS), D ** -0.5),
        'b_in_attn': nrm((L, SWA_COLS), 0.02),
        'rw_mu': uni((L, SHIFT_COLS), 0.0, 1.0),
        'rw_w0': uni((L, C), -6.0, -1.0),
        'rw_decay_up': nrm((L, DECAY_LORA, C), 0.1),
        'rw_a0': nrm((L, C), 0.1),
        'rw_aaa_up': nrm((L, AAA_LORA, C), 0.5 * AAA_LORA ** -0.5),
        'rw_gate_up': nrm((L, GATE_LORA, C), GATE_LORA ** -0.5),
        'rw_k_k': 0.85 + nrm((L, C), 0.02),
        'rw_k_a': 1.0 + nrm((L, C), 0.02),
        'rw_r_k': nrm((L, RWKV_HEADS, HEAD_DIM), 0.1),
        'rw_lnx_w': gain((L, C)),
        'rw_lnx_b': nrm((L, C), 0.02),
        'attn_sinks': nrm((L, SWA_Q_HEADS), 0.5),
        'w_out': nrm((L, D, D), D ** -0.5),
        'b_out': nrm((L, D), 0.02),
        'xa_norm': gain((L, D)),
        'mem_norm': gain((L, D)),
        'w_xq': nrm((L, D, D), D ** -0.5),
        'w_xkv': nrm((L, D, 2 * D), D ** -0.5),
        'w_xo': nrm((L, D, D), D ** -0.5),
        'f2_norm': gain((L, D)),
        'f2_gate': nrm((L, D, D_FF), D ** -0.5),
        'f2_up': nrm((L, D, D_FF), D ** -0.5),
        'f2_down': nrm((L, D_FF, D), D_FF ** -0.5),
        'final_norm': gain((D,)),
    }

def reference(x, mem, f1_norm, f1_gate, f1_up, f1_down, mix_norm, w_in, b_in_attn, rw_mu, rw_w0,
              rw_decay_up, rw_a0, rw_aaa_up, rw_gate_up, rw_k_k, rw_k_a, rw_r_k, rw_lnx_w, rw_lnx_b,
              attn_sinks, w_out, b_out, xa_norm, mem_norm, w_xq, w_xkv, w_xo, f2_norm, f2_gate, f2_up,
              f2_down, final_norm):
    B, T, _ = x.shape
    pos = jnp.arange(T, dtype=jnp.float32)
    kv_w = SWA_KV_HEADS * HEAD_DIM
    for l in range(DEPTH):
        x = x + 0.5 * _swiglu(_rmsnorm(x, f1_norm[l]), f1_gate[l], f1_up[l], f1_down[l])
        h = _rmsnorm(x, mix_norm[l])
        proj = h @ w_in[l]
        zr = proj[..., :SHIFT_COLS]
        zr_prev = jnp.pad(zr[:, :-1], ((0, 0), (1, 0), (0, 0)))
        zr = zr + (zr_prev - zr) * rw_mu[l]
        za = proj[..., SHIFT_COLS:] + b_in_attn[l]
        q = za[..., :SWA_WIDTH].reshape(B, T, SWA_Q_HEADS, HEAD_DIM)
        k = za[..., SWA_WIDTH:SWA_WIDTH + kv_w].reshape(B, T, SWA_KV_HEADS, HEAD_DIM)
        v = za[..., SWA_WIDTH + kv_w:].reshape(B, T, SWA_KV_HEADS, HEAD_DIM)
        y_rwkv = _rwkv7_time_mix(zr, rw_w0[l], rw_decay_up[l], rw_a0[l], rw_aaa_up[l], rw_gate_up[l],
                                 rw_k_k[l], rw_k_a[l], rw_r_k[l], rw_lnx_w[l], rw_lnx_b[l])
        y_swa = _swa_gqa_sinks(_rope(q, pos), _rope(k, pos), v, attn_sinks[l])
        x = x + jnp.concatenate([y_rwkv, y_swa], axis=-1) @ w_out[l] + b_out[l]
        x = x + _memory_cross_attn(_rmsnorm(x, xa_norm[l]), _rmsnorm(mem, mem_norm[l]), w_xq[l], w_xkv[l], w_xo[l])
        x = x + 0.5 * _swiglu(_rmsnorm(x, f2_norm[l]), f2_gate[l], f2_up[l], f2_down[l])
    return _rmsnorm(x, final_norm)


_drawn_inputs = setup_inputs


def setup_inputs(seed=0):
    import zlib

    import numpy as np

    out = dict(_drawn_inputs(seed))
    spreads = {}
    factors = {'f1_norm': 5.645,
     'mix_norm': 3.973,
     'b_in_attn': 20.941,
     'rw_decay_up': 4.302,
     'rw_a0': 3.842,
     'rw_k_k': 64.0,
     'rw_k_a': 7.731,
     'rw_lnx_w': 64.0,
     'rw_lnx_b': 64.0,
     'attn_sinks': 57.808,
     'b_out': 24.528,
     'xa_norm': 8.0,
     'mem_norm': 8.0,
     'f2_norm': 33.575,
     'final_norm': 7.538}
    for name, (base, spread) in spreads.items():
        noise = np.random.default_rng([zlib.crc32(name.encode()), seed]).standard_normal(out[name].shape)
        drawn = base * np.exp(spread * noise) if base else spread * noise
        out[name] = __import__('jax').numpy.asarray(drawn.astype(out[name].dtype))
    for name, factor in factors.items():
        out[name] = (out[name] * factor).astype(out[name].dtype)
    return out
```

```python
from contextlib import ExitStack

import numpy as np
import concourse.bass as bass
from concourse import mybir

F32 = mybir.dt.float32
F32R = mybir.dt.float32r
ALU = mybir.AluOpType
ACT = mybir.ActivationFunctionType
AX_X = mybir.AxisListType.X

P = 128
D = 2048
T = 256
KT = D // P
D_FF = 5632
FT = D_FF // P
RMS_EPS = 1e-6
GN_EPS = 64e-5
HD = 64
C = 1024
UN = C // P
LORA_COL = 3 * C
GATE_COL = LORA_COL + 128
TAIL_COL = GATE_COL + 32
Q_COL = GATE_COL + 160
KV_COL = Q_COL + 1024
L = 64
TC = T // L
LEVELS = [2, 4, 8, 16, 32]
DECAY = float(np.exp(-0.5))

COLS = 2 * P
KC = 4
CHUNK = KC * COLS
RING = 4
LEAD = 3
STEPS = D_FF // COLS

PARAMS = [("f1_norm", 16), ("mix_norm", 16), ("mem_norm", 16), ("xa_norm", 16), ("f2_norm", 16), ("final_norm", 16),
          ("b_out", 16), ("b_q", 8), ("b_kv", 2), ("mu", 24), ("mu_lora", 2), ("mu_tail", 1), ("w0", 8), ("a0", 8),
          ("k_k", 8), ("k_a", 8), ("r_k", 8), ("lnx_w", 8), ("lnx_b", 8), ("sinks", 16)]
PCOL = {}
for _n, _k in PARAMS:
    PCOL[_n] = sum(k for _, k in PARAMS[:len(PCOL)])
NPAR = sum(k for _, k in PARAMS)

SWA_CONSTS = [("swap", 128), ("select", 512), ("cos", 256), ("sin", 256), ("band", 384)]
RW_CONSTS = [("stack", 64), ("same_head", 128), ("pair", 128), ("level", 640), ("pair_t", 64), ("before_t", 64),
             ("upto_t", 64)]


def columns(spec):
    at, out = 0, {}
    for n, k in spec:
        out[n] = (at, at + k)
        at += k
    return out, at


def swa_consts():
    p = np.arange(P)
    swap = np.zeros((P, P), np.float32)
    swap[p, p ^ 32] = 1.0
    select = np.zeros((P, 4, P), np.float32)
    for g in range(2):
        for e in range(2):
            select[g * HD + np.arange(HD), 2 * g + e, e * HD + np.arange(HD)] = 1.0
    freq = (np.float32(10000.0) ** (-np.arange(0, HD, 2, dtype=np.float32) / np.float32(HD))).astype(np.float32)
    ang = np.arange(T, dtype=np.float32)[None, :] * freq[p % 32][:, None]
    cos, sin = np.cos(ang), np.sin(ang) * np.where(p % HD < 32, -1.0, 1.0)[:, None]
    q = np.arange(P)[:, None]
    k = np.arange(P)[None, :]
    own = np.where(q >= k, 0.0, -1e30)
    prev = np.where(q < k, 0.0, -1e30)
    band = np.concatenate([own, prev, own], axis=1)
    return np.concatenate([swap, select.reshape(P, -1), cos, sin, band], axis=1).astype(np.float32)


def rw_consts():
    p = np.arange(P)
    h, t = p // L, p % L
    stack = (t[:, None] == np.arange(L)[None, :])
    same = h[:, None] == h[None, :]

    def off(b, row, col):
        return (row // (2 * b) == col // (2 * b)) & (row // b % 2 == 1) & (col // b % 2 == 0)
    pair = same & off(1, t[:, None], t[None, :])
    level = [same & off(b, t[:, None], t[None, :]) for b in LEVELS]
    c = np.arange(L)
    pair_t = off(1, c[None, :], t[:, None])
    before_t = t[:, None] < c[None, :]
    upto_t = t[:, None] <= c[None, :]
    return np.concatenate([stack, same, pair] + level + [pair_t, before_t, upto_t], axis=1).astype(np.float32)


class Weights:

    def __init__(self):
        self.real = []

    def add(self, pattern, times=1):
        first = len(self.real)
        self.real += list(pattern) * times
        return first

    def count(self, v):
        return sum(self.real[u] for u in range(v % RING, min(v + 1, len(self.real)), RING))

    def uses(self, v, i=0, per=0):
        n = self.count(v)
        if isinstance(i, int) and i == 0:
            return n
        return i * (self.count(v + per) - n) + n

    def missing(self, v):
        return v >= len(self.real) or not self.real[v]


class Blocks:

    def __init__(self):
        self.pair = []

    def add(self, pairs, times=1):
        first = len(self.pair)
        self.pair += list(pairs) * times
        return first

    def before(self, b, i=0, nb=0):
        n = sum(q == self.pair[b] for q in self.pair[:b])
        if isinstance(i, int) and i == 0:
            return n
        return i * (sum(q == self.pair[b] for q in self.pair[:b + nb]) - n) + n


class Own:

    def __init__(self, sem):
        self.sem, self.n, self.i, self.per = sem, 0, 0, 0

    def __call__(self, eng):
        self.n += 1
        eng.wait_ge(self.sem, self.i * self.per + self.n if self.per else self.n)

    def rounds(self, i, per):
        self.i, self.per, self.start = i, per, self.n

    def end(self, rounds):
        assert self.n == self.start + self.per, (self.n - self.start, self.per)
        self.n, self.per = self.start + rounds * self.per, 0


def build(nc, A, out):
    W, B = Weights(), Blocks()
    full = [True] * 4
    V_UP1, B_UP1 = W.add(full, 2 * STEPS), B.add([0, 1], STEPS)
    V_DOWN1, B_DOWN1 = W.add([True] * 11 + [False], 8), B.add([0, 1], 4)
    V_Q, B_Q = W.add(full, 4), B.add([0, 1], 2)
    V_KV, B_KV = W.add(full), B.add([0])
    V_LORA, B_LORA = W.add(full), B.add([1])
    V_TAIL, B_TAIL = W.add([True, True, False, False]), B.add([0])
    V_RKV, B_RKV = W.add(full, 12), B.add([1, 0, 1], 4)
    V_MEM, B_MEM = W.add(full, 16), B.add([0, 1], 8)
    V_OUT, B_OUT = W.add(full, 8), B.add([0, 1], 4)
    V_XQ, B_XQ = W.add(full, 8), B.add([0, 1], 4)
    V_XO, B_XO = W.add(full, 8), B.add([0, 1], 4)
    V_UP2, B_UP2 = W.add(full, 2 * STEPS), B.add([0, 1], STEPS)
    V_DOWN2, B_DOWN2 = W.add([True] * 11 + [False], 8), B.add([0, 1], 4)
    X1, MIX, MEM, XA, F2, FINAL = range(6)
    FILL_X, FILL_MIX, FILL_MEM, FILL_XA, FILL_F2 = range(5)

    ctx = ExitStack()
    with ctx:
        def sb(name, shape, dt=F32):
            return ctx.enter_context(nc.sbuf_tensor(name, shape, dt))

        sems = {}

        def S(name):
            if name not in sems:
                sems[name] = ctx.enter_context(nc.semaphore(name))
            return sems[name]

        def need(eng, i, *names):
            for n in names:
                eng.wait_ge(S(n), i + 1)

        raw = sb("raw", [P, RING, CHUNK])
        parts = sb("parts", [P, RING, KC, 2, COLS], F32R)
        xs = sb("xs", [P, KT, 2, T], F32R)
        par = sb("par", [P, NPAR])
        low = sb("low", [P, 2, 2, T])
        total = sb("total", [P, 2, T])
        gate = sb("gate", [P, 2, T])
        sig = sb("sig", [P, 2, T])
        up = sb("up", [P, 2, T])
        sq = sb("sq", [P, 2, T])
        sqacc = sb("sqacc", [P, T])
        ones = sb("ones", [P, P])
        ident = sb("unit", [P, P])
        ms = sb("ms", [P, T])
        rstd = sb("rstd", [P, T])
        small = sb("small", [P, 144])
        rcol = sb("rcol", [P, 2])
        HS_AT = KT * T
        M_WORDS = 27632
        at = -(-nc.sbuf_base // 32) * 32
        M = sb("M", [P, M_WORDS])
        hs = nc.alloc_sbuf_tensor_at("hs", [P, FT, 2, T], F32R, offset=at + 4 * HS_AT)

        def view(words, *dims):
            a = cursor[0]
            cursor[0] += words
            assert cursor[0] <= M_WORDS, cursor[0]
            v = M[:, a:a + words]
            if len(dims) == 2:
                v = v.rearrange("p (a b) -> p a b", b=dims[1])
            if len(dims) == 3:
                v = v.rearrange("p (a b c) -> p a b c", b=dims[1], c=dims[2])
            return v

        cursor = [0]
        x = view(HS_AT, KT, T)
        rkv = view(24 * T, 24, T)
        lora = view(3 * T, 3, T)
        q_all = view(UN * T, UN, T)
        WORK = cursor[0]
        swc, nsw = columns(SWA_CONSTS)
        swt = view(nsw)
        k_v = view(2 * T, 2, T)
        krot = view(T)
        ktmp = view(T)
        kpad = view(4 * T, 4, T)
        vpad = view(2 * 512, 2, 512)
        vg = view(512, 4, P)
        qg = view(512, 2, T)
        qtmp = view(512, 2, T)
        sc = view(4 * 384, 4, 384)
        pt = view(12 * P, 12, P)
        shifted = view(2 * 257 + 6)[:, 0:514].rearrange("p (a b) -> p a b", b=257)
        rwc, nrw = columns(RW_CONSTS)
        cursor[0] = WORK
        RW0 = cursor[0]
        rwt = view(nrw)
        daw = view(C)
        Bh = view(1024, UN, P)
        Kh = view(1024, UN, P)
        Abd = view(1024, UN, P)
        rhs = view(1024, UN, P)
        Wx = view(UN * 65, UN, 65)
        Winv = view(512, UN, L)
        Vc = Winv
        cum = view(512, UN, L)
        aa = view(512, UN, L)
        Uc = aa
        kk = view(512, UN, L)
        Rc = kk
        ArkT = view(512, UN, L)
        ArbT = view(512, UN, L)
        AakT = view(1024, UN, P)
        Pm = view(1024, UN, P)
        Ubd = Pm
        RW1 = cursor[0]
        X0 = [0]

        def xview(words, *dims):
            a = X0[0]
            X0[0] += words
            assert X0[0] <= HS_AT
            return M[:, a:a + words].rearrange("p (a b) -> p a b", b=dims[1])
        Am = xview(1024, UN, P)
        Xi = xview(1024, UN, P)
        Yi = xview(1024, UN, P)
        Araw = xview(1024, UN, P)
        Vbd = view(1024, UN, P)
        Sbd = view(1024, UN, P)
        Sc = view(512, UN, L)
        t1 = sig[:, :, :].rearrange("p a b -> p (a b)").rearrange("p (a b) -> p a b", b=L)
        t2 = sq[:, :, :].rearrange("p a b -> p (a b)").rearrange("p (a b) -> p a b", b=L)
        tzc = small[:, 0:64]
        cursor[0] = WORK
        gup = view(2 * C, 2, C)
        cursor[0] = HS_AT
        KX = view(KT * T, KT, T)
        VX = view(2 * D, 2, D)
        QX = view(KT * T, KT, T)
        SX = view(1024, 4, T)
        PX = view(1024, 4, T)
        YT0 = FT - KT
        assert cursor[0] <= HS_AT + YT0 * 512
        GUP_END = WORK + 2 * C
        assert GUP_END <= HS_AT + YT0 * 512

        acc = [ctx.enter_context(nc.psum_tensor(f"acc{p}", [P, 2, 2, T], F32)) for p in range(2)]
        mid = ctx.enter_context(nc.psum_tensor("mid", [P, 4, 512], F32))
        bank = [mid[:, n, :] for n in range(4)]
        b8 = [bk.rearrange("p (u t) -> p u t", t=L) for bk in bank]
        b4 = [bk.rearrange("p (u t) -> p u t", t=P) for bk in bank]
        b2 = [bk.rearrange("p (u t) -> p u t", t=T) for bk in bank]
        two = [mid[:, 2 * n:2 * n + 2, :].rearrange("p b (u t) -> p (b u) t", t=P) for n in range(2)]
        dram_x = nc.dram_tensor("spill_x", (D, T), F32, kind="Internal").ap().rearrange("(t p) n -> p t n", p=P)
        dram_k = nc.dram_tensor("spill_k", (D, T), F32, kind="Internal").ap().rearrange("(t p) n -> p t n", p=P)
        dram_v = nc.dram_tensor("spill_v", (T, D), F32, kind="Internal").ap().rearrange("(t p) n -> p t n", p=P)
        out_v = out.rearrange("(t p) n -> p t n", p=P)

        raw_landed = [S(f"raw_landed{s}") for s in range(RING)]
        high_ready = [S(f"high_ready{s}") for s in range(RING)]
        low_ready = [S(f"low_ready{s}") for s in range(RING)]
        parts_used = [S(f"parts_used{s}") for s in range(RING)]
        bank_free = [S(f"bank_free{p}") for p in range(2)]
        low_copied = S("low_copied")
        own = Own(S("dve_step"))
        block = ctx.enter_context(nc.Block())

        def pc(name, k=0):
            a = PCOL[name] + k
            return par[:, bass.ds(a, 1)] if not isinstance(a, int) else par[:, a:a + 1]

        def plain(eng):
            eng.sem_inc(S("passed"), 1)

        def per_unit(name):
            return par[:, PCOL[name]:PCOL[name] + UN].unsqueeze(2).to_broadcast([P, UN, L])

        def rc(name):
            a, b = rwc[name]
            return rwt[:, a:b]

        def sc_(name):
            a, b = swc[name]
            return swt[:, a:b]

        def is_first(i):
            return isinstance(i, int) and i == 0

        def load(sp, v, src, i=0, per=0):
            s, n = v % RING, W.uses(v, i, per)
            if W.count(v) > 1:
                sp.wait_ge(low_ready[s], n - 1)
                if not isinstance(i, int):
                    plain(sp)
            sp.dma_start(raw[:, s, :].rearrange("p (t n) -> p t n", n=src.shape[2]), src).then_inc(raw_landed[s], 16)

        def split_high(act, v, i=0, per=0):
            if W.missing(v):
                return
            s, n = v % RING, W.uses(v, i, per)
            act.wait_ge(raw_landed[s], 16 * n)
            if W.count(v) > 1:
                act.wait_ge(parts_used[s], n - 1)
            act.activation(parts[:, s, :, 0, :], raw[:, s, :].rearrange("p (t n) -> p t n", n=COLS), ACT.Copy)\
               .then_inc(high_ready[s], 1)

        def split_low(dve, v, i=0, per=0):
            if W.missing(v):
                return
            s = v % RING
            dve.wait_ge(high_ready[s], W.uses(v, i, per))
            dve.tensor_tensor(parts[:, s, :, 1, :], raw[:, s, :].rearrange("p (t n) -> p t n", n=COLS),
                              parts[:, s, :, 0, :].bitcast(F32), ALU.subtract).then_inc(low_ready[s], 1)

        def ahead(split, eng, v, chunks, i=0, per=0):
            for j in range(chunks):
                split(eng, v + j + LEAD, i, per)

        def chunk_products(pe, b, v, j, chunks, moving, ready=None, i=0, per=0, nb=0, by_token=False, first_tile=0,
                           order=None):
            p, s = B.pair[b], (v + j) % RING
            if j == 0:
                pe.wait_ge(bank_free[p], 1 + B.before(b, i, nb))
            if ready is not None:
                ready(pe, j)
            pe.wait_ge(low_ready[s], W.uses(v + j, i, per))
            for t in range(KC):
                k = j * KC + t
                at = first_tile + (order[j] if order else j) * KC + t
                first, last = k == 0, k == chunks * KC - 1
                for n in range(2):
                    if by_token:
                        pe.matmul(acc[p][:, n, :, :], moving[:, k, 0, n * P:(n + 1) * P], parts[:, s, t, :, :],
                                  start=first, stop=False, skip_group_check=True)
                        m = pe.matmul(acc[p][:, n, 1, :], moving[:, k, 1, n * P:(n + 1) * P], parts[:, s, t, 0, :],
                                      start=False, stop=last, skip_group_check=True)
                    else:
                        pe.matmul(acc[p][:, n, :, :], parts[:, s, t, 0, n * P:(n + 1) * P],
                                  moving[:, at, :, :], start=first, stop=False, skip_group_check=True)
                        m = pe.matmul(acc[p][:, n, 1, :], parts[:, s, t, 1, n * P:(n + 1) * P],
                                      moving[:, at, 0, :], start=False, stop=last, skip_group_check=True)
            m.then_inc(parts_used[s], 1)

        def products(pe, b, v, chunks, moving, ready=None, i=0, per=0, nb=0, **kw):
            for j in range(chunks):
                chunk_products(pe, b, v, j, chunks, moving, ready, i, per, nb, **kw)

        def copy_low(act, b, v_last, i=0, per=0):
            p = B.pair[b]
            act.wait_ge(parts_used[v_last % RING], W.uses(v_last, i, per))
            act.activation(low[:, p, :, :], acc[p][:, :, 1, :], ACT.Copy).then_inc(low_copied, 1)

        def add_low(dve, b, i=0, nb=0):
            p = B.pair[b]
            dve.wait_ge(low_copied, b + 1 + i * nb)
            dve.tensor_tensor(total[:, :, :], acc[p][:, :, 0, :], low[:, p, :, :], ALU.add).then_inc(bank_free[p], 1)
            dve.wait_ge(bank_free[p], 2 + B.before(b, i, nb))

        rb = rstd[:, :].unsqueeze(1).to_broadcast([P, 2, T])

        def fill_act(act, norm, gain, blk, src, fill):
            n = 8 * norm + blk
            for e in range(2):
                k = 2 * blk + e
                m = act.activation(xs[:, bass.ds(k, 1), 0, :], src[:, bass.ds(k, 1), :], ACT.Copy, scale=pc(gain, k))
            m.then_inc(S("xs_high"), 1)
            act.wait_ge(S("sq_added"), 2 * n + 1)
            plain(act)
            act.activation(sq[:, :, :], src[:, bass.ds(2 * blk, 2), :], ACT.Square).then_inc(S("sq_ready"), 1)

        def fill_dve(dve, gain, blk, src, fill):
            dve.wait_ge(S("xs_high"), 8 * fill + blk + 1)
            for e in range(2):
                k = 2 * blk + e
                m = dve.scalar_tensor_tensor(xs[:, bass.ds(k, 1), 1, :], src[:, bass.ds(k, 1), :], pc(gain, k),
                                             xs[:, bass.ds(k, 1), 0, :].bitcast(F32), ALU.mult, ALU.subtract)
            m.then_inc(S("xs_ready"), 1)

        def filled(fill):
            def ready(pe, j):
                pe.wait_ge(S("xs_ready"), 8 * fill + 2 * (j + 1))
            return ready

        def sum_squares(pool, norm):
            if norm:
                pool.wait_ge(S("ms_ready"), norm)
            pool.memset(sqacc[:, :], 0.0).then_inc(S("sq_cleared"), 1)
            pool.wait_ge(S("sq_cleared"), norm + 1)
            with pool.Fori(0, 8) as blk:
                pool.wait_ge(S("sq_ready"), 8 * norm + blk + 1)
                pool.tensor_tensor(sqacc[:, :], sqacc[:, :], sq[:, 0, :], ALU.add).then_inc(S("sq_added"), 1)
                pool.wait_ge(S("sq_added"), 16 * norm + 2 * blk + 2)
                pool.tensor_tensor(sqacc[:, :], sqacc[:, :], sq[:, 1, :], ALU.add).then_inc(S("sq_added"), 1)
                pool.wait_ge(S("sq_added"), 16 * norm + 2 * blk + 3)

        def norm_pe(pe, norm):
            pe.wait_ge(S("sq_added"), 16 * norm + 17)
            if norm == MEM:
                for e in range(2):
                    pe.matmul(bank[0][:, 256 + e:257 + e], sqacc[:, e * P:(e + 1) * P], ones[:, 0:1],
                              start=True, stop=True)
            pe.matmul(bank[0][:, 0:T], ones[:, :], sqacc[:, :], start=True, stop=True).then_inc(S("ms_ready"), 1)

        def norm_act(act, norm):
            act.wait_ge(S("ms_eps"), norm + 1)
            if norm == MEM:
                act.activation(small[:, 66:68], small[:, 64:66], ACT.Sqrt)
            act.activation(ms[:, :], ms[:, :], ACT.Sqrt).then_inc(S("root_ready"), 1)

        def norm_dve(dve, norm):
            dve.wait_ge(S("ms_ready"), norm + 1)
            if norm == MEM:
                dve.tensor_scalar(small[:, 64:66], bank[0][:, 256:258], RMS_EPS, None, ALU.add)
            dve.tensor_scalar(ms[:, :], bank[0][:, 0:T], RMS_EPS, None, ALU.add).then_inc(S("ms_eps"), 1)
            dve.wait_ge(S("root_ready"), norm + 1)
            if norm == MEM:
                dve.reciprocal(rcol[:, :], small[:, 66:68])
            dve.reciprocal(rstd[:, :], ms[:, :]).then_inc(S("dve_step"), 1)
            own(dve)

        def b_step(b):
            base = B_UP1 if b < B_DOWN1 else B_UP2
            return (b - base) // 2 + 1

        def ffn_act(act, ffn, b0, v0, vend):
            def gate_part(b, v, i=0):
                n = STEPS * ffn + b_step(b) + i
                copy_low(act, b, v + 3, i, 8)
                act.wait_ge(S("gate_ready"), n)
                act.activation(sig[:, :, :], gate[:, :, :], ACT.Sigmoid).then_inc(S("sigmoid_ready"), 1)

            def up_part(b, v, step, i=0):
                n = STEPS * ffn + b_step(b) + i
                copy_low(act, b, v + 3, i, 8)
                act.wait_ge(S("hidden_ready"), n)
                plain(act)
                act.activation(hs[:, bass.ds(step * 2, 2), 0, :], total[:, :, :], ACT.Copy)\
                   .then_inc(S("hidden_high"), 1)
            gate_part(b0, v0)
            with act.Fori(0, STEPS - 1) as i:
                ahead(split_high, act, v0 + 4, 4, i, 8)
                up_part(b0 + 1, v0 + 4, i, i)
                ahead(split_high, act, v0 + 8, 4, i, 8)
                gate_part(b0 + 2, v0 + 8, i)
            ahead(split_high, act, vend - 4, 4)
            up_part(b0 + 2 * STEPS - 1, vend - 4, STEPS - 1)

        def ffn_dve(dve, ffn, b0, v0, vend):
            def gate_part(b, i=0):
                add_low(dve, b, i, 2)
                dve.tensor_tensor(gate[:, :, :], total[:, :, :], rb, ALU.mult).then_inc(S("gate_ready"), 1)

            def up_part(b, step, i=0):
                n = STEPS * ffn + b_step(b) + i
                add_low(dve, b, i, 2)
                dve.tensor_tensor(up[:, :, :], total[:, :, :], rb, ALU.mult).then_inc(S("dve_step"), 1)
                own(dve)
                dve.tensor_tensor(gate[:, :, :], gate[:, :, :], up[:, :, :], ALU.mult).then_inc(S("dve_step"), 1)
                own(dve)
                dve.wait_ge(S("sigmoid_ready"), n)
                dve.tensor_tensor(total[:, :, :], gate[:, :, :], sig[:, :, :], ALU.mult)\
                   .then_inc(S("hidden_ready"), 1)
                dve.wait_ge(S("hidden_high"), n)
                dve.tensor_tensor(hs[:, bass.ds(step * 2, 2), 1, :], total[:, :, :],
                                  hs[:, bass.ds(step * 2, 2), 0, :].bitcast(F32), ALU.subtract)\
                   .then_inc(S("hidden_split"), 1)
            gate_part(b0)
            with dve.Fori(0, STEPS - 1) as i:
                own.rounds(i, 2)
                ahead(split_low, dve, v0 + 4, 4, i, 8)
                up_part(b0 + 1, i, i)
                ahead(split_low, dve, v0 + 8, 4, i, 8)
                gate_part(b0 + 2, i)
            own.end(STEPS - 1)
            ahead(split_low, dve, vend - 4, 4)
            up_part(b0 + 2 * STEPS - 1, STEPS - 1)

        def ffn_pe(pe, ffn, b0, v0, vend, norm, fill):
            products(pe, b0, v0, 4, xs, filled(fill))
            norm_pe(pe, norm)
            with pe.Fori(0, STEPS - 1) as i:
                products(pe, b0 + 1, v0 + 4, 4, xs, None, i, 8, 2)
                products(pe, b0 + 2, v0 + 8, 4, xs, None, i, 8, 2)
            products(pe, b0 + 2 * STEPS - 1, vend - 4, 4, xs)

        def hidden(ffn):
            def ready(pe, j):
                pe.wait_ge(S("hidden_split"), STEPS * ffn + 2 * (j + 1))
            return ready

        def resid_act(act, res, b, v_last, blk, norm, gain, fill, i=0, per=0):
            copy_low(act, b, v_last, i, per)
            act.wait_ge(S("x_updated"), 8 * res + blk + 1)
            plain(act)
            if fill is None:
                act.wait_ge(S("sq_added"), 2 * (8 * norm + blk) + 1)
                plain(act)
                act.activation(sq[:, :, :], x[:, bass.ds(2 * blk, 2), :], ACT.Square).then_inc(S("sq_ready"), 1)
            else:
                fill_act(act, norm, gain, blk, x, fill)

        def resid_dve(dve, res, b, blk, gain, fill, half, bias=None, i=0, nb=0):
            add_low(dve, b, i, nb)
            xx = x[:, bass.ds(2 * blk, 2), :]
            if bias:
                for e in range(2):
                    xe = x[:, bass.ds(2 * blk + e, 1), :]
                    m = dve.scalar_tensor_tensor(xe, total[:, e:e + 1, :], pc(bias, 2 * blk + e), xe, ALU.add, ALU.add)
            else:
                m = dve.scalar_tensor_tensor(xx, total[:, :, :], half, xx, ALU.mult, ALU.add)
            m.then_inc(S("x_updated"), 1)
            dve.wait_ge(S("x_updated"), 8 * res + blk + 1)
            if fill is not None:
                fill_dve(dve, gain, blk, x, fill)

        @block.sync
        def _(sp):
            def cols(name):
                return A[name].rearrange("(t p) n -> p t n", p=P)

            def piece(w, j, c0):
                return w[:, KC * j:KC * (j + 1), c0:c0 + COLS] if isinstance(c0, int) else \
                    w[:, KC * j:KC * (j + 1), bass.ds(c0, COLS)]

            def ffn(v_up, v_down, pre):
                wg, wu, wd = cols(pre + "_gate"), cols(pre + "_up"), cols(pre + "_down")
                for j in range(8):
                    load(sp, v_up + j, piece((wg, wu)[j // 4], j % 4, 0))
                with sp.Fori(0, STEPS - 1) as i:
                    for j in range(8):
                        load(sp, v_up + 8 + j, piece((wg, wu)[j // 4], j % 4, i * COLS + COLS), i, 8)
                with sp.Fori(0, 8) as i:
                    for j in range(11):
                        load(sp, v_down + j, piece(wd, j, i * COLS), i, 12)

            def square(v, name, c0=0, order=(0, 1, 2, 3)):
                w = cols(name)
                with sp.Fori(0, 8) as i:
                    for j in range(4):
                        load(sp, v + j, piece(w, order[j], i * COLS + c0), i, 4)
            ffn(V_UP1, V_DOWN1, "f1")
            win = cols("w_in")
            for b in range(4):
                for j in range(4):
                    load(sp, V_Q + 4 * b + j, piece(win, j, Q_COL + COLS * b))
                if b == 0:
                    sp.wait_ge(S("x_updated"), 8)
                    sp.dma_start(dram_x, x[:, :, :]).then_inc(S("x_spilled"), 16)
            for j in range(4):
                load(sp, V_KV + j, piece(win, j, KV_COL))
            for j in range(4):
                load(sp, V_LORA + j, piece(win, j, LORA_COL))
            for j in range(2):
                load(sp, V_TAIL + j, win[:, 8 * j:8 * j + 8, TAIL_COL:TAIL_COL + P])
            with sp.Fori(0, 12) as i:
                for j in range(4):
                    load(sp, V_RKV + j, piece(win, j, i * COLS), i, 4)
            wkv = cols("w_xkv")
            with sp.Fori(0, 4) as i:
                for b in range(4):
                    for j in range(4):
                        c0 = i * (2 * COLS) + (b % 2) * COLS + (b // 2) * D
                        load(sp, V_MEM + 4 * b + j, piece(wkv, j, c0), i, 16)
            square(V_OUT, "w_out", 0, (2, 3, 0, 1))
            square(V_XQ, "w_xq")
            square(V_XO, "w_xo")
            ffn(V_UP2, V_DOWN2, "f2")
            for g in range(4):
                sp.wait_ge(S("out_ready"), g + 1)
                sp.dma_start(out_v[:, 4 * g:4 * g + 4, :], x[:, 4 * g:4 * g + 4, :]).then_inc(S("stored"), 16)
            sp.wait_ge(S("stored"), 64)

        @block.gpsimd
        def _(pool):
            pool.memset(small[:, 140:141], 0.0).then_inc(bank_free[0], 1)
            pool.memset(small[:, 141:142], 0.0).then_inc(bank_free[1], 1)
            pool.memset(small[:, 142:143], 0.0).then_inc(S("sq_added"), 1)
            pool.memset(ones[:, :], 1.0 / D).then_inc(S("ones_ready"), 1)
            sum_squares(pool, X1)
            sum_squares(pool, MIX)
            pool.dma_start(swt, A["swa_consts"]).then_inc(S("swa_tables"), 16)
            pool.memset(vpad[:, :, :], 0.0).then_inc(S("vpad_cleared"), 1)
            pool.memset(shifted[:, :, 0:1], 0.0).then_inc(S("shift_cleared"), 1)
            pool.wait_ge(S("x_spilled"), 16)
            pool.wait_ge(S("xs_ready"), 8 * FILL_MEM)
            pool.dma_start(x[:, :, :], A["mem_t"].rearrange("(t p) n -> p t n", p=P)).then_inc(S("mem_landed"), 16)
            pool.wait_ge(S("swa_done"), 4)
            pool.dma_start(rwt, A["rw_consts"]).then_inc(S("rw_tables"), 16)
            pool.dma_start(daw[0:64, :], A["rw_decay_up"]).then_inc(S("rw_tables"), 16)
            pool.dma_start(daw[64:128, :], A["rw_aaa_up"]).then_inc(S("rw_tables"), 16)
            sum_squares(pool, MEM)
            for m in (Bh, Kh, Abd, AakT, Pm):
                pool.memset(m, 0.0).then_inc(S("rw_cleared"), 1)
            pool.wait_ge(S("rw_tables"), 48)
            pool.memset(small[:, 143:144], 0.0).then_inc(S("spills_done"), 1)
            with pool.Fori(0, TC) as c:
                need(pool, c, "A_ready")
                pool.tensor_tensor(Xi, Araw, rc("pair").unsqueeze(1).to_broadcast([P, UN, P]), ALU.mult)\
                    .then_inc(S("X_pairs"), 1)
                need(pool, c, "X_pairs")
                pool.tensor_tensor(Xi, Xi, ident[:, :].unsqueeze(1).to_broadcast([P, UN, P]), ALU.add)
                for n in range(5):
                    if n:
                        pool.wait_ge(S("P_done"), c * 5 + n)
                    a = rwc["level"][0] + n * P
                    pool.tensor_tensor(Am, Araw, rwt[:, a:a + P].unsqueeze(1).to_broadcast([P, UN, P]), ALU.mult)\
                        .then_inc(S("Am"), 1)
                for n in range(2):
                    pool.wait_ge(S("kv_out"), c * 4 + n + 1)
                    pool.dma_start(dram_k[:, bass.ds(c * 4 + 2 * n, 2), :], (gate, up)[n][:, :, :])\
                        .then_inc(S("k_spilled"), 16)
                    pool.wait_ge(S("k_spilled"), c * 32 + 16 * (n + 1))
                for n in range(2):
                    pool.wait_ge(S("kv_out"), c * 4 + n + 3)
                    pool.dma_start(dram_v[:, :, bass.ds(c * 512 + 256 * n, 256)], (gate, up)[n][:, :, :])\
                        .then_inc(S("v_spilled"), 16)
                    pool.wait_ge(S("v_spilled"), c * 32 + 16 * (n + 1))
                plain(pool)
                pool.memset(small[:, 143:144], 0.0).then_inc(S("spills_done"), 1)
                need(pool, c, "chunk_done")
            pool.memset(gup[0:96, 1, :], 0.0).then_inc(S("gup_cleared"), 1)
            pool.dma_start(gup[:, 0, :], A["rw_gate_up"][0:128, :]).then_inc(S("gup_landed"), 16)
            pool.dma_start(gup[96:128, 1, :], A["rw_gate_up"][128:160, :]).then_inc(S("gup_landed"), 16)
            pool.dma_start(x[:, :, :], dram_x).then_inc(S("x_back"), 16)
            need(pool, 5, "y_split")
            pool.dma_start(KX, dram_k).then_inc(S("kv_back"), 16)
            pool.dma_start(VX, dram_v).then_inc(S("kv_back"), 16)
            sum_squares(pool, XA)
            sum_squares(pool, F2)
            sum_squares(pool, FINAL)


        def rkv_chunk(eng, kind, i, j):
            v, b = V_RKV, B_RKV + j // 4
            if kind == "pe":
                chunk_products(eng, b, v + j - j % 4, j % 4, 4, xs, None, i, 12, 3)
            elif kind == "act":
                split_high(eng, v + j + LEAD, i, 12)
                if j % 4 == 3:
                    copy_low(eng, b, v + j, i, 12)
            else:
                split_low(eng, v + j + LEAD, i, 12)
                if j % 4 == 3:
                    add_low(eng, b, i, 3)
                    n = j // 4
                    shift_in(eng)
                    for e in range(2):
                        k = i * 6 + 2 * n + e
                        m = eng.scalar_tensor_tensor(rkv[:, bass.ds(k, 1), :], up[:, e:e + 1, :], pc("mu", k),
                                                     shifted[:, e:e + 1, 1:257], ALU.mult, ALU.add)
                    m.then_inc(S("rkv_ready"), 1)

        def shift_in(dve):
            dve.tensor_tensor(shifted[:, :, 1:257], total[:, :, :], rb, ALU.mult).then_inc(S("dve_step"), 1)
            own(dve)
            dve.tensor_tensor(up[:, :, :], shifted[:, :, 0:256], shifted[:, :, 1:257], ALU.subtract)\
               .then_inc(S("dve_step"), 1)
            own(dve)

        def mem_chunk(eng, kind, c, j):
            v, n = V_MEM, j // 4
            b = B_MEM + n
            if kind == "pe":
                chunk_products(eng, b, v + j - j % 4, j % 4, 4, xs, filled(FILL_MEM) if n == 0 else None,
                               c, 16, 4, by_token=n >= 2)
            elif kind == "act":
                split_high(eng, v + j + LEAD, c, 16)
                if j % 4 == 3:
                    copy_low(eng, b, v + j, c, 16)
            else:
                split_low(eng, v + j + LEAD, c, 16)
                if j % 4 == 3:
                    add_low(eng, b, c, 4)
                    if n == 0:
                        eng.wait_ge(S("spills_done"), c + 1)
                    if n >= 2:
                        eng.wait_ge(S("k_spilled"), c * 32 + 16 * (n - 1))
                    by = rb if n < 2 else rcol[:, :].unsqueeze(2).to_broadcast([P, 2, T])
                    eng.tensor_tensor((gate, up)[n % 2][:, :, :], total[:, :, :], by, ALU.mult)\
                       .then_inc(S("kv_out"), 1)

        XSCALE = float(D // 4) ** -0.5
        xmax, xneg, xsum, xrec = (small[:, 112 + 4 * n:116 + 4 * n] for n in range(4))

        mx, negm, es, sums, rden = (small[:, 72 + 8 * n:80 + 8 * n] for n in range(5))

        def halves(eng, dst, src, name, mask=None, scale=None):
            for h in range(2):
                rows, co = slice(h * HD, h * HD + HD), slice(h * L, h * L + L)
                if mask is not None:
                    m = eng.tensor_tensor(dst[rows, :, co], src[rows, :, :],
                                          mask[rows, :].unsqueeze(1).to_broadcast([HD, UN, L]), ALU.mult)
                elif scale is not None:
                    m = eng.tensor_tensor(dst[rows, :, co], src[rows, :, :], scale[rows, :, :], ALU.mult)
                elif eng is nc.scalar:
                    m = eng.activation(dst[rows, :, co], src[rows, :, :], ACT.Copy)
                else:
                    m = eng.tensor_copy(dst[rows, :, co], src[rows, :, :])
            if name:
                m.then_inc(S(name), 1)

        def bcast(table):
            return table.unsqueeze(1).to_broadcast([P, UN, L])

        def odd(m, b, e):
            return m.rearrange("p (n two b) -> p n two b", two=2, b=b)[:, :, e, :]

        @block.scalar
        def _(act):
            act.dma_start(par[:, :], A["params"]).then_inc(S("par_landed"), 16)
            xin = A["x_t"].rearrange("(t p) n -> p t n", p=P)
            for g in range(4):
                act.dma_start(x[:, 4 * g:4 * g + 4, :], xin[:, 4 * g:4 * g + 4, :]).then_inc(S(f"x_landed{g}"), 16)
            act.dma_start(ident[:, :], A["ident"]).then_inc(S("ident_landed"), 16)
            act.wait_ge(S("par_landed"), 16)
            for b in range(8):
                act.wait_ge(S(f"x_landed{b // 2}"), 16)
                fill_act(act, X1, "f1_norm", b, x, FILL_X)
                if b % 2:
                    split_high(act, V_UP1 + b // 2)
            ahead(split_high, act, V_UP1 + 1, 3)
            norm_act(act, X1)
            ffn_act(act, 0, B_UP1, V_UP1, V_DOWN1)
            with act.Fori(0, 4) as i:
                for u in range(2):
                    ahead(split_high, act, V_DOWN1 + 12 * u, 12, i, 24)
                    resid_act(act, 0, B_DOWN1 + u, V_DOWN1 + 12 * u + 10, 2 * i + u, MIX, "mix_norm", FILL_MIX, i, 24)
            ahead(split_high, act, V_Q, 4)
            norm_act(act, MIX)
            copy_low(act, B_Q, V_Q + 3)
            for b in range(1, 4):
                ahead(split_high, act, V_Q + 4 * b, 4)
                copy_low(act, B_Q + b, V_Q + 4 * b + 3)
            ahead(split_high, act, V_KV, 4)
            copy_low(act, B_KV, V_KV + 3)
            ahead(split_high, act, V_LORA, 4)
            copy_low(act, B_LORA, V_LORA + 3)
            need(act, 0, "v_turned", "vpad_cleared")
            for g in range(2):
                vp = vpad[:, g, :].rearrange("p (b e n) -> p b e n", b=2, e=2)
                for e in range(2):
                    m = act.activation(vp[:, :, e, e * HD:(e + 1) * HD],
                                       bank[1].rearrange("p (b n) -> p b n", n=P)[:, 0:2, g * HD:(g + 1) * HD],
                                       ACT.Copy)
            m.then_inc(S("vpad_ready"), 1)
            need(act, 0, "k_selected")
            act.activation(kpad, mid[:, 2:4, :].rearrange("p b (u t) -> p (b u) t", t=T), ACT.Copy)\
               .then_inc(S("kpad_ready"), 1)
            ahead(split_high, act, V_TAIL, 4)
            copy_low(act, B_TAIL, V_TAIL + 1)
            need(act, 1, "lora_ready")
            act.activation(lora[0:64, 0, :], lora[0:64, 0, :], ACT.Tanh)
            act.activation(lora[:, 1:3, :], lora[:, 1:3, :], ACT.Sigmoid).then_inc(S("lora_act"), 1)
            with act.Fori(0, 4) as i:
                for j in range(4):
                    rkv_chunk(act, "act", i, j)
                need(act, i, "sinks_less_max")
                act.activation(es, es, ACT.Exp).then_inc(S("sink_exp"), 1)
                for h in range(4):
                    act.activation(sc[:, h, 0:128], sc[:, h, 0:128], ACT.Exp, bias=negm[:, h:h + 1],
                                   accum_out=sums[:, h:h + 1])
                    m = act.activation(sc[:, h, 128:384], sc[:, h, 128:384], ACT.Exp, bias=negm[:, 4 + h:5 + h],
                                       accum_out=sums[:, 4 + h:5 + h])
                m.then_inc(S("swa_exp"), 1)
                for j in range(4, 8):
                    rkv_chunk(act, "act", i, j)
                need(act, i, "probs_turned")
                act.activation(pt, mid[:, 0:3, :].rearrange("p b (u t) -> p (b u) t", t=P), ACT.Copy)\
                   .then_inc(S("pt_ready"), 1)
                for j in range(8, 12):
                    rkv_chunk(act, "act", i, j)
            act.wait_ge(S("mem_landed"), 16)
            for b in range(8):
                fill_act(act, MEM, "mem_norm", b, x, FILL_MEM)
            norm_act(act, MEM)
            with act.Fori(0, TC) as c:
                ts = bass.ds(c * L, L)
                rv, kv_, vv = rkv[:, 0:8, ts], rkv[:, 8:16, ts], rkv[:, 16:24, ts]

                def mem(*js):
                    for j in js:
                        mem_chunk(act, "act", c, j)
                plain(act)
                act.activation(tzc, lora[:, 0, ts], ACT.Copy).then_inc(S("tz_copied"), 1)
                act.wait_ge(S("rw_cleared"), 9)
                halves(act, Pm, vv, None)
                mem(0)
                need(act, c, "z_decay")
                act.activation(t1, t1, ACT.Sigmoid).then_inc(S("decay_sig"), 1)
                need(act, c, "z_a")
                act.activation(aa, aa, ACT.Sigmoid).then_inc(S("a_ready"), 1)
                need(act, c, "kk_raw")
                act.activation(t2, kk, ACT.Square).then_inc(S("kk_sq"), 1)
                mem(1)
                need(act, c, "kk_sum")
                act.activation(t2, b8[3], ACT.Sqrt).then_inc(S("kk_norm"), 1)
                need(act, c, "cum_ready")
                act.activation(Wx[:, :, 1:65], cum, ACT.Exp, scale=-DECAY)
                act.activation(Winv, cum, ACT.Exp, scale=DECAY).then_inc(S("W_ready"), 1)
                need(act, c, "a_scaled")
                halves(act, Abd, rhs[:, :, 0:64], "Abd_ready")
                mem(2, 3)
                need(act, c, "A_prod")
                act.activation(Araw, two[0], ACT.Copy).then_inc(S("A_ready"), 1)
                mem(4)
                need(act, c, "B_turned")
                act.activation(Bh, two[1], ACT.Copy).then_inc(S("BT_ready"), 1)
                need(act, c, "K_turned")
                act.activation(Kh, two[0], ACT.Copy).then_inc(S("KT_ready"), 1)
                need(act, c, "V_turned")
                act.activation(Vc, b8[2], ACT.Copy).then_inc(S("Vc_ready"), 1)
                mem(5)
                for n in range(5):
                    act.wait_ge(S("P_done"), c * 5 + n + 1)
                    act.activation(Pm, two[0], ACT.Copy).then_inc(S("P_ready"), 1)
                    mem(6 + n)
                need(act, c, "R_done")
                act.activation(Rc, b8[0], ACT.Copy).then_inc(S("R_ready"), 1)
                mem(11)
                need(act, c, "U_done")
                act.activation(Uc, b8[1], ACT.Copy).then_inc(S("U_ready"), 1)
                mem(12)
                need(act, c, "y_done")
                act.activation(cum, b8[2], ACT.Copy).then_inc(S("y_copied"), 1)
                need(act, c, "S_new")
                halves(act, Sbd, Sc, None)
                mem(13)
                need(act, c, "y_centred")
                act.activation(t2, t1, ACT.Square).then_inc(S("y_sq"), 1)
                mem(14)
                need(act, c, "y_var")
                act.activation(t2, t2, ACT.Sqrt).then_inc(S("y_root"), 1)
                mem(15)
                need(act, c, "chunk_done")
            for g in range(2):
                act.activation(hs[:, YT0 + 8 + 4 * g:YT0 + 12 + 4 * g, 0, :], q_all[:, 4 * g:4 * g + 4, :], ACT.Copy)\
                   .then_inc(S("y_high"), 1)
            for g in range(4):
                act.wait_ge(S("y_gated"), g + 1)
                act.activation(hs[:, YT0 + 2 * g:YT0 + 2 * g + 2, 0, :], rkv[:, 2 * g:2 * g + 2, :], ACT.Copy)\
                   .then_inc(S("y_high"), 1)
            with act.Fori(0, 4) as i:
                for u in range(2):
                    ahead(split_high, act, V_OUT + 4 * u, 4, i, 8)
                    resid_act(act, 1, B_OUT + u, V_OUT + 4 * u + 3, 2 * i + u, XA, "xa_norm", FILL_XA, i, 8)
            ahead(split_high, act, V_XQ, 4)
            norm_act(act, XA)
            copy_low(act, B_XQ, V_XQ + 3)
            with act.Fori(0, 3) as i:
                for u in range(1, 3):
                    ahead(split_high, act, V_XQ + 4 * u, 4, i, 8)
                    copy_low(act, B_XQ + u, V_XQ + 4 * u + 3, i, 8)
            ahead(split_high, act, V_XQ + 28, 4)
            copy_low(act, B_XQ + 7, V_XQ + 31)

            def x_exp(h):
                act.wait_ge(S("x_negmax"), h + 1)
                for q in range(2):
                    k = 2 * (h % 2) + q
                    m = act.activation(SX[:, k, :], b2[h % 2][:, q, :], ACT.Exp, scale=XSCALE,
                                       bias=xneg[:, k:k + 1], accum_out=xsum[:, k:k + 1])
                m.then_inc(S("x_exp"), 1)

            def x_out(h):
                act.wait_ge(S("x_turned"), h + 1)
                act.activation(PX[:, 2 * (h % 2):2 * (h % 2) + 2, :], b2[2], ACT.Copy).then_inc(S("x_probs"), 1)
                for g in range(2):
                    act.wait_ge(S("o_done"), 2 * h + g + 1)
                    a = YT0 + 4 * h + 2 * g
                    act.activation(hs[:, a:a + 2, 0, :], b2[3 - g], ACT.Copy).then_inc(S("o_high"), 1)
            x_exp(0)
            for h in range(4):
                if h < 3:
                    x_exp(h + 1)
                x_out(h)
            with act.Fori(0, 4) as i:
                for u in range(2):
                    ahead(split_high, act, V_XO + 4 * u, 4, i, 8)
                    resid_act(act, 2, B_XO + u, V_XO + 4 * u + 3, 2 * i + u, F2, "f2_norm", FILL_F2, i, 8)
            ahead(split_high, act, V_UP2, 4)
            norm_act(act, F2)
            ffn_act(act, 1, B_UP2, V_UP2, V_DOWN2)
            with act.Fori(0, 3) as i:
                for u in range(2):
                    ahead(split_high, act, V_DOWN2 + 12 * u, 12, i, 24)
                    resid_act(act, 3, B_DOWN2 + u, V_DOWN2 + 12 * u + 10, 2 * i + u, FINAL, None, None, i, 24)
            for u in range(6, 8):
                ahead(split_high, act, V_DOWN2 + 12 * u, 12)
                resid_act(act, 3, B_DOWN2 + u, V_DOWN2 + 12 * u + 10, u, FINAL, None, None)
            norm_act(act, FINAL)

        @block.vector
        def _(dve):
            dve.wait_ge(S("par_landed"), 16)
            for b in range(8):
                dve.wait_ge(S(f"x_landed{b // 2}"), 16)
                fill_dve(dve, "f1_norm", b, x, FILL_X)
                if b % 2:
                    split_low(dve, V_UP1 + b // 2)
            ahead(split_low, dve, V_UP1 + 1, 3)
            norm_dve(dve, X1)
            ffn_dve(dve, 0, B_UP1, V_UP1, V_DOWN1)
            with dve.Fori(0, 4) as i:
                for u in range(2):
                    ahead(split_low, dve, V_DOWN1 + 12 * u, 12, i, 24)
                    resid_dve(dve, 0, B_DOWN1 + u, 2 * i + u, "mix_norm", FILL_MIX, 0.5, None, i, 2)
            ahead(split_low, dve, V_Q, 4)
            norm_dve(dve, MIX)

            def scaled(b, dst, bias, k, name):
                add_low(dve, b)
                dve.tensor_tensor(dst, total[:, :, :], rb, ALU.mult).then_inc(S("dve_step"), 1)
                own(dve)
                a = PCOL[bias] + k
                dve.tensor_tensor(dst, dst, par[:, a:a + 2].unsqueeze(2).to_broadcast([P, 2, T]), ALU.add)\
                   .then_inc(S(name), 1)
            scaled(B_Q, q_all[:, 0:2, :], "b_q", 0, "q_in")
            for b in range(1, 4):
                ahead(split_low, dve, V_Q + 4 * b, 4)
                scaled(B_Q + b, q_all[:, 2 * b:2 * b + 2, :], "b_q", 2 * b, "q_in")
            ahead(split_low, dve, V_KV, 4)
            scaled(B_KV, k_v, "b_kv", 0, "kv_in")
            ahead(split_low, dve, V_LORA, 4)
            dve.wait_ge(S("swa_tables"), 16)
            need(dve, 0, "k_swapped", "kv_in")
            dve.tensor_tensor(ktmp, bank[0][:, 0:T], sc_("sin"), ALU.mult)
            dve.tensor_tensor(krot, k_v[:, 0, :], sc_("cos"), ALU.mult).then_inc(S("dve_step"), 1)
            own(dve)
            dve.tensor_tensor(krot, krot, ktmp, ALU.add).then_inc(S("k_rotated"), 1)

            def lora_part(b, dst, ntiles, mu):
                add_low(dve, b)
                need(dve, 0, "shift_cleared")
                shift_in(dve)
                for e in range(ntiles):
                    m = dve.scalar_tensor_tensor(dst[:, e, :], up[:, e, :], pc(mu, e), shifted[:, e, 1:257],
                                                 ALU.mult, ALU.add)
                m.then_inc(S("lora_ready"), 1)
            lora_part(B_LORA, lora[:, 0:2, :], 2, "mu_lora")
            ahead(split_low, dve, V_TAIL, 4)
            lora_part(B_TAIL, lora[:, 2:3, :], 1, "mu_tail")
            need(dve, 0, "vpad_ready")
            with dve.Fori(0, 4) as i:
                own.rounds(i, 13)
                qi = q_all[:, bass.ds(i * 2, 2), :]

                def rkvs(*js):
                    for j in js:
                        rkv_chunk(dve, "dve", i, j)
                cosb = sc_("cos").unsqueeze(1).to_broadcast([P, 2, T])
                sinb = sc_("sin").unsqueeze(1).to_broadcast([P, 2, T])
                need(dve, i, "q_swapped")
                dve.tensor_tensor(qtmp, b2[0], sinb, ALU.mult)
                dve.tensor_tensor(qg, qi, cosb, ALU.mult).then_inc(S("dve_step"), 1)
                own(dve)
                dve.tensor_tensor(qg, qg, qtmp, ALU.add).then_inc(S("q_rotated"), 1)
                dve.tensor_scalar(vg, vpad[:, bass.ds(i // 2, 1), :].rearrange("p a (b n) -> p (a b) n", n=P), 1.0, None,
                                  ALU.mult)\
                   .then_inc(S("vg_ready"), 1)
                rkvs(0, 1)
                for h in range(4):
                    dve.wait_ge(S("swa_scores"), i * 4 + h + 1)
                    m = dve.scalar_tensor_tensor(sc[:, h, :], bank[h][:, 0:384], HD ** -0.5, sc_("band"),
                                                 ALU.mult, ALU.add)
                m.then_inc(S("dve_step"), 1)
                own(dve)
                dve.reduce_max(mx[:, 0:4], sc[:, :, 0:128], AX_X)
                dve.reduce_max(mx[:, 4:8], sc[:, :, 128:384], AX_X).then_inc(S("dve_step"), 1)
                own(dve)
                sink = par[:, bass.ds(i * 4 + PCOL["sinks"], 4)].unsqueeze(1).to_broadcast([P, 2, 4])

                def pair4(s):
                    return s.rearrange("p (a b) -> p a b", b=4)
                dve.tensor_tensor(pair4(mx), pair4(mx), sink, ALU.max).then_inc(S("dve_step"), 1)
                own(dve)
                dve.tensor_scalar(negm, mx, -1.0, None, ALU.mult).then_inc(S("dve_step"), 1)
                own(dve)
                dve.tensor_tensor(pair4(es), sink, pair4(negm), ALU.add).then_inc(S("sinks_less_max"), 1)
                rkvs(2, 3)
                need(dve, i, "sink_exp", "swa_exp")
                dve.tensor_tensor(sums, sums, es, ALU.add).then_inc(S("dve_step"), 1)
                own(dve)
                dve.reciprocal(rden, sums).then_inc(S("dve_step"), 1)
                own(dve)
                dve.tensor_tensor(sc[:, :, 0:128], sc[:, :, 0:128], rden[:, 0:4].unsqueeze(2).to_broadcast([P, 4, 128]),
                                  ALU.mult)
                dve.tensor_tensor(sc[:, :, 128:384], sc[:, :, 128:384],
                                  rden[:, 4:8].unsqueeze(2).to_broadcast([P, 4, 256]), ALU.mult)\
                   .then_inc(S("swa_probs"), 1)
                rkvs(4, 5, 6, 7, 8)
                need(dve, i, "swa_out")
                dve.tensor_scalar(qi, b2[3], 1.0, None, ALU.mult).then_inc(S("swa_done"), 1)
                rkvs(9, 10, 11)
            own.end(4)
            dve.wait_ge(S("mem_landed"), 16)
            for b in range(8):
                fill_dve(dve, "mem_norm", b, x, FILL_MEM)
            norm_dve(dve, MEM)
            dve.memset(Yi, 0.0).then_inc(S("rw_cleared"), 1)
            dve.memset(Vbd, 0.0)
            dve.memset(Sbd, 0.0).then_inc(S("rw_cleared"), 1)
            dve.memset(Sc, 0.0).then_inc(S("rw_cleared"), 1)
            dve.memset(Wx[:, :, 0:1], 1.0).then_inc(S("rw_cleared"), 1)
            dve.wait_ge(S("rw_cleared"), 9)
            dve.wait_ge(S("rw_tables"), 48)
            with dve.Fori(0, TC) as c:
                own.rounds(c, 11)
                ts = bass.ds(c * L, L)
                rv, kv_, vv = rkv[:, 0:8, ts], rkv[:, 8:16, ts], rkv[:, 16:24, ts]

                def mem(*js):
                    for j in js:
                        mem_chunk(dve, "dve", c, j)
                dve.tensor_tensor(kk, kv_, per_unit("k_k"), ALU.mult).then_inc(S("kk_raw"), 1)
                need(dve, c, "lora_z")
                dve.tensor_tensor(t1, b8[0], per_unit("w0"), ALU.add).then_inc(S("z_decay"), 1)
                dve.tensor_tensor(aa, b8[1], per_unit("a0"), ALU.add).then_inc(S("z_a"), 1)
                mem(0)
                need(dve, c, "decay_sig")
                for u in range(UN):
                    m = dve.tensor_tensor_scan(cum[:, u, :], t1[:, u, :], t1[:, u, :], 0.0, ALU.add, ALU.max)
                m.then_inc(S("cum_ready"), 1)
                mem(1)
                need(dve, c, "kk_norm")
                dve.tensor_scalar(t2, t2, 1e-12, None, ALU.max).then_inc(S("dve_step"), 1)
                own(dve)
                dve.reciprocal(t2, t2).then_inc(S("dve_step"), 1)
                own(dve)
                need(dve, c, "kk_raw")
                dve.tensor_tensor(kk, kk, t2, ALU.mult)
                need(dve, c, "a_ready", "cum_ready")
                dve.scalar_tensor_tensor(t1, aa, -1.0, per_unit("k_a"), ALU.add, ALU.mult).then_inc(S("dve_step"), 1)
                own(dve)
                dve.scalar_tensor_tensor(kv_, t1, 1.0, kv_, ALU.add, ALU.mult).then_inc(S("dve_step"), 1)
                own(dve)
                need(dve, c, "W_ready")
                dve.scalar_tensor_tensor(rhs[:, :, 0:64], kk, -1.0, Wx[:, :, 0:64], ALU.mult, ALU.mult)\
                   .then_inc(S("a_scaled"), 1)
                dve.tensor_tensor(rhs[:, :, 64:128], rv, Wx[:, :, 1:65], ALU.mult)
                dve.tensor_tensor(aa, kk, aa, ALU.mult).then_inc(S("dve_step"), 1)
                own(dve)
                halves(dve, Bh, aa, "B_scaled", scale=Winv)
                halves(dve, Kh, kv_, "K_scaled", scale=Winv)
                mem(2)
                gT = two[0][:, :, 0:64]
                need(dve, c, "B_prod")
                halves(dve, Yi, gT, "dve_step", mask=rc("pair_t"))
                dve.tensor_tensor(ArbT, two[0][:, :, 64:128], bcast(rc("upto_t")), ALU.mult)\
                   .then_inc(S("Arb_ready"), 1)
                own(dve)
                dve.tensor_tensor(Yi, Yi, ident[:, :].unsqueeze(1).to_broadcast([P, UN, P]), ALU.add)\
                   .then_inc(S("Y_init"), 1)
                mem(3)
                need(dve, c, "K_prod")
                halves(dve, AakT, two[1][:, :, 0:64], None, mask=rc("before_t"))
                dve.tensor_tensor(ArkT, two[1][:, :, 64:128], bcast(rc("upto_t")), ALU.mult)\
                   .then_inc(S("Ark_ready"), 1)
                mem(4)
                need(dve, c, "Vc_ready")
                halves(dve, Vbd, Vc, None)
                mem(5)
                for n, b in enumerate(LEVELS):
                    dve.wait_ge(S("Y_more"), c * 5 + n + 1)
                    if True:
                        yo = Yi.rearrange("p u (n two b) -> p (u n) two b", two=2, b=b)[:, :, 1, :]
                        dve.tensor_tensor(yo, yo, bank[2].rearrange("p (n b) -> p n b", b=b), ALU.add)\
                           .then_inc(S("Y_level"), 1)
                    if n < 4:
                        dve.wait_ge(S("X_more"), c * 4 + n + 1)
                        xo = Xi.rearrange("p u (n two b) -> p (u n) two b", two=2, b=b)[:, :, 0, :]
                        dve.tensor_tensor(xo, xo, bank[3].rearrange("p (n b) -> p n b", b=b), ALU.add)\
                           .then_inc(S("X_level"), 1)
                    mem(6 + n)
                mem(11)
                need(dve, c, "U_ready")
                halves(dve, Ubd, Uc, "Ubd_ready")
                mem(12)
                need(dve, c, "S_done")
                dve.tensor_tensor(Sc, Sc, b8[3], ALU.add).then_inc(S("S_sum"), 1)
                need(dve, c, "S_sum")
                dve.tensor_tensor(Sc, Sc, Wx[:, :, 64:65].to_broadcast([P, UN, L]), ALU.mult).then_inc(S("S_new"), 1)
                need(dve, c, "U_done")
                dve.tensor_tensor(kk, rv, kv_, ALU.mult).then_inc(S("dve_step"), 1)
                own(dve)
                dve.tensor_tensor(kk, kk, per_unit("r_k"), ALU.mult).then_inc(S("rkr"), 1)
                mem(13)
                need(dve, c, "y_sum", "y_copied")
                dve.scalar_tensor_tensor(t1, b8[0], -1.0 / HD, cum, ALU.mult, ALU.add).then_inc(S("y_centred"), 1)
                mem(14)
                need(dve, c, "y_sqsum")
                dve.tensor_scalar(t2, b8[1], 1.0 / HD, GN_EPS, ALU.mult, ALU.add).then_inc(S("y_var"), 1)
                need(dve, c, "bonus_sum")
                dve.tensor_tensor(kk, b8[3], vv, ALU.mult)
                mem(15)
                need(dve, c, "y_root")
                dve.reciprocal(t2, t2).then_inc(S("dve_step"), 1)
                own(dve)
                dve.tensor_tensor(t1, t1, t2, ALU.mult).then_inc(S("dve_step"), 1)
                own(dve)
                dve.tensor_tensor(t1, t1, per_unit("lnx_w"), ALU.mult).then_inc(S("dve_step"), 1)
                own(dve)
                dve.tensor_tensor(t1, t1, per_unit("lnx_b"), ALU.add).then_inc(S("dve_step"), 1)
                own(dve)
                dve.tensor_tensor(rv, t1, kk, ALU.add).then_inc(S("chunk_done"), 1)
                need(dve, c, "chunk_done")
            own.end(TC)
            for g in range(2):
                need(dve, g, "y_high")
                t = slice(YT0 + 8 + 4 * g, YT0 + 12 + 4 * g)
                dve.tensor_tensor(hs[:, t, 1, :], q_all[:, 4 * g:4 * g + 4, :], hs[:, t, 0, :].bitcast(F32),
                                  ALU.subtract).then_inc(S("y_split"), 1)
            need(dve, 3, "chunk_done")
            for g in range(4):
                need(dve, g, "gate_done")
                dve.tensor_tensor(rkv[:, 2 * g:2 * g + 2, :], rkv[:, 2 * g:2 * g + 2, :], b2[g], ALU.mult)\
                   .then_inc(S("y_gated"), 1)
            for g in range(4):
                need(dve, 2 + g, "y_high")
                need(dve, g, "y_gated")
                t = slice(YT0 + 2 * g, YT0 + 2 * g + 2)
                dve.tensor_tensor(hs[:, t, 1, :], rkv[:, 2 * g:2 * g + 2, :], hs[:, t, 0, :].bitcast(F32),
                                  ALU.subtract).then_inc(S("y_split"), 1)
            dve.wait_ge(S("x_back"), 16)
            with dve.Fori(0, 4) as i:
                for u in range(2):
                    ahead(split_low, dve, V_OUT + 4 * u, 4, i, 8)
                    resid_dve(dve, 1, B_OUT + u, 2 * i + u, "xa_norm", FILL_XA, 1.0, "b_out", i, 2)
            ahead(split_low, dve, V_XQ, 4)
            norm_dve(dve, XA)

            def x_query(b, blk, i=0):
                add_low(dve, b, i, 2)
                dve.tensor_tensor(QX[:, bass.ds(2 * blk, 2), :], total[:, :, :], rb, ALU.mult).then_inc(S("xq_ready"), 1)
            x_query(B_XQ, 0)
            with dve.Fori(0, 3) as i:
                for u in range(1, 3):
                    ahead(split_low, dve, V_XQ + 4 * u, 4, i, 8)
                    x_query(B_XQ + u, 2 * i + u, i)
            ahead(split_low, dve, V_XQ + 28, 4)
            x_query(B_XQ + 7, 7)

            def x_max(h):
                k = 2 * (h % 2)
                dve.wait_ge(S("x_scores"), h + 1)
                dve.reduce_max(xmax[:, k:k + 2], b2[h % 2], AX_X).then_inc(S("dve_step"), 1)
                own(dve)
                dve.tensor_scalar(xneg[:, k:k + 2], xmax[:, k:k + 2], -XSCALE, None, ALU.mult)\
                   .then_inc(S("x_negmax"), 1)

            def x_norm(h):
                k = 2 * (h % 2)
                dve.wait_ge(S("x_exp"), h + 1)
                dve.reciprocal(xrec[:, k:k + 2], xsum[:, k:k + 2]).then_inc(S("dve_step"), 1)
                own(dve)
                dve.tensor_tensor(SX[:, k:k + 2, :], SX[:, k:k + 2, :],
                                  xrec[:, k:k + 2].unsqueeze(2).to_broadcast([P, 2, T]), ALU.mult)\
                   .then_inc(S("x_normed"), 1)

            def x_out(h):
                for g in range(2):
                    need(dve, 2 * h + g, "o_high")
                    a = YT0 + 4 * h + 2 * g
                    dve.tensor_tensor(hs[:, a:a + 2, 1, :], b2[3 - g], hs[:, a:a + 2, 0, :].bitcast(F32),
                                      ALU.subtract).then_inc(S("o_split"), 1)
            x_max(0)
            x_norm(0)
            for h in range(4):
                if h < 3:
                    x_max(h + 1)
                    x_norm(h + 1)
                x_out(h)
            with dve.Fori(0, 4) as i:
                for u in range(2):
                    ahead(split_low, dve, V_XO + 4 * u, 4, i, 8)
                    resid_dve(dve, 2, B_XO + u, 2 * i + u, "f2_norm", FILL_F2, 1.0, None, i, 2)
            ahead(split_low, dve, V_UP2, 4)
            norm_dve(dve, F2)
            ffn_dve(dve, 1, B_UP2, V_UP2, V_DOWN2)
            with dve.Fori(0, 3) as i:
                for u in range(2):
                    ahead(split_low, dve, V_DOWN2 + 12 * u, 12, i, 24)
                    resid_dve(dve, 3, B_DOWN2 + u, 2 * i + u, None, None, 0.5, None, i, 2)
            for u in range(6, 8):
                ahead(split_low, dve, V_DOWN2 + 12 * u, 12)
                resid_dve(dve, 3, B_DOWN2 + u, u, None, None, 0.5)
            norm_dve(dve, FINAL)
            for k in range(KT):
                m = dve.scalar_tensor_tensor(x[:, k, :], x[:, k, :], pc("final_norm", k), rstd[:, :], ALU.mult, ALU.mult)
                if k % 4 == 3:
                    m.then_inc(S("out_ready"), 1)

        @block.tensor
        def _(pe):
            need(pe, 0, "ones_ready")
            pe.wait_ge(S("ident_landed"), 16)
            ffn_pe(pe, 0, B_UP1, V_UP1, V_DOWN1, X1, FILL_X)
            with pe.Fori(0, 4) as i:
                for u in range(2):
                    products(pe, B_DOWN1 + u, V_DOWN1 + 12 * u, 11, hs, hidden(0), i, 24, 2)
            products(pe, B_Q, V_Q, 4, xs, filled(FILL_MIX))
            norm_pe(pe, MIX)
            for b in range(1, 4):
                products(pe, B_Q + b, V_Q + 4 * b, 4, xs)
            products(pe, B_KV, V_KV, 4, xs)
            products(pe, B_LORA, V_LORA, 4, xs)
            pe.wait_ge(S("swa_tables"), 16)
            need(pe, 0, "kv_in")
            pe.matmul(bank[0][:, 0:T], sc_("swap"), k_v[:, 0, :], start=True, stop=True).then_inc(S("k_swapped"), 1)
            for e in range(2):
                m = pe.transpose(bank[1][:, e * P:(e + 1) * P], k_v[:, 1, e * P:(e + 1) * P], ident[:, :])
            m.then_inc(S("v_turned"), 1)
            need(pe, 0, "k_rotated")
            for n in range(4):
                m = pe.matmul(b2[2 + n // 2][:, n % 2, :], sc_("select")[:, n * P:(n + 1) * P], krot,
                              start=True, stop=True)
            m.then_inc(S("k_selected"), 1)
            for t in range(KT):
                if t == 0:
                    pe.wait_ge(bank_free[0], 1 + B.before(B_TAIL))
                if t % 8 == 0:
                    pe.wait_ge(low_ready[(V_TAIL + t // 8) % RING], W.uses(V_TAIL + t // 8))
                s, a, c0 = (V_TAIL + t // 8) % RING, t % 8 // 2, t % 2 * P
                pe.matmul(acc[0][:, 0, :, :], parts[:, s, a, 0, c0:c0 + P], xs[:, t, :, :],
                          start=t == 0, stop=False, skip_group_check=True)
                m = pe.matmul(acc[0][:, 0, 1, :], parts[:, s, a, 1, c0:c0 + P], xs[:, t, 0, :],
                              start=False, stop=t == KT - 1, skip_group_check=True)
                if t % 8 == 7:
                    m.then_inc(parts_used[s], 1)
            need(pe, 3, "q_in")
            need(pe, 0, "kpad_ready")
            need(pe, 0, "vpad_ready")
            with pe.Fori(0, 4) as i:
                def rkvs(*js):
                    for j in js:
                        rkv_chunk(pe, "pe", i, j)
                pe.matmul(bank[0], sc_("swap"), q_all[:, bass.ds(i * 2, 2), :], start=True, stop=True)\
                  .then_inc(S("q_swapped"), 1)
                rkvs(0, 1)
                need(pe, i, "q_rotated")
                for h in range(4):
                    kp = kpad[:, bass.ds(i // 2 * 2 + h % 2, 1), :]
                    pe.matmul(bank[h][:, 0:128], qg[:, h // 2, 0:128], kp[:, :, 0:128], start=True, stop=True)
                    pe.matmul(bank[h][:, 128:384], qg[:, h // 2, 128:256], kp[:, :, :], start=True, stop=True)\
                      .then_inc(S("swa_scores"), 1)
                rkvs(2, 3, 4, 5, 6)
                need(pe, i, "swa_probs")
                for piece in range(3):
                    for h in range(4):
                        m = pe.transpose(bank[piece][:, h * P:(h + 1) * P], sc[:, h, piece * P:(piece + 1) * P],
                                         ident[:, :])
                m.then_inc(S("probs_turned"), 1)
                rkvs(7, 8)
                need(pe, i, "pt_ready", "vg_ready")
                for e in range(2):
                    for q in range(2):
                        terms = [(0, o, 0) for o in range(2)] if q == 0 else \
                            [(blk, o, 1 + blk) for o in range(2) for blk in range(2)]
                        for n, (blk, o, piece) in enumerate(terms):
                            m = pe.matmul(b2[3][:, e, q * P:(q + 1) * P], vg[:, 2 * blk + o, :],
                                          pt[:, 4 * piece + 2 * e + o, :], start=n == 0, stop=n == len(terms) - 1)
                m.then_inc(S("swa_out"), 1)
                rkvs(9, 10, 11)
                need(pe, i, "swa_done")
            norm_pe(pe, MEM)
            pe.wait_ge(S("rw_cleared"), 9)
            pe.wait_ge(S("rw_tables"), 48)
            need(pe, 0, "lora_act")
            with pe.Fori(0, TC) as c:
                def mem(*js):
                    for j in js:
                        mem_chunk(pe, "pe", c, j)

                def units(dst, lhs, rh, name, last=True, first=True, wide=False):
                    for u in range(UN):
                        m = pe.matmul(dst(u), lhs(u), rh(u), start=first, stop=last, skip_group_check=True)
                    if name:
                        m.then_inc(S(name), 1)
                need(pe, c, "tz_copied")
                for h in range(2):
                    rows = slice(64 * h, 64 * h + 64)
                    for u in range(UN):
                        m = pe.matmul(b8[h][:, u, :], daw[rows, u * P:(u + 1) * P], tzc[rows, :], start=True, stop=True)
                m.then_inc(S("lora_z"), 1)
                mem(0)
                need(pe, c, "kk_sq")
                pe.matmul(bank[3], rc("same_head"), t2, start=True, stop=True).then_inc(S("kk_sum"), 1)
                mem(1, 2)
                need(pe, c, "B_scaled")
                units(lambda u: two[0][:, u, :], lambda u: Bh[:, u, :], lambda u: rhs[:, u, :], "B_prod")
                need(pe, c, "K_scaled", "kk_norm")
                units(lambda u: two[1][:, u, :], lambda u: Kh[:, u, :], lambda u: rhs[:, u, :], "K_prod")
                mem(3)
                need(pe, c, "Abd_ready", "Arb_ready")
                units(lambda u: two[0][:, u, :], lambda u: Abd[:, u, :], lambda u: Bh[:, u, :], "A_prod")
                mem(4)
                need(pe, c, "Ark_ready")
                for u in range(UN):
                    m = pe.transpose(two[1][:, u, :], Bh[:, u, :], ident[:, :])
                m.then_inc(S("B_turned"), 1)
                need(pe, c, "A_ready")
                for u in range(UN):
                    m = pe.transpose(two[0][:, u, :], Kh[:, u, :], ident[:, :])
                m.then_inc(S("K_turned"), 1)
                need(pe, c, "BT_ready")
                units(lambda u: b8[2][:, u, :], lambda u: Pm[:, u, :], lambda u: rc("stack"), "V_turned")
                mem(5)
                need(pe, c, "KT_ready", "Vc_ready", "Y_init")
                for n, b in enumerate(LEVELS):
                    pe.wait_ge(S("Am"), c * 5 + n + 1)
                    if n:
                        pe.wait_ge(S("Y_level"), c * 5 + n)
                        pe.wait_ge(S("X_level"), c * 4 + n)
                    units(lambda u: two[0][:, u, :], lambda u: Am[:, u, :], lambda u: Yi[:, u, :], "P_done")
                    mem(6 + n)
                    pe.wait_ge(S("P_ready"), c * 5 + n + 1)
                    units(lambda u: b8[2][:, u, :], lambda u: Xi[:, u, :], lambda u: odd(Pm[:, u, :], b, 1), "Y_more")
                    if n < 4:
                        units(lambda u: b8[3][:, u, :], lambda u: Pm[:, u, :], lambda u: odd(Xi[:, u, :], b, 0),
                              "X_more")
                for u in range(UN):
                    pe.matmul(b8[0][:, u, :], Abd[:, u, :], Sc[:, u, :], start=True, stop=False, skip_group_check=True)
                    m = pe.matmul(b8[0][:, u, :], AakT[:, u, :], Vc[:, u, :], start=False, stop=True,
                                  skip_group_check=True)
                m.then_inc(S("R_done"), 1)
                mem(11)
                need(pe, c, "R_ready")
                pe.wait_ge(S("Y_level"), c * 5 + 5)
                units(lambda u: b8[1][:, u, :], lambda u: Yi[:, u, :], lambda u: Rc[:, u, :], "U_done")
                mem(12)
                need(pe, c, "Ubd_ready")
                for u in range(UN):
                    pe.matmul(b8[2][:, u, :], Sbd[:, u, :], rhs[:, u, 64:128], start=True, stop=False,
                              skip_group_check=True)
                    pe.matmul(b8[2][:, u, :], Vbd[:, u, :], ArkT[:, u, :], start=False, stop=False,
                              skip_group_check=True)
                    m = pe.matmul(b8[2][:, u, :], Ubd[:, u, :], ArbT[:, u, :], start=False, stop=True,
                                  skip_group_check=True)
                m.then_inc(S("y_done"), 1)
                for u in range(UN):
                    pe.matmul(b8[3][:, u, :], Bh[:, u, :], Uc[:, u, :], start=True, stop=False, skip_group_check=True)
                    m = pe.matmul(b8[3][:, u, :], Kh[:, u, :], Vc[:, u, :], start=False, stop=True,
                                  skip_group_check=True)
                m.then_inc(S("S_done"), 1)
                mem(13)
                need(pe, c, "y_copied")
                pe.matmul(bank[0], rc("same_head"), cum, start=True, stop=True).then_inc(S("y_sum"), 1)
                need(pe, c, "rkr", "S_sum")
                pe.matmul(bank[3], rc("same_head"), kk, start=True, stop=True).then_inc(S("bonus_sum"), 1)
                mem(14)
                need(pe, c, "y_sq")
                pe.matmul(bank[1], rc("same_head"), t2, start=True, stop=True).then_inc(S("y_sqsum"), 1)
                mem(15)
                need(pe, c, "chunk_done")
            pe.wait_ge(S("gup_landed"), 32)
            need(pe, 0, "gup_cleared")
            for g in range(4):
                for e in range(2):
                    u = 2 * g + e
                    pe.matmul(b2[g][:, e, :], gup[:, 0, u * P:(u + 1) * P], lora[:, 1, :], start=True, stop=False,
                              skip_group_check=True)
                    m = pe.matmul(b2[g][:, e, :], gup[:, 1, u * P:(u + 1) * P], lora[:, 2, :], start=False, stop=True,
                                  skip_group_check=True)
                m.then_inc(S("gate_done"), 1)

            def mixed(pe, j):
                pe.wait_ge(S("y_split"), (1, 2, 4, 6)[j])
            with pe.Fori(0, 4) as i:
                for u in range(2):
                    products(pe, B_OUT + u, V_OUT + 4 * u, 4, hs, mixed, i, 8, 2, first_tile=YT0, order=(2, 3, 0, 1))
            products(pe, B_XQ, V_XQ, 4, xs, filled(FILL_XA))
            norm_pe(pe, XA)
            with pe.Fori(0, 3) as i:
                for u in range(1, 3):
                    products(pe, B_XQ + u, V_XQ + 4 * u, 4, xs, None, i, 8, 2)
            products(pe, B_XQ + 7, V_XQ + 28, 4, xs)
            pe.wait_ge(S("kv_back"), 32)

            def x_scores(h):
                pe.wait_ge(S("xq_ready"), 2 * h + 2)
                if h >= 2:
                    pe.wait_ge(S("x_exp"), h - 1)
                for q in range(2):
                    for t in range(4):
                        m = pe.matmul(b2[h % 2][:, q, :], QX[:, 4 * h + t, q * P:(q + 1) * P], KX[:, 4 * h + t, :],
                                      start=t == 0, stop=t == 3)
                m.then_inc(S("x_scores"), 1)

            def x_out(h):
                pe.wait_ge(S("x_normed"), h + 1)
                if h:
                    pe.wait_ge(S("o_split"), 2 * h)
                for q in range(2):
                    for t in range(2):
                        m = pe.transpose(b2[2][:, t, q * P:(q + 1) * P], SX[:, 2 * (h % 2) + q, t * P:(t + 1) * P],
                                         ident[:, :])
                m.then_inc(S("x_turned"), 1)
                pe.wait_ge(S("x_probs"), h + 1)
                for g in range(2):
                    for e in range(2):
                        a = h * 512 + (2 * g + e) * P
                        for t in range(2):
                            m = pe.matmul(b2[3 - g][:, e, :], VX[:, t, a:a + P], PX[:, 2 * (h % 2) + t, :],
                                          start=t == 0, stop=t == 1)
                    m.then_inc(S("o_done"), 1)
            x_scores(0)
            x_scores(1)
            for h in range(4):
                x_out(h)
                if h < 2:
                    x_scores(h + 2)

            def attended(pe, j):
                pe.wait_ge(S("o_split"), 2 * (j + 1))
            with pe.Fori(0, 4) as i:
                for u in range(2):
                    products(pe, B_XO + u, V_XO + 4 * u, 4, hs, attended, i, 8, 2, first_tile=YT0)
            ffn_pe(pe, 1, B_UP2, V_UP2, V_DOWN2, F2, FILL_F2)
            with pe.Fori(0, 4) as i:
                for u in range(2):
                    products(pe, B_DOWN2 + u, V_DOWN2 + 12 * u, 11, hs, hidden(1), i, 24, 2)
            norm_pe(pe, FINAL)


def kernel(**inputs):
    import numpy as _np
    import concourse.bacc as _bacc
    from concourse import mybir as _mybir
    from concourse.bass_utils import run_bass_kernel_spmd as _run

    nc = _bacc.Bacc("TRN2", target_bir_lowering=False, num_devices=1)
    f = {k: _np.asarray(v) for k, v in inputs.items()}
    arrays, A = {}, {}

    def dram(name, a):
        arrays[name] = _np.ascontiguousarray(a)
        A[name] = nc.dram_tensor(name, a.shape, _mybir.dt.from_np(a.dtype), kind="ExternalInput").ap()

    def tiles(a):
        return a.reshape(-1, P).T
    mu = f["rw_mu"][0]
    columns_of = {
        "b_out": tiles(f["b_out"][0]), "b_q": tiles(f["b_in_attn"][0, :1024]), "b_kv": tiles(f["b_in_attn"][0, 1024:]),
        "mu": tiles(mu[:3 * C]), "mu_lora": tiles(mu[LORA_COL:LORA_COL + 256]),
        "mu_tail": tiles(mu[TAIL_COL:TAIL_COL + P]), "w0": tiles(f["rw_w0"][0]), "a0": tiles(f["rw_a0"][0]),
        "k_k": tiles(f["rw_k_k"][0]), "k_a": tiles(f["rw_k_a"][0]), "r_k": tiles(f["rw_r_k"][0]),
        "lnx_w": tiles(f["rw_lnx_w"][0]), "lnx_b": tiles(f["rw_lnx_b"][0]),
        "sinks": _np.broadcast_to(f["attn_sinks"][0], (P, 16)), "final_norm": tiles(f["final_norm"]),
    }
    for n in ("f1_norm", "mix_norm", "mem_norm", "xa_norm", "f2_norm"):
        columns_of[n] = tiles(f[n][0])
    dram("params", _np.concatenate([columns_of[n] for n, _ in PARAMS], axis=1))
    dram("swa_consts", swa_consts())
    dram("rw_consts", rw_consts())
    dram("ident", _np.eye(P, dtype=_np.float32))
    dram("x_t", f["x"][0].T)
    dram("mem_t", f["mem"][0].T)
    for n in ("f1_gate", "f1_up", "f1_down", "w_in", "w_out", "w_xq", "w_xkv", "w_xo", "f2_gate", "f2_up", "f2_down",
              "rw_decay_up", "rw_aaa_up", "rw_gate_up"):
        dram(n, f[n][0])
    out = nc.dram_tensor("out_t", (D, T), _mybir.dt.float32, kind="ExternalOutput").ap()
    build(nc, A, out)
    r = _run(nc, [arrays], core_ids=[0])
    return _np.ascontiguousarray(r.results[0]["out_t"].T).reshape(1, T, D)
```

```python
from contextlib import ExitStack

import numpy as np
import concourse.bass as bass
from concourse import mybir

F32 = mybir.dt.float32
F32R = mybir.dt.float32r
ALU = mybir.AluOpType
ACT = mybir.ActivationFunctionType
AX_X = mybir.AxisListType.X

P = 128
D = 2048
T = 256
KT = D // P
D_FF = 5632
FT = D_FF // P
RMS_EPS = 1e-6
GN_EPS = 64e-5
HD = 64
C = 1024
UN = C // P
LORA_COL = 3 * C
GATE_COL = LORA_COL + 128
TAIL_COL = GATE_COL + 32
Q_COL = GATE_COL + 160
KV_COL = Q_COL + 1024
L = 64
TC = T // L
LEVELS = [2, 4, 8, 16, 32]
DECAY = float(np.exp(-0.5))

COLS = 2 * P
KC = 4
CHUNK = KC * COLS
RING = 4
LEAD = 3
STEPS = D_FF // COLS

PARAMS = [("f1_norm", 16), ("mix_norm", 16), ("mem_norm", 16), ("xa_norm", 16), ("f2_norm", 16), ("final_norm", 16),
          ("b_out", 16), ("b_q", 8), ("b_kv", 2), ("mu", 24), ("mu_lora", 2), ("mu_tail", 1), ("w0", 8), ("a0", 8),
          ("k_k", 8), ("k_a", 8), ("r_k", 8), ("lnx_w", 8), ("lnx_b", 8), ("sinks", 16)]
PCOL = {}
for _n, _k in PARAMS:
    PCOL[_n] = sum(k for _, k in PARAMS[:len(PCOL)])
NPAR = sum(k for _, k in PARAMS)

SWA_CONSTS = [("swap", 128), ("select", 512), ("cos", 256), ("sin", 256), ("band", 384)]
RW_CONSTS = [("stack", 64), ("same_head", 128), ("pair", 128), ("level", 640), ("pair_t", 64), ("before_t", 64),
             ("upto_t", 64)]


def columns(spec):
    at, out = 0, {}
    for n, k in spec:
        out[n] = (at, at + k)
        at += k
    return out, at


def swa_consts():
    p = np.arange(P)
    swap = np.zeros((P, P), np.float32)
    swap[p, p ^ 32] = 1.0
    select = np.zeros((P, 4, P), np.float32)
    for g in range(2):
        for e in range(2):
            select[g * HD + np.arange(HD), 2 * g + e, e * HD + np.arange(HD)] = 1.0
    freq = (np.float32(10000.0) ** (-np.arange(0, HD, 2, dtype=np.float32) / np.float32(HD))).astype(np.float32)
    ang = np.arange(T, dtype=np.float32)[None, :] * freq[p % 32][:, None]
    cos, sin = np.cos(ang), np.sin(ang) * np.where(p % HD < 32, -1.0, 1.0)[:, None]
    q = np.arange(P)[:, None]
    k = np.arange(P)[None, :]
    own = np.where(q >= k, 0.0, -1e30)
    prev = np.where(q < k, 0.0, -1e30)
    band = np.concatenate([own, prev, own], axis=1)
    return np.concatenate([swap, select.reshape(P, -1), cos, sin, band], axis=1).astype(np.float32)


def rw_consts():
    p = np.arange(P)
    h, t = p // L, p % L
    stack = (t[:, None] == np.arange(L)[None, :])
    same = h[:, None] == h[None, :]

    def off(b, row, col):
        return (row // (2 * b) == col // (2 * b)) & (row // b % 2 == 1) & (col // b % 2 == 0)
    pair = same & off(1, t[:, None], t[None, :])
    level = [same & off(b, t[:, None], t[None, :]) for b in LEVELS]
    c = np.arange(L)
    pair_t = off(1, c[None, :], t[:, None])
    before_t = t[:, None] < c[None, :]
    upto_t = t[:, None] <= c[None, :]
    return np.concatenate([stack, same, pair] + level + [pair_t, before_t, upto_t], axis=1).astype(np.float32)


class Weights:

    def __init__(self):
        self.real = []

    def add(self, pattern, times=1):
        first = len(self.real)
        self.real += list(pattern) * times
        return first

    def count(self, v):
        return sum(self.real[u] for u in range(v % RING, min(v + 1, len(self.real)), RING))

    def uses(self, v, i=0, per=0):
        n = self.count(v)
        if isinstance(i, int) and i == 0:
            return n
        return i * (self.count(v + per) - n) + n

    def missing(self, v):
        return v >= len(self.real) or not self.real[v]


class Blocks:

    def __init__(self):
        self.pair = []

    def add(self, pairs, times=1):
        first = len(self.pair)
        self.pair += list(pairs) * times
        return first

    def before(self, b, i=0, nb=0):
        n = sum(q == self.pair[b] for q in self.pair[:b])
        if isinstance(i, int) and i == 0:
            return n
        return i * (sum(q == self.pair[b] for q in self.pair[:b + nb]) - n) + n


class Own:

    def __init__(self, sem):
        self.sem, self.n, self.i, self.per = sem, 0, 0, 0

    def __call__(self, eng):
        self.n += 1
        eng.wait_ge(self.sem, self.i * self.per + self.n if self.per else self.n)

    def rounds(self, i, per):
        self.i, self.per, self.start = i, per, self.n

    def end(self, rounds):
        assert self.n == self.start + self.per, (self.n - self.start, self.per)
        self.n, self.per = self.start + rounds * self.per, 0


def build(nc, A, out):
    W, B = Weights(), Blocks()
    full = [True] * 4
    V_UP1, B_UP1 = W.add(full, 2 * STEPS), B.add([0, 1], STEPS)
    V_DOWN1, B_DOWN1 = W.add([True] * 11 + [False], 8), B.add([0, 1], 4)
    V_Q, B_Q = W.add(full, 4), B.add([0, 1], 2)
    V_KV, B_KV = W.add(full), B.add([0])
    V_LORA, B_LORA = W.add(full), B.add([1])
    V_TAIL, B_TAIL = W.add([True, True, False, False]), B.add([0])
    V_RKV, B_RKV = W.add(full, 12), B.add([1, 0, 1], 4)
    V_MEM, B_MEM = W.add(full, 16), B.add([0, 1], 8)
    V_OUT, B_OUT = W.add(full, 8), B.add([0, 1], 4)
    V_XQ, B_XQ = W.add(full, 8), B.add([0, 1], 4)
    V_XO, B_XO = W.add(full, 8), B.add([0, 1], 4)
    V_UP2, B_UP2 = W.add(full, 2 * STEPS), B.add([0, 1], STEPS)
    V_DOWN2, B_DOWN2 = W.add([True] * 11 + [False], 8), B.add([0, 1], 4)
    X1, MIX, MEM, XA, F2, FINAL = range(6)
    FILL_X, FILL_MIX, FILL_MEM, FILL_XA, FILL_F2 = range(5)

    ctx = ExitStack()
    with ctx:
        def sb(name, shape, dt=F32):
            return ctx.enter_context(nc.sbuf_tensor(name, shape, dt))

        sems = {}

        def S(name):
            if name not in sems:
                sems[name] = ctx.enter_context(nc.semaphore(name))
            return sems[name]

        def need(eng, i, *names):
            for n in names:
                eng.wait_ge(S(n), i + 1)

        raw = sb("raw", [P, RING, CHUNK])
        parts = sb("parts", [P, RING, KC, 2, COLS], F32R)
        xs = sb("xs", [P, KT, 2, T], F32R)
        par = sb("par", [P, NPAR])
        low = sb("low", [P, 2, 2, T])
        total = sb("total", [P, 2, T])
        gate = sb("gate", [P, 2, T])
        sig = sb("sig", [P, 2, T])
        up = sb("up", [P, 2, T])
        sq = sb("sq", [P, 2, T])
        sqacc = sb("sqacc", [P, T])
        ones = sb("ones", [P, P])
        ident = sb("unit", [P, P])
        ms = sb("ms", [P, T])
        rstd = sb("rstd", [P, T])
        small = sb("small", [P, 152])
        rcol = sb("rcol", [P, 2])
        HS_AT = KT * T
        M_WORDS = 27632
        at = -(-nc.sbuf_base // 32) * 32
        M = sb("M", [P, M_WORDS])
        hs = nc.alloc_sbuf_tensor_at("hs", [P, FT, 2, T], F32R, offset=at + 4 * HS_AT)

        def view(words, *dims):
            a = cursor[0]
            cursor[0] += words
            assert cursor[0] <= M_WORDS, cursor[0]
            v = M[:, a:a + words]
            if len(dims) == 2:
                v = v.rearrange("p (a b) -> p a b", b=dims[1])
            if len(dims) == 3:
                v = v.rearrange("p (a b c) -> p a b c", b=dims[1], c=dims[2])
            return v

        cursor = [0]
        x = view(HS_AT, KT, T)
        rkv = view(24 * T, 24, T)
        lora = view(3 * T, 3, T)
        q_all = view(UN * T, UN, T)
        WORK = cursor[0]
        swc, nsw = columns(SWA_CONSTS)
        swt = view(nsw)
        k_v = view(2 * T, 2, T)
        krot = view(T)
        ktmp = view(T)
        kpad = view(4 * T, 4, T)
        vpad = view(2 * 512, 2, 512)
        vg = view(512, 4, P)
        qg = view(512, 2, T)
        qtmp = view(512, 2, T)
        sc = view(4 * 384, 4, 384)
        pt = view(12 * P, 12, P)
        shifted = view(2 * 257 + 6)[:, 0:514].rearrange("p (a b) -> p a b", b=257)
        rwc, nrw = columns(RW_CONSTS)
        cursor[0] = WORK
        RW0 = cursor[0]
        rwt = view(nrw)
        Y_SWA = cursor[0]
        daw = view(C)
        aa = view(512, UN, L)
        kk = view(512, UN, L)
        y_swa = M[:, Y_SWA:Y_SWA + 2048].rearrange("p (a b) -> p a b", b=T)
        Bh = view(1024, UN, P)
        Kh = view(1024, UN, P)
        Abd = view(1024, UN, P)
        rhs = view(1024, UN, P)
        Wx = view(UN * 65, UN, 65)
        Winv = view(512, UN, L)
        cum = view(512, UN, L)
        WL = small[:, 64:72]
        ArkT = view(512, UN, L)
        ArbT = view(512, UN, L)
        AakT = view(1024, UN, P)
        Pm = view(1024, UN, P)
        Ubd = Pm
        RW1 = cursor[0]
        X0 = [0]

        def xview(words, *dims):
            a = X0[0]
            X0[0] += words
            assert X0[0] <= HS_AT
            return M[:, a:a + words].rearrange("p (a b) -> p a b", b=dims[1])
        Xi = xview(1024, UN, P)
        Yi = xview(1024, UN, P)
        gup = M[:, X0[0]:X0[0] + 2 * C].rearrange("p (a b) -> p a b", b=C)
        Am = xview(1024, UN, P)
        Araw = xview(1024, UN, P)
        Vbd = view(1024, UN, P)
        Sbd = view(1024, UN, P)
        Sc = view(512, UN, L)
        t1 = sig[:, :, :].rearrange("p a b -> p (a b)").rearrange("p (a b) -> p a b", b=L)
        tzc = small[:, 0:64]
        Vc, Uc, Rc, t2 = (q_all[:, 2 * n:2 * n + 2, :].rearrange("p a b -> p (a b)").rearrange("p (a b) -> p a b", b=L)
                      for n in range(4))
        cursor[0] = HS_AT
        KX = view(KT * T, KT, T)
        VX = view(2 * D, 2, D)
        QX = view(KT * T, KT, T)
        SX = view(1024, 4, T)
        PX = view(1024, 4, T)
        YT0 = FT - KT
        assert cursor[0] <= HS_AT + YT0 * 512
        assert Y_SWA + 2048 <= HS_AT + YT0 * 512

        acc = [ctx.enter_context(nc.psum_tensor(f"acc{p}", [P, 2, 2, T], F32)) for p in range(2)]
        mid = ctx.enter_context(nc.psum_tensor("mid", [P, 4, 512], F32))
        bank = [mid[:, n, :] for n in range(4)]
        b8 = [bk.rearrange("p (u t) -> p u t", t=L) for bk in bank]
        b4 = [bk.rearrange("p (u t) -> p u t", t=P) for bk in bank]
        b2 = [bk.rearrange("p (u t) -> p u t", t=T) for bk in bank]
        two = [mid[:, 2 * n:2 * n + 2, :].rearrange("p b (u t) -> p (b u) t", t=P) for n in range(2)]
        dram_x = nc.dram_tensor("spill_x", (D, T), F32, kind="Internal").ap().rearrange("(t p) n -> p t n", p=P)
        dram_k = nc.dram_tensor("spill_k", (D, T), F32, kind="Internal").ap().rearrange("(t p) n -> p t n", p=P)
        dram_v = nc.dram_tensor("spill_v", (T, D), F32, kind="Internal").ap().rearrange("(t p) n -> p t n", p=P)
        dram_q = nc.dram_tensor("spill_q", (C, T), F32, kind="Internal").ap().rearrange("(t p) n -> p t n", p=P)
        out_v = out.rearrange("(t p) n -> p t n", p=P)

        raw_landed = [S(f"raw_landed{s}") for s in range(RING)]
        high_ready = [S(f"high_ready{s}") for s in range(RING)]
        low_ready = [S(f"low_ready{s}") for s in range(RING)]
        parts_used = [S(f"parts_used{s}") for s in range(RING)]
        bank_free = [S(f"bank_free{p}") for p in range(2)]
        low_copied = S("low_copied")
        own = Own(S("dve_step"))
        kv_spilled = [S(f"kv_spilled{p}") for p in range(2)]
        block = ctx.enter_context(nc.Block())

        def mem_block(n, c):
            return n in (1, 2), (c * 2, c * 2 + 8, c * 2 + 9, c * 2 + 1, c * 2 + 2)[n]

        def pc(name, k=0):
            a = PCOL[name] + k
            return par[:, bass.ds(a, 1)] if not isinstance(a, int) else par[:, a:a + 1]

        def plain(eng):
            eng.sem_inc(S("passed"), 1)

        def per_unit(name):
            return par[:, PCOL[name]:PCOL[name] + UN].unsqueeze(2).to_broadcast([P, UN, L])

        def rc(name):
            a, b = rwc[name]
            return rwt[:, a:b]

        def sc_(name):
            a, b = swc[name]
            return swt[:, a:b]

        def is_first(i):
            return isinstance(i, int) and i == 0

        def load(sp, v, src, i=0, per=0):
            s, n = v % RING, W.uses(v, i, per)
            if W.count(v) > 1:
                sp.wait_ge(low_ready[s], n - 1)
                if not isinstance(i, int):
                    plain(sp)
            sp.dma_start(raw[:, s, :].rearrange("p (t n) -> p t n", n=src.shape[2]), src).then_inc(raw_landed[s], 16)

        def split_high(act, v, i=0, per=0):
            if W.missing(v):
                return
            s, n = v % RING, W.uses(v, i, per)
            act.wait_ge(raw_landed[s], 16 * n)
            if W.count(v) > 1:
                act.wait_ge(parts_used[s], n - 1)
            act.activation(parts[:, s, :, 0, :], raw[:, s, :].rearrange("p (t n) -> p t n", n=COLS), ACT.Copy)\
               .then_inc(high_ready[s], 1)

        def split_low(dve, v, i=0, per=0):
            if W.missing(v):
                return
            s = v % RING
            dve.wait_ge(high_ready[s], W.uses(v, i, per))
            dve.tensor_tensor(parts[:, s, :, 1, :], raw[:, s, :].rearrange("p (t n) -> p t n", n=COLS),
                              parts[:, s, :, 0, :].bitcast(F32), ALU.subtract).then_inc(low_ready[s], 1)

        def ahead(split, eng, v, chunks, i=0, per=0):
            for j in range(chunks):
                split(eng, v + j + LEAD, i, per)

        def chunk_products(pe, b, v, j, chunks, moving, ready=None, i=0, per=0, nb=0, by_token=False, first_tile=0,
                           order=None, tiles=range(KC)):
            p, s = B.pair[b], (v + j) % RING
            if tiles[0] == 0:
                if j == 0:
                    pe.wait_ge(bank_free[p], 1 + B.before(b, i, nb))
                if ready is not None:
                    ready(pe, j)
                pe.wait_ge(low_ready[s], W.uses(v + j, i, per))
            for t in tiles:
                k = j * KC + t
                at = first_tile + (order[j] if order else j) * KC + t
                first, last = k == 0, k == chunks * KC - 1
                for n in range(2):
                    if by_token:
                        pe.matmul(acc[p][:, n, :, :], moving[:, k, 0, n * P:(n + 1) * P], parts[:, s, t, :, :],
                                  start=first, stop=False, skip_group_check=True)
                        m = pe.matmul(acc[p][:, n, 1, :], moving[:, k, 1, n * P:(n + 1) * P], parts[:, s, t, 0, :],
                                      start=False, stop=last, skip_group_check=True)
                    else:
                        pe.matmul(acc[p][:, n, :, :], parts[:, s, t, 0, n * P:(n + 1) * P],
                                  moving[:, at, :, :], start=first, stop=False, skip_group_check=True)
                        m = pe.matmul(acc[p][:, n, 1, :], parts[:, s, t, 1, n * P:(n + 1) * P],
                                      moving[:, at, 0, :], start=False, stop=last, skip_group_check=True)
            if tiles[-1] == KC - 1:
                m.then_inc(parts_used[s], 1)

        def products(pe, b, v, chunks, moving, ready=None, i=0, per=0, nb=0, **kw):
            for j in range(chunks):
                chunk_products(pe, b, v, j, chunks, moving, ready, i, per, nb, **kw)

        def copy_low(act, b, v_last, i=0, per=0):
            p = B.pair[b]
            act.wait_ge(parts_used[v_last % RING], W.uses(v_last, i, per))
            act.activation(low[:, p, :, :], acc[p][:, :, 1, :], ACT.Copy).then_inc(low_copied, 1)

        def add_low(dve, b, i=0, nb=0):
            p = B.pair[b]
            dve.wait_ge(low_copied, b + 1 + i * nb)
            dve.tensor_tensor(total[:, :, :], acc[p][:, :, 0, :], low[:, p, :, :], ALU.add).then_inc(bank_free[p], 1)
            dve.wait_ge(bank_free[p], 2 + B.before(b, i, nb))

        rb = rstd[:, :].unsqueeze(1).to_broadcast([P, 2, T])

        def fill_act(act, norm, gain, blk, src, fill):
            n = 8 * norm + blk
            for e in range(2):
                k = 2 * blk + e
                m = act.activation(xs[:, bass.ds(k, 1), 0, :], src[:, bass.ds(k, 1), :], ACT.Copy, scale=pc(gain, k))
            m.then_inc(S("xs_high"), 1)
            act.wait_ge(S("sq_added"), 2 * n + 1)
            plain(act)
            act.activation(sq[:, :, :], src[:, bass.ds(2 * blk, 2), :], ACT.Square).then_inc(S("sq_ready"), 1)

        def fill_dve(dve, gain, blk, src, fill):
            dve.wait_ge(S("xs_high"), 8 * fill + blk + 1)
            for e in range(2):
                k = 2 * blk + e
                m = dve.scalar_tensor_tensor(xs[:, bass.ds(k, 1), 1, :], src[:, bass.ds(k, 1), :], pc(gain, k),
                                             xs[:, bass.ds(k, 1), 0, :].bitcast(F32), ALU.mult, ALU.subtract)
            m.then_inc(S("xs_ready"), 1)

        def filled(fill):
            def ready(pe, j):
                pe.wait_ge(S("xs_ready"), 8 * fill + 2 * (j + 1))
            return ready

        def sum_squares(pool, norm):
            if norm:
                pool.wait_ge(S("ms_ready"), norm)
            pool.memset(sqacc[:, :], 0.0).then_inc(S("sq_cleared"), 1)
            pool.wait_ge(S("sq_cleared"), norm + 1)
            with pool.Fori(0, 8) as blk:
                pool.wait_ge(S("sq_ready"), 8 * norm + blk + 1)
                pool.tensor_tensor(sqacc[:, :], sqacc[:, :], sq[:, 0, :], ALU.add).then_inc(S("sq_added"), 1)
                pool.wait_ge(S("sq_added"), 16 * norm + 2 * blk + 2)
                pool.tensor_tensor(sqacc[:, :], sqacc[:, :], sq[:, 1, :], ALU.add).then_inc(S("sq_added"), 1)
                pool.wait_ge(S("sq_added"), 16 * norm + 2 * blk + 3)

        def norm_pe(pe, norm):
            pe.wait_ge(S("sq_added"), 16 * norm + 17)
            to = bank[2 if norm == MEM else 0]
            if norm == MEM:
                for e in range(2):
                    pe.matmul(to[:, 256 + e:257 + e], sqacc[:, e * P:(e + 1) * P], ones[:, 0:1],
                              start=True, stop=True)
            pe.matmul(to[:, 0:T], ones[:, :], sqacc[:, :], start=True, stop=True).then_inc(S("ms_ready"), 1)

        def norm_act(act, norm):
            act.wait_ge(S("ms_eps"), norm + 1)
            if norm == MEM:
                act.activation(small[:, 146:148], small[:, 144:146], ACT.Sqrt)
            act.activation(ms[:, :], ms[:, :], ACT.Sqrt).then_inc(S("root_ready"), 1)

        def norm_dve(dve, norm):
            dve.wait_ge(S("ms_ready"), norm + 1)
            to = bank[2 if norm == MEM else 0]
            if norm == MEM:
                dve.tensor_scalar(small[:, 144:146], to[:, 256:258], RMS_EPS, None, ALU.add)
            dve.tensor_scalar(ms[:, :], to[:, 0:T], RMS_EPS, None, ALU.add).then_inc(S("ms_eps"), 1)
            dve.wait_ge(S("root_ready"), norm + 1)
            if norm == MEM:
                dve.reciprocal(rcol[:, :], small[:, 146:148])
            dve.reciprocal(rstd[:, :], ms[:, :]).then_inc(S("dve_step"), 1)
            own(dve)

        def b_step(b):
            base = B_UP1 if b < B_DOWN1 else B_UP2
            return (b - base) // 2 + 1

        def ffn_act(act, ffn, b0, v0, vend):
            def gate_part(b, v, i=0):
                n = STEPS * ffn + b_step(b) + i
                copy_low(act, b, v + 3, i, 8)
                act.wait_ge(S("gate_ready"), n)
                act.activation(sig[:, :, :], gate[:, :, :], ACT.Sigmoid).then_inc(S("sigmoid_ready"), 1)

            def up_part(b, v, step, i=0):
                n = STEPS * ffn + b_step(b) + i
                copy_low(act, b, v + 3, i, 8)
                act.wait_ge(S("hidden_ready"), n)
                plain(act)
                act.activation(hs[:, bass.ds(step * 2, 2), 0, :], total[:, :, :], ACT.Copy)\
                   .then_inc(S("hidden_high"), 1)
            gate_part(b0, v0)
            with act.Fori(0, STEPS - 1) as i:
                ahead(split_high, act, v0 + 4, 4, i, 8)
                up_part(b0 + 1, v0 + 4, i, i)
                ahead(split_high, act, v0 + 8, 4, i, 8)
                gate_part(b0 + 2, v0 + 8, i)
            ahead(split_high, act, vend - 4, 4)
            up_part(b0 + 2 * STEPS - 1, vend - 4, STEPS - 1)

        def ffn_dve(dve, ffn, b0, v0, vend):
            def gate_part(b, i=0):
                add_low(dve, b, i, 2)
                dve.tensor_tensor(gate[:, :, :], total[:, :, :], rb, ALU.mult).then_inc(S("gate_ready"), 1)

            def up_part(b, step, i=0):
                n = STEPS * ffn + b_step(b) + i
                add_low(dve, b, i, 2)
                dve.tensor_tensor(up[:, :, :], total[:, :, :], rb, ALU.mult).then_inc(S("dve_step"), 1)
                own(dve)
                dve.tensor_tensor(gate[:, :, :], gate[:, :, :], up[:, :, :], ALU.mult).then_inc(S("dve_step"), 1)
                own(dve)
                dve.wait_ge(S("sigmoid_ready"), n)
                dve.tensor_tensor(total[:, :, :], gate[:, :, :], sig[:, :, :], ALU.mult)\
                   .then_inc(S("hidden_ready"), 1)
                dve.wait_ge(S("hidden_high"), n)
                dve.tensor_tensor(hs[:, bass.ds(step * 2, 2), 1, :], total[:, :, :],
                                  hs[:, bass.ds(step * 2, 2), 0, :].bitcast(F32), ALU.subtract)\
                   .then_inc(S("hidden_split"), 1)
            gate_part(b0)
            with dve.Fori(0, STEPS - 1) as i:
                own.rounds(i, 2)
                ahead(split_low, dve, v0 + 4, 4, i, 8)
                up_part(b0 + 1, i, i)
                ahead(split_low, dve, v0 + 8, 4, i, 8)
                gate_part(b0 + 2, i)
            own.end(STEPS - 1)
            ahead(split_low, dve, vend - 4, 4)
            up_part(b0 + 2 * STEPS - 1, STEPS - 1)

        def ffn_pe(pe, ffn, b0, v0, vend, norm, fill):
            products(pe, b0, v0, 4, xs, filled(fill))
            norm_pe(pe, norm)
            with pe.Fori(0, STEPS - 1) as i:
                products(pe, b0 + 1, v0 + 4, 4, xs, None, i, 8, 2)
                products(pe, b0 + 2, v0 + 8, 4, xs, None, i, 8, 2)
            products(pe, b0 + 2 * STEPS - 1, vend - 4, 4, xs)

        def hidden(ffn):
            def ready(pe, j):
                pe.wait_ge(S("hidden_split"), STEPS * ffn + 2 * (j + 1))
            return ready

        def resid_act(act, res, b, v_last, blk, norm, gain, fill, i=0, per=0):
            copy_low(act, b, v_last, i, per)
            act.wait_ge(S("x_updated"), 8 * res + blk + 1)
            plain(act)
            if fill is None:
                act.wait_ge(S("sq_added"), 2 * (8 * norm + blk) + 1)
                plain(act)
                act.activation(sq[:, :, :], x[:, bass.ds(2 * blk, 2), :], ACT.Square).then_inc(S("sq_ready"), 1)
            else:
                fill_act(act, norm, gain, blk, x, fill)

        def resid_dve(dve, res, b, blk, gain, fill, half, bias=None, i=0, nb=0):
            add_low(dve, b, i, nb)
            xx = x[:, bass.ds(2 * blk, 2), :]
            if bias:
                for e in range(2):
                    xe = x[:, bass.ds(2 * blk + e, 1), :]
                    m = dve.scalar_tensor_tensor(xe, total[:, e:e + 1, :], pc(bias, 2 * blk + e), xe, ALU.add, ALU.add)
            else:
                m = dve.scalar_tensor_tensor(xx, total[:, :, :], half, xx, ALU.mult, ALU.add)
            m.then_inc(S("x_updated"), 1)
            dve.wait_ge(S("x_updated"), 8 * res + blk + 1)
            if fill is not None:
                fill_dve(dve, gain, blk, x, fill)

        @block.sync
        def _(sp):
            def cols(name):
                return A[name].rearrange("(t p) n -> p t n", p=P)

            def piece(w, j, c0):
                return w[:, KC * j:KC * (j + 1), c0:c0 + COLS] if isinstance(c0, int) else \
                    w[:, KC * j:KC * (j + 1), bass.ds(c0, COLS)]

            def ffn(v_up, v_down, pre):
                wg, wu, wd = cols(pre + "_gate"), cols(pre + "_up"), cols(pre + "_down")
                for j in range(8):
                    load(sp, v_up + j, piece((wg, wu)[j // 4], j % 4, 0))
                with sp.Fori(0, STEPS - 1) as i:
                    for j in range(8):
                        load(sp, v_up + 8 + j, piece((wg, wu)[j // 4], j % 4, i * COLS + COLS), i, 8)
                with sp.Fori(0, 8) as i:
                    for j in range(11):
                        load(sp, v_down + j, piece(wd, j, i * COLS), i, 12)

            def square(v, name, c0=0, order=(0, 1, 2, 3)):
                w = cols(name)
                with sp.Fori(0, 8) as i:
                    for j in range(4):
                        load(sp, v + j, piece(w, order[j], i * COLS + c0), i, 4)
            ffn(V_UP1, V_DOWN1, "f1")
            win = cols("w_in")
            for b in range(4):
                for j in range(4):
                    load(sp, V_Q + 4 * b + j, piece(win, j, Q_COL + COLS * b))
                if b == 0:
                    sp.wait_ge(S("x_updated"), 8)
                    sp.dma_start(dram_x, x[:, :, :]).then_inc(S("x_spilled"), 16)
            for j in range(4):
                load(sp, V_KV + j, piece(win, j, KV_COL))
            for j in range(4):
                load(sp, V_LORA + j, piece(win, j, LORA_COL))
            for j in range(2):
                load(sp, V_TAIL + j, win[:, 8 * j:8 * j + 8, TAIL_COL:TAIL_COL + P])
            with sp.Fori(0, 12) as i:
                for j in range(4):
                    load(sp, V_RKV + j, piece(win, j, i * COLS), i, 4)
            wkv = cols("w_xkv")
            for j in range(4):
                load(sp, V_MEM + j, piece(wkv, j, 0))
            with sp.Fori(0, TC - 1) as c:
                for m in range(1, 5):
                    for j in range(4):
                        load(sp, V_MEM + 4 * m + j, piece(wkv, j, mem_block(m, c)[1] * COLS), c, 16)
            for m in range(1, 4):
                for j in range(4):
                    load(sp, V_MEM + 4 * m + j, piece(wkv, j, mem_block(m, TC - 1)[1] * COLS), TC - 1, 16)
            square(V_OUT, "w_out", 0, (2, 3, 0, 1))
            square(V_XQ, "w_xq")
            square(V_XO, "w_xo")
            ffn(V_UP2, V_DOWN2, "f2")
            for g in range(4):
                sp.wait_ge(S("out_ready"), g + 1)
                sp.dma_start(out_v[:, 4 * g:4 * g + 4, :], x[:, 4 * g:4 * g + 4, :]).then_inc(S("stored"), 16)
            sp.wait_ge(S("stored"), 64)

        @block.gpsimd
        def _(pool):
            pool.memset(small[:, 140:141], 0.0).then_inc(bank_free[0], 1)
            pool.memset(small[:, 141:142], 0.0).then_inc(bank_free[1], 1)
            pool.memset(small[:, 142:143], 0.0).then_inc(S("sq_added"), 1)
            pool.memset(ones[:, :], 1.0 / D).then_inc(S("ones_ready"), 1)
            sum_squares(pool, X1)
            sum_squares(pool, MIX)
            pool.dma_start(swt, A["swa_consts"]).then_inc(S("swa_tables"), 16)
            pool.memset(vpad[:, :, :], 0.0).then_inc(S("vpad_cleared"), 1)
            pool.memset(shifted[:, :, 0:1], 0.0).then_inc(S("shift_cleared"), 1)
            pool.wait_ge(S("x_spilled"), 16)
            pool.wait_ge(S("xs_ready"), 8 * FILL_MEM)
            pool.dma_start(x[:, :, :], A["mem_t"].rearrange("(t p) n -> p t n", p=P)).then_inc(S("mem_landed"), 16)
            pool.wait_ge(S("swa_done"), 4)
            pool.dma_start(dram_q, q_all).then_inc(S("y_spilled"), 16)
            pool.dma_start(rwt, A["rw_consts"]).then_inc(S("rw_tables"), 16)
            pool.dma_start(daw[0:64, :], A["rw_decay_up"]).then_inc(S("rw_tables"), 16)
            pool.dma_start(daw[64:128, :], A["rw_aaa_up"]).then_inc(S("rw_tables"), 16)
            for m in (Bh, Kh, Abd, AakT, Pm):
                pool.memset(m, 0.0).then_inc(S("rw_cleared"), 1)
            sum_squares(pool, MEM)
            for p in range(2):
                pool.memset(small[:, 148 + p:149 + p], 0.0).then_inc(kv_spilled[p], 16)
            pool.wait_ge(S("rw_tables"), 48)

            def masks(c):
                need(pool, c, "A_ready")
                pool.tensor_tensor(Xi, Araw, rc("pair").unsqueeze(1).to_broadcast([P, UN, P]), ALU.mult)\
                    .then_inc(S("X_pairs"), 1)
                need(pool, c, "X_pairs")
                pool.tensor_tensor(Xi, Xi, ident[:, :].unsqueeze(1).to_broadcast([P, UN, P]), ALU.add)
                for n in range(5):
                    if n:
                        pool.wait_ge(S("P_done"), c * 5 + n)
                    a = rwc["level"][0] + n * P
                    pool.tensor_tensor(Am, Araw, rwt[:, a:a + P].unsqueeze(1).to_broadcast([P, UN, P]), ALU.mult)\
                        .then_inc(S("Am"), 1)
            with pool.Fori(0, TC - 1) as c:
                masks(c)
            masks(TC - 1)
            pool.dma_start(y_swa, dram_q).then_inc(S("y_back"), 16)
            pool.wait_ge(S("P_done"), 5 * TC)
            pool.memset(gup[0:96, 1, :], 0.0).then_inc(S("gup_cleared"), 1)
            pool.dma_start(gup[:, 0, :], A["rw_gate_up"][0:128, :]).then_inc(S("gup_landed"), 16)
            pool.dma_start(gup[96:128, 1, :], A["rw_gate_up"][128:160, :]).then_inc(S("gup_landed"), 16)
            need(pool, TC - 1, "U_done")
            pool.dma_start(x[:, 0:8, :], dram_x[:, 0:8, :]).then_inc(S("x_back"), 16)
            need(pool, 3, "gate_done")
            pool.dma_start(x[:, 8:16, :], dram_x[:, 8:16, :]).then_inc(S("x_back"), 16)
            need(pool, 5, "y_split")
            for p in range(2):
                pool.wait_ge(kv_spilled[p], 16 * 9)
            pool.dma_start(KX, dram_k).then_inc(S("kv_back"), 16)
            pool.dma_start(VX, dram_v).then_inc(S("kv_back"), 16)
            sum_squares(pool, XA)
            sum_squares(pool, F2)
            sum_squares(pool, FINAL)


        def rkv_chunk(eng, kind, i, j):
            v, b = V_RKV, B_RKV + j // 4
            if kind == "pe":
                chunk_products(eng, b, v + j - j % 4, j % 4, 4, xs, None, i, 12, 3)
            elif kind == "act":
                split_high(eng, v + j + LEAD, i, 12)
                if j % 4 == 3:
                    copy_low(eng, b, v + j, i, 12)
            else:
                split_low(eng, v + j + LEAD, i, 12)
                if j % 4 == 3:
                    add_low(eng, b, i, 3)
                    n = j // 4
                    shift_in(eng)
                    for e in range(2):
                        k = i * 6 + 2 * n + e
                        m = eng.scalar_tensor_tensor(rkv[:, bass.ds(k, 1), :], up[:, e:e + 1, :], pc("mu", k),
                                                     shifted[:, e:e + 1, 1:257], ALU.mult, ALU.add)
                    m.then_inc(S("rkv_ready"), 1)

        def shift_in(dve):
            dve.tensor_tensor(shifted[:, :, 1:257], total[:, :, :], rb, ALU.mult).then_inc(S("dve_step"), 1)
            own(dve)
            dve.tensor_tensor(up[:, :, :], shifted[:, :, 0:256], shifted[:, :, 1:257], ALU.subtract)\
               .then_inc(S("dve_step"), 1)
            own(dve)

        def mem_chunk(eng, kind, c, m, j, tiles=range(KC)):
            v, b, by_token = V_MEM + 4 * m, B_MEM + m, mem_block(m, c)[0]
            odd_one = m % 2
            if kind == "pe":
                chunk_products(eng, b, v, j, 4, xs, filled(FILL_MEM) if m == 0 else None, c, 16, 4,
                               by_token=by_token, tiles=tiles)
            elif kind == "act":
                split_high(eng, v + j + LEAD, c, 16)
                if j == 3:
                    copy_low(eng, b, v + 3, c, 16)
            else:
                split_low(eng, v + j + LEAD, c, 16)
                if j == 3:
                    add_low(eng, b, c, 4)
                    eng.wait_ge(kv_spilled[odd_one], c * 32 + 16 * (m // 2 + 1))
                    by = rcol[:, :].unsqueeze(2).to_broadcast([P, 2, T]) if by_token else rb
                    eng.tensor_tensor((gate, up)[odd_one][:, :, :], total[:, :, :], by, ALU.mult)\
                       .then_inc(S("kv_out"), 1)

        def mem_store(act, c, m):
            by_token, col = mem_block(m, c)
            act.wait_ge(S("kv_out"), c * 4 + m + 1)
            if by_token:
                dst = dram_v[:, :, bass.ds((col - 8) * COLS, COLS)]
            else:
                dst = dram_k[:, bass.ds(col * 2, 2), :]
            act.dma_start(dst, (gate, up)[m % 2][:, :, :]).then_inc(kv_spilled[m % 2], 16)

        XSCALE = float(D // 4) ** -0.5
        xmax, xneg, xsum, xrec = (small[:, 112 + 4 * n:116 + 4 * n] for n in range(4))

        mx, negm, es, sums, rden = (small[:, 72 + 8 * n:80 + 8 * n] for n in range(5))

        def halves(eng, dst, src, name, mask=None, scale=None):
            for h in range(2):
                rows, co = slice(h * HD, h * HD + HD), slice(h * L, h * L + L)
                if mask is not None:
                    m = eng.tensor_tensor(dst[rows, :, co], src[rows, :, :],
                                          mask[rows, :].unsqueeze(1).to_broadcast([HD, UN, L]), ALU.mult)
                elif scale is not None:
                    m = eng.tensor_tensor(dst[rows, :, co], src[rows, :, :], scale[rows, :, :], ALU.mult)
                elif eng is nc.scalar:
                    m = eng.activation(dst[rows, :, co], src[rows, :, :], ACT.Copy)
                else:
                    m = eng.tensor_copy(dst[rows, :, co], src[rows, :, :])
            if name:
                m.then_inc(S(name), 1)

        def bcast(table):
            return table.unsqueeze(1).to_broadcast([P, UN, L])

        def odd(m, b, e):
            return m.rearrange("p (n two b) -> p n two b", two=2, b=b)[:, :, e, :]

        @block.scalar
        def _(act):
            act.dma_start(par[:, :], A["params"]).then_inc(S("par_landed"), 16)
            xin = A["x_t"].rearrange("(t p) n -> p t n", p=P)
            for g in range(4):
                act.dma_start(x[:, 4 * g:4 * g + 4, :], xin[:, 4 * g:4 * g + 4, :]).then_inc(S(f"x_landed{g}"), 16)
            act.dma_start(ident[:, :], A["ident"]).then_inc(S("ident_landed"), 16)
            act.wait_ge(S("par_landed"), 16)
            for b in range(8):
                act.wait_ge(S(f"x_landed{b // 2}"), 16)
                fill_act(act, X1, "f1_norm", b, x, FILL_X)
                if b % 2:
                    split_high(act, V_UP1 + b // 2)
            ahead(split_high, act, V_UP1 + 1, 3)
            norm_act(act, X1)
            ffn_act(act, 0, B_UP1, V_UP1, V_DOWN1)
            with act.Fori(0, 4) as i:
                for u in range(2):
                    ahead(split_high, act, V_DOWN1 + 12 * u, 12, i, 24)
                    resid_act(act, 0, B_DOWN1 + u, V_DOWN1 + 12 * u + 10, 2 * i + u, MIX, "mix_norm", FILL_MIX, i, 24)
            ahead(split_high, act, V_Q, 4)
            norm_act(act, MIX)
            copy_low(act, B_Q, V_Q + 3)
            for b in range(1, 4):
                ahead(split_high, act, V_Q + 4 * b, 4)
                copy_low(act, B_Q + b, V_Q + 4 * b + 3)
            ahead(split_high, act, V_KV, 4)
            copy_low(act, B_KV, V_KV + 3)
            ahead(split_high, act, V_LORA, 4)
            copy_low(act, B_LORA, V_LORA + 3)
            need(act, 0, "v_turned", "vpad_cleared")
            for g in range(2):
                vp = vpad[:, g, :].rearrange("p (b e n) -> p b e n", b=2, e=2)
                for e in range(2):
                    m = act.activation(vp[:, :, e, e * HD:(e + 1) * HD],
                                       bank[1].rearrange("p (b n) -> p b n", n=P)[:, 0:2, g * HD:(g + 1) * HD],
                                       ACT.Copy)
            m.then_inc(S("vpad_ready"), 1)
            need(act, 0, "k_selected")
            act.activation(kpad, mid[:, 2:4, :].rearrange("p b (u t) -> p (b u) t", t=T), ACT.Copy)\
               .then_inc(S("kpad_ready"), 1)
            ahead(split_high, act, V_TAIL, 4)
            copy_low(act, B_TAIL, V_TAIL + 1)
            need(act, 1, "lora_ready")
            act.activation(lora[0:64, 0, :], lora[0:64, 0, :], ACT.Tanh)
            act.activation(lora[:, 1:3, :], lora[:, 1:3, :], ACT.Sigmoid).then_inc(S("lora_act"), 1)
            with act.Fori(0, 4) as i:
                for j in range(4):
                    rkv_chunk(act, "act", i, j)
                need(act, i, "sinks_less_max")
                act.activation(es, es, ACT.Exp).then_inc(S("sink_exp"), 1)
                for h in range(4):
                    act.activation(sc[:, h, 0:128], sc[:, h, 0:128], ACT.Exp, bias=negm[:, h:h + 1],
                                   accum_out=sums[:, h:h + 1])
                    m = act.activation(sc[:, h, 128:384], sc[:, h, 128:384], ACT.Exp, bias=negm[:, 4 + h:5 + h],
                                       accum_out=sums[:, 4 + h:5 + h])
                m.then_inc(S("swa_exp"), 1)
                for j in range(4, 8):
                    rkv_chunk(act, "act", i, j)
                need(act, i, "probs_turned")
                act.activation(pt, mid[:, 0:3, :].rearrange("p b (u t) -> p (b u) t", t=P), ACT.Copy)\
                   .then_inc(S("pt_ready"), 1)
                for j in range(8, 12):
                    rkv_chunk(act, "act", i, j)

            def prepare(n, step):
                if step == 0:
                    ts = bass.ds(n * L, L)
                    if not isinstance(n, int):
                        plain(act)
                    act.activation(tzc, lora[:, 0, ts], ACT.Copy).then_inc(S("tz_copied"), 1)
                    need(act, n, "kk_raw")
                    act.activation(t2, kk, ACT.Square).then_inc(S("kk_sq"), 1)
                if step == 1:
                    need(act, n, "z_decay")
                    act.activation(t1, t1, ACT.Sigmoid).then_inc(S("decay_sig"), 1)
                    need(act, n, "z_a")
                    act.activation(aa, aa, ACT.Sigmoid).then_inc(S("a_ready"), 1)
                    need(act, n, "kk_sum")
                    act.activation(t2, b8[0], ACT.Sqrt).then_inc(S("kk_norm"), 1)
                if step == 2:
                    need(act, n, "cum_ready")
                    act.activation(Wx[:, :, 1:65], cum, ACT.Exp, scale=-DECAY)
                    act.activation(Winv, cum, ACT.Exp, scale=DECAY).then_inc(S("W_ready"), 1)

            def turn(n, *parts):
                for part in parts:
                    dst, src = ((Araw, two[0]), (Bh, two[1]), (Kh, two[0]), (Vc, b8[2]))[part]
                    need(act, n, ("A_prod", "B_turned", "K_turned", "V_turned")[part])
                    act.activation(dst, src, ACT.Copy).then_inc(S(("A_ready", "BT_ready", "KT_ready", "Vc_ready")[part]), 1)

            def scaled_blocks(n):
                need(act, n, "a_scaled")
                ts = bass.ds(n * L, L)
                halves(act, Abd, rhs[:, :, 0:64], None)
                halves(act, Pm, rkv[:, 16:24, ts], "Abd_ready")

            def solve(c, more):
                for n in range(5):
                    act.wait_ge(S("P_done"), c * 5 + n + 1)
                    act.activation(Pm, two[0], ACT.Copy).then_inc(S("P_ready"), 1)
                    if more and n < 3:
                        prepare(c + 1, n)
                    mem(c, n)

            def mem(c, *js):
                for j in js:
                    if isinstance(c, int) and j >= 12:
                        continue
                    mem_chunk(act, "act", c, 1 + j // 4, j % 4)
                    if j % 4 == 1:
                        mem_store(act, c, j // 4)
            act.wait_ge(S("rw_tables"), 48)
            act.wait_ge(S("rw_cleared"), 8)
            act.wait_ge(S("y_spilled"), 16)
            act.wait_ge(S("mem_landed"), 16)
            for step in range(4):
                fill_act(act, MEM, "mem_norm", 2 * step, x, FILL_MEM)
                fill_act(act, MEM, "mem_norm", 2 * step + 1, x, FILL_MEM)
                if step < 3:
                    prepare(0, step)
                    mem_chunk(act, "act", 0, 0, step)
            norm_act(act, MEM)
            scaled_blocks(0)
            mem_chunk(act, "act", 0, 0, 3)
            turn(0, 0, 1, 2, 3)

            def round_(c, more):
                solve(c, more)
                need(act, c, "R_done")
                act.activation(Rc, b8[0], ACT.Copy).then_inc(S("R_ready"), 1)
                mem(c, 5)
                need(act, c, "U_done")
                act.activation(Uc, b8[1], ACT.Copy).then_inc(S("U_ready"), 1)
                mem(c, 6)
                need(act, c, "y_done")
                act.activation(cum, b8[2], ACT.Copy).then_inc(S("y_copied"), 1)
                mem(c, 7)
                need(act, c, "S_new")
                halves(act, Sbd, Sc, None)
                need(act, c, "y_centred")
                act.activation(t2, t1, ACT.Square).then_inc(S("y_sq"), 1)
                mem(c, 8)
                need(act, c, "y_var")
                act.activation(t2, t2, ACT.Sqrt).then_inc(S("y_root"), 1)
                if more:
                    scaled_blocks(c + 1)
                    mem(c, 9, 10)
                    for part in range(4):
                        turn(c + 1, part)
                        mem(c, 11 + part)
                    mem(c, 15)
                else:
                    mem(c, 9, 10, 11)
            with act.Fori(0, TC - 1) as c:
                round_(c, True)
            round_(TC - 1, False)
            mem_store(act, TC - 1, 3)
            act.wait_ge(S("y_back"), 16)
            for g in range(2):
                act.activation(hs[:, YT0 + 8 + 4 * g:YT0 + 12 + 4 * g, 0, :], y_swa[:, 4 * g:4 * g + 4, :], ACT.Copy)\
                   .then_inc(S("y_high"), 1)
            for g in range(4):
                act.wait_ge(S("y_gated"), g + 1)
                act.activation(hs[:, YT0 + 2 * g:YT0 + 2 * g + 2, 0, :], rkv[:, 2 * g:2 * g + 2, :], ACT.Copy)\
                   .then_inc(S("y_high"), 1)
            with act.Fori(0, 4) as i:
                for u in range(2):
                    ahead(split_high, act, V_OUT + 4 * u, 4, i, 8)
                    resid_act(act, 1, B_OUT + u, V_OUT + 4 * u + 3, 2 * i + u, XA, "xa_norm", FILL_XA, i, 8)
            ahead(split_high, act, V_XQ, 4)
            norm_act(act, XA)
            copy_low(act, B_XQ, V_XQ + 3)
            with act.Fori(0, 3) as i:
                for u in range(1, 3):
                    ahead(split_high, act, V_XQ + 4 * u, 4, i, 8)
                    copy_low(act, B_XQ + u, V_XQ + 4 * u + 3, i, 8)
            ahead(split_high, act, V_XQ + 28, 4)
            copy_low(act, B_XQ + 7, V_XQ + 31)

            def x_exp(h):
                act.wait_ge(S("x_negmax"), h + 1)
                for q in range(2):
                    k = 2 * (h % 2) + q
                    m = act.activation(SX[:, k, :], b2[h % 2][:, q, :], ACT.Exp, scale=XSCALE,
                                       bias=xneg[:, k:k + 1], accum_out=xsum[:, k:k + 1])
                m.then_inc(S("x_exp"), 1)

            def x_out(h):
                act.wait_ge(S("x_turned"), h + 1)
                act.activation(PX[:, 2 * (h % 2):2 * (h % 2) + 2, :], b2[2], ACT.Copy).then_inc(S("x_probs"), 1)
                for g in range(2):
                    act.wait_ge(S("o_done"), 2 * h + g + 1)
                    a = YT0 + 4 * h + 2 * g
                    act.activation(hs[:, a:a + 2, 0, :], b2[3 - g], ACT.Copy).then_inc(S("o_high"), 1)
            x_exp(0)
            for h in range(4):
                if h < 3:
                    x_exp(h + 1)
                x_out(h)
            with act.Fori(0, 4) as i:
                for u in range(2):
                    ahead(split_high, act, V_XO + 4 * u, 4, i, 8)
                    resid_act(act, 2, B_XO + u, V_XO + 4 * u + 3, 2 * i + u, F2, "f2_norm", FILL_F2, i, 8)
            ahead(split_high, act, V_UP2, 4)
            norm_act(act, F2)
            ffn_act(act, 1, B_UP2, V_UP2, V_DOWN2)
            with act.Fori(0, 3) as i:
                for u in range(2):
                    ahead(split_high, act, V_DOWN2 + 12 * u, 12, i, 24)
                    resid_act(act, 3, B_DOWN2 + u, V_DOWN2 + 12 * u + 10, 2 * i + u, FINAL, None, None, i, 24)
            for u in range(6, 8):
                ahead(split_high, act, V_DOWN2 + 12 * u, 12)
                resid_act(act, 3, B_DOWN2 + u, V_DOWN2 + 12 * u + 10, u, FINAL, None, None)
            norm_act(act, FINAL)

        @block.vector
        def _(dve):
            dve.wait_ge(S("par_landed"), 16)
            for b in range(8):
                dve.wait_ge(S(f"x_landed{b // 2}"), 16)
                fill_dve(dve, "f1_norm", b, x, FILL_X)
                if b % 2:
                    split_low(dve, V_UP1 + b // 2)
            ahead(split_low, dve, V_UP1 + 1, 3)
            norm_dve(dve, X1)
            ffn_dve(dve, 0, B_UP1, V_UP1, V_DOWN1)
            with dve.Fori(0, 4) as i:
                for u in range(2):
                    ahead(split_low, dve, V_DOWN1 + 12 * u, 12, i, 24)
                    resid_dve(dve, 0, B_DOWN1 + u, 2 * i + u, "mix_norm", FILL_MIX, 0.5, None, i, 2)
            ahead(split_low, dve, V_Q, 4)
            norm_dve(dve, MIX)

            def scaled(b, dst, bias, k, name):
                add_low(dve, b)
                dve.tensor_tensor(dst, total[:, :, :], rb, ALU.mult).then_inc(S("dve_step"), 1)
                own(dve)
                a = PCOL[bias] + k
                dve.tensor_tensor(dst, dst, par[:, a:a + 2].unsqueeze(2).to_broadcast([P, 2, T]), ALU.add)\
                   .then_inc(S(name), 1)
            scaled(B_Q, q_all[:, 0:2, :], "b_q", 0, "q_in")
            for b in range(1, 4):
                ahead(split_low, dve, V_Q + 4 * b, 4)
                scaled(B_Q + b, q_all[:, 2 * b:2 * b + 2, :], "b_q", 2 * b, "q_in")
            ahead(split_low, dve, V_KV, 4)
            scaled(B_KV, k_v, "b_kv", 0, "kv_in")
            ahead(split_low, dve, V_LORA, 4)
            dve.wait_ge(S("swa_tables"), 16)
            need(dve, 0, "k_swapped", "kv_in")
            dve.tensor_tensor(ktmp, bank[0][:, 0:T], sc_("sin"), ALU.mult)
            dve.tensor_tensor(krot, k_v[:, 0, :], sc_("cos"), ALU.mult).then_inc(S("dve_step"), 1)
            own(dve)
            dve.tensor_tensor(krot, krot, ktmp, ALU.add).then_inc(S("k_rotated"), 1)

            def lora_part(b, dst, ntiles, mu):
                add_low(dve, b)
                need(dve, 0, "shift_cleared")
                shift_in(dve)
                for e in range(ntiles):
                    m = dve.scalar_tensor_tensor(dst[:, e, :], up[:, e, :], pc(mu, e), shifted[:, e, 1:257],
                                                 ALU.mult, ALU.add)
                m.then_inc(S("lora_ready"), 1)
            lora_part(B_LORA, lora[:, 0:2, :], 2, "mu_lora")
            ahead(split_low, dve, V_TAIL, 4)
            lora_part(B_TAIL, lora[:, 2:3, :], 1, "mu_tail")
            need(dve, 0, "vpad_ready")
            with dve.Fori(0, 4) as i:
                own.rounds(i, 13)
                qi = q_all[:, bass.ds(i * 2, 2), :]

                def rkvs(*js):
                    for j in js:
                        rkv_chunk(dve, "dve", i, j)
                cosb = sc_("cos").unsqueeze(1).to_broadcast([P, 2, T])
                sinb = sc_("sin").unsqueeze(1).to_broadcast([P, 2, T])
                need(dve, i, "q_swapped")
                dve.tensor_tensor(qtmp, b2[0], sinb, ALU.mult)
                dve.tensor_tensor(qg, qi, cosb, ALU.mult).then_inc(S("dve_step"), 1)
                own(dve)
                dve.tensor_tensor(qg, qg, qtmp, ALU.add).then_inc(S("q_rotated"), 1)
                dve.tensor_scalar(vg, vpad[:, bass.ds(i // 2, 1), :].rearrange("p a (b n) -> p (a b) n", n=P), 1.0, None,
                                  ALU.mult)\
                   .then_inc(S("vg_ready"), 1)
                rkvs(0, 1)
                for h in range(4):
                    dve.wait_ge(S("swa_scores"), i * 4 + h + 1)
                    m = dve.scalar_tensor_tensor(sc[:, h, :], bank[h][:, 0:384], HD ** -0.5, sc_("band"),
                                                 ALU.mult, ALU.add)
                m.then_inc(S("dve_step"), 1)
                own(dve)
                dve.reduce_max(mx[:, 0:4], sc[:, :, 0:128], AX_X)
                dve.reduce_max(mx[:, 4:8], sc[:, :, 128:384], AX_X).then_inc(S("dve_step"), 1)
                own(dve)
                sink = par[:, bass.ds(i * 4 + PCOL["sinks"], 4)].unsqueeze(1).to_broadcast([P, 2, 4])

                def pair4(s):
                    return s.rearrange("p (a b) -> p a b", b=4)
                dve.tensor_tensor(pair4(mx), pair4(mx), sink, ALU.max).then_inc(S("dve_step"), 1)
                own(dve)
                dve.tensor_scalar(negm, mx, -1.0, None, ALU.mult).then_inc(S("dve_step"), 1)
                own(dve)
                dve.tensor_tensor(pair4(es), sink, pair4(negm), ALU.add).then_inc(S("sinks_less_max"), 1)
                rkvs(2, 3)
                need(dve, i, "sink_exp", "swa_exp")
                dve.tensor_tensor(sums, sums, es, ALU.add).then_inc(S("dve_step"), 1)
                own(dve)
                dve.reciprocal(rden, sums).then_inc(S("dve_step"), 1)
                own(dve)
                dve.tensor_tensor(sc[:, :, 0:128], sc[:, :, 0:128], rden[:, 0:4].unsqueeze(2).to_broadcast([P, 4, 128]),
                                  ALU.mult)
                dve.tensor_tensor(sc[:, :, 128:384], sc[:, :, 128:384],
                                  rden[:, 4:8].unsqueeze(2).to_broadcast([P, 4, 256]), ALU.mult)\
                   .then_inc(S("swa_probs"), 1)
                rkvs(4, 5, 6, 7, 8)
                need(dve, i, "swa_out")
                dve.tensor_scalar(qi, b2[3], 1.0, None, ALU.mult).then_inc(S("swa_done"), 1)
                rkvs(9, 10, 11)
            own.end(4)
            dve.memset(Vbd, 0.0)
            dve.memset(Sbd, 0.0).then_inc(S("rw_cleared"), 1)
            dve.memset(Sc, 0.0).then_inc(S("rw_cleared"), 1)
            dve.memset(Wx[:, :, 0:1], 1.0).then_inc(S("rw_cleared"), 1)
            dve.wait_ge(S("rw_cleared"), 8)
            dve.wait_ge(S("rw_tables"), 48)
            def mem(c, *js):
                for j in js:
                    if not (isinstance(c, int) and j >= 12):
                        mem_chunk(dve, "dve", c, 1 + j // 4, j % 4)

            def prepare(n, step):
                ts = bass.ds(n * L, L)
                kv_ = rkv[:, 8:16, ts]
                if step == 0:
                    dve.tensor_tensor(kk, kv_, per_unit("k_k"), ALU.mult).then_inc(S("kk_raw"), 1)
                    need(dve, n, "lora_z")
                    dve.tensor_tensor(t1, b8[0], per_unit("w0"), ALU.add).then_inc(S("z_decay"), 1)
                    dve.tensor_tensor(aa, b8[1], per_unit("a0"), ALU.add).then_inc(S("z_a"), 1)
                if step == 1:
                    need(dve, n, "decay_sig")
                    for u in range(UN):
                        m = dve.tensor_tensor_scan(cum[:, u, :], t1[:, u, :], t1[:, u, :], 0.0, ALU.add, ALU.max)
                    m.then_inc(S("cum_ready"), 1)
                if step == 2:
                    need(dve, n, "kk_norm")
                    dve.tensor_scalar(t2, t2, 1e-12, None, ALU.max).then_inc(S("dve_step"), 1)
                    own(dve)
                    dve.reciprocal(t2, t2).then_inc(S("dve_step"), 1)
                    own(dve)
                if step == 3:
                    dve.tensor_tensor(kk, kk, t2, ALU.mult)
                    need(dve, n, "a_ready")
                    dve.scalar_tensor_tensor(t1, aa, -1.0, per_unit("k_a"), ALU.add, ALU.mult)\
                       .then_inc(S("dve_step"), 1)
                    own(dve)
                    dve.scalar_tensor_tensor(kv_, t1, 1.0, kv_, ALU.add, ALU.mult).then_inc(S("dve_step"), 1)
                    own(dve)
                if step == 4:
                    dve.tensor_tensor(aa, kk, aa, ALU.mult).then_inc(S("dve_step"), 1)
                    own(dve)

            def scale_a(n):
                ts = bass.ds(n * L, L)
                need(dve, n, "W_ready")
                dve.scalar_tensor_tensor(rhs[:, :, 0:64], kk, -1.0, Wx[:, :, 0:64], ALU.mult, ALU.mult)\
                   .then_inc(S("a_scaled"), 1)
                dve.tensor_tensor(rhs[:, :, 64:128], rkv[:, 0:8, ts], Wx[:, :, 1:65], ALU.mult)
                dve.tensor_copy(WL, Wx[:, :, 64])

            def scale_b(n):
                ts = bass.ds(n * L, L)
                halves(dve, Bh, aa, "B_scaled", scale=Winv)
                halves(dve, Kh, rkv[:, 8:16, ts], "K_scaled", scale=Winv)

            def take_b(n):
                need(dve, n, "B_prod")
                halves(dve, Yi, two[0][:, :, 0:64], "dve_step", mask=rc("pair_t"))
                dve.tensor_tensor(ArbT, two[0][:, :, 64:128], bcast(rc("upto_t")), ALU.mult)\
                   .then_inc(S("Arb_ready"), 1)
                own(dve)
                dve.tensor_tensor(Yi, Yi, ident[:, :].unsqueeze(1).to_broadcast([P, UN, P]), ALU.add)\
                   .then_inc(S("Y_init"), 1)

            def take_k(n):
                need(dve, n, "K_prod")
                halves(dve, AakT, two[1][:, :, 0:64], None, mask=rc("before_t"))
                dve.tensor_tensor(ArkT, two[1][:, :, 64:128], bcast(rc("upto_t")), ALU.mult)\
                   .then_inc(S("Ark_ready"), 1)

            def take_v(n):
                need(dve, n, "Vc_ready")
                halves(dve, Vbd, Vc, None)

            def solve(c, more):
                for n, b in enumerate(LEVELS):
                    dve.wait_ge(S("Y_more"), c * 5 + n + 1)
                    yo = Yi.rearrange("p u (n two b) -> p (u n) two b", two=2, b=b)[:, :, 1, :]
                    dve.tensor_tensor(yo, yo, bank[2].rearrange("p (n b) -> p n b", b=b), ALU.add)\
                       .then_inc(S("Y_level"), 1)
                    if n < 4:
                        dve.wait_ge(S("X_more"), c * 4 + n + 1)
                        xo = Xi.rearrange("p u (n two b) -> p (u n) two b", two=2, b=b)[:, :, 0, :]
                        dve.tensor_tensor(xo, xo, bank[3].rearrange("p (n b) -> p n b", b=b), ALU.add)\
                           .then_inc(S("X_level"), 1)
                    if more:
                        prepare(c + 1, n)
                    mem(c, n)

            def round_(c, more):
                ts = bass.ds(c * L, L)
                rv, kv_, vv = rkv[:, 0:8, ts], rkv[:, 8:16, ts], rkv[:, 16:24, ts]
                solve(c, more)
                mem(c, 5)
                need(dve, c, "U_ready")
                halves(dve, Ubd, Uc, "Ubd_ready")
                dve.tensor_tensor(Rc, rv, kv_, ALU.mult).then_inc(S("dve_step"), 1)
                own(dve)
                dve.tensor_tensor(Rc, Rc, per_unit("r_k"), ALU.mult).then_inc(S("rkr"), 1)
                mem(c, 6)
                need(dve, c, "S_done")
                dve.tensor_tensor(Sc, Sc, b8[3], ALU.add).then_inc(S("S_sum"), 1)
                need(dve, c, "S_sum")
                dve.tensor_tensor(Sc, Sc, WL.unsqueeze(2).to_broadcast([P, UN, L]), ALU.mult).then_inc(S("S_new"), 1)
                mem(c, 7)
                need(dve, c, "y_sum", "y_copied")
                dve.scalar_tensor_tensor(t1, b8[0], -1.0 / HD, cum, ALU.mult, ALU.add).then_inc(S("y_centred"), 1)
                if more:
                    scale_a(c + 1)
                mem(c, 8)
                need(dve, c, "y_sqsum")
                dve.tensor_scalar(t2, b8[1], 1.0 / HD, GN_EPS, ALU.mult, ALU.add).then_inc(S("y_var"), 1)
                need(dve, c, "bonus_sum")
                dve.tensor_tensor(Rc, b8[3], vv, ALU.mult).then_inc(S("bonus"), 1)
                if more:
                    scale_b(c + 1)
                    mem(c, 9)
                    take_b(c + 1)
                    mem(c, 10)
                    take_k(c + 1)
                    mem(c, 11, 12)
                else:
                    mem(c, 9, 10, 11)
                    for g in range(2):
                        need(dve, g, "y_high")
                        t = slice(YT0 + 8 + 4 * g, YT0 + 12 + 4 * g)
                        dve.tensor_tensor(hs[:, t, 1, :], y_swa[:, 4 * g:4 * g + 4, :], hs[:, t, 0, :].bitcast(F32),
                                          ALU.subtract).then_inc(S("y_split"), 1)
                need(dve, c, "y_root")
                dve.reciprocal(t2, t2).then_inc(S("dve_step"), 1)
                own(dve)
                if more:
                    mem(c, 13)
                dve.tensor_tensor(t1, t1, t2, ALU.mult).then_inc(S("dve_step"), 1)
                own(dve)
                dve.tensor_tensor(t1, t1, per_unit("lnx_w"), ALU.mult).then_inc(S("dve_step"), 1)
                own(dve)
                if more:
                    take_v(c + 1)
                    mem(c, 14)
                dve.tensor_tensor(t1, t1, per_unit("lnx_b"), ALU.add).then_inc(S("dve_step"), 1)
                own(dve)
                dve.tensor_tensor(rv, t1, Rc, ALU.add).then_inc(S("chunk_done"), 1)
                if more:
                    mem(c, 15)
                need(dve, c, "chunk_done")
            dve.wait_ge(S("mem_landed"), 16)
            for step in range(4):
                fill_dve(dve, "mem_norm", 2 * step, x, FILL_MEM)
                fill_dve(dve, "mem_norm", 2 * step + 1, x, FILL_MEM)
                prepare(0, step)
                if step < 3:
                    mem_chunk(dve, "dve", 0, 0, step)
            prepare(0, 4)
            norm_dve(dve, MEM)
            scale_a(0)
            scale_b(0)
            mem_chunk(dve, "dve", 0, 0, 3)
            dve.memset(Yi, 0.0).then_inc(S("Y_cleared"), 1)
            need(dve, 0, "Y_cleared")
            take_b(0)
            take_k(0)
            take_v(0)
            with dve.Fori(0, TC - 1) as c:
                own.rounds(c, 11)
                round_(c, True)
            own.end(TC - 1)
            round_(TC - 1, False)
            for g in range(4):
                need(dve, g, "gate_done")
                dve.tensor_tensor(rkv[:, 2 * g:2 * g + 2, :], rkv[:, 2 * g:2 * g + 2, :], b2[g], ALU.mult)\
                   .then_inc(S("y_gated"), 1)
            for g in range(4):
                need(dve, 2 + g, "y_high")
                t = slice(YT0 + 2 * g, YT0 + 2 * g + 2)
                dve.tensor_tensor(hs[:, t, 1, :], rkv[:, 2 * g:2 * g + 2, :], hs[:, t, 0, :].bitcast(F32),
                                  ALU.subtract).then_inc(S("y_split"), 1)
            dve.wait_ge(S("x_back"), 32)
            with dve.Fori(0, 4) as i:
                for u in range(2):
                    ahead(split_low, dve, V_OUT + 4 * u, 4, i, 8)
                    resid_dve(dve, 1, B_OUT + u, 2 * i + u, "xa_norm", FILL_XA, 1.0, "b_out", i, 2)
            ahead(split_low, dve, V_XQ, 4)
            norm_dve(dve, XA)

            def x_query(b, blk, i=0):
                add_low(dve, b, i, 2)
                dve.tensor_tensor(QX[:, bass.ds(2 * blk, 2), :], total[:, :, :], rb, ALU.mult).then_inc(S("xq_ready"), 1)
            x_query(B_XQ, 0)
            with dve.Fori(0, 3) as i:
                for u in range(1, 3):
                    ahead(split_low, dve, V_XQ + 4 * u, 4, i, 8)
                    x_query(B_XQ + u, 2 * i + u, i)
            ahead(split_low, dve, V_XQ + 28, 4)
            x_query(B_XQ + 7, 7)

            def x_max(h):
                k = 2 * (h % 2)
                dve.wait_ge(S("x_scores"), h + 1)
                dve.reduce_max(xmax[:, k:k + 2], b2[h % 2], AX_X).then_inc(S("dve_step"), 1)
                own(dve)
                dve.tensor_scalar(xneg[:, k:k + 2], xmax[:, k:k + 2], -XSCALE, None, ALU.mult)\
                   .then_inc(S("x_negmax"), 1)

            def x_norm(h):
                k = 2 * (h % 2)
                dve.wait_ge(S("x_exp"), h + 1)
                dve.reciprocal(xrec[:, k:k + 2], xsum[:, k:k + 2]).then_inc(S("dve_step"), 1)
                own(dve)
                dve.tensor_tensor(SX[:, k:k + 2, :], SX[:, k:k + 2, :],
                                  xrec[:, k:k + 2].unsqueeze(2).to_broadcast([P, 2, T]), ALU.mult)\
                   .then_inc(S("x_normed"), 1)

            def x_out(h):
                for g in range(2):
                    need(dve, 2 * h + g, "o_high")
                    a = YT0 + 4 * h + 2 * g
                    dve.tensor_tensor(hs[:, a:a + 2, 1, :], b2[3 - g], hs[:, a:a + 2, 0, :].bitcast(F32),
                                      ALU.subtract).then_inc(S("o_split"), 1)
            x_max(0)
            x_norm(0)
            for h in range(4):
                if h < 3:
                    x_max(h + 1)
                    x_norm(h + 1)
                x_out(h)
            with dve.Fori(0, 4) as i:
                for u in range(2):
                    ahead(split_low, dve, V_XO + 4 * u, 4, i, 8)
                    resid_dve(dve, 2, B_XO + u, 2 * i + u, "f2_norm", FILL_F2, 1.0, None, i, 2)
            ahead(split_low, dve, V_UP2, 4)
            norm_dve(dve, F2)
            ffn_dve(dve, 1, B_UP2, V_UP2, V_DOWN2)
            with dve.Fori(0, 3) as i:
                for u in range(2):
                    ahead(split_low, dve, V_DOWN2 + 12 * u, 12, i, 24)
                    resid_dve(dve, 3, B_DOWN2 + u, 2 * i + u, None, None, 0.5, None, i, 2)
            for u in range(6, 8):
                ahead(split_low, dve, V_DOWN2 + 12 * u, 12)
                resid_dve(dve, 3, B_DOWN2 + u, u, None, None, 0.5)
            norm_dve(dve, FINAL)
            for k in range(KT):
                m = dve.scalar_tensor_tensor(x[:, k, :], x[:, k, :], pc("final_norm", k), rstd[:, :], ALU.mult, ALU.mult)
                if k % 4 == 3:
                    m.then_inc(S("out_ready"), 1)

        @block.tensor
        def _(pe):
            need(pe, 0, "ones_ready")
            pe.wait_ge(S("ident_landed"), 16)
            ffn_pe(pe, 0, B_UP1, V_UP1, V_DOWN1, X1, FILL_X)
            with pe.Fori(0, 4) as i:
                for u in range(2):
                    products(pe, B_DOWN1 + u, V_DOWN1 + 12 * u, 11, hs, hidden(0), i, 24, 2)
            products(pe, B_Q, V_Q, 4, xs, filled(FILL_MIX))
            norm_pe(pe, MIX)
            for b in range(1, 4):
                products(pe, B_Q + b, V_Q + 4 * b, 4, xs)
            products(pe, B_KV, V_KV, 4, xs)
            products(pe, B_LORA, V_LORA, 4, xs)
            pe.wait_ge(S("swa_tables"), 16)
            need(pe, 0, "kv_in")
            pe.matmul(bank[0][:, 0:T], sc_("swap"), k_v[:, 0, :], start=True, stop=True).then_inc(S("k_swapped"), 1)
            for e in range(2):
                m = pe.transpose(bank[1][:, e * P:(e + 1) * P], k_v[:, 1, e * P:(e + 1) * P], ident[:, :])
            m.then_inc(S("v_turned"), 1)
            need(pe, 0, "k_rotated")
            for n in range(4):
                m = pe.matmul(b2[2 + n // 2][:, n % 2, :], sc_("select")[:, n * P:(n + 1) * P], krot,
                              start=True, stop=True)
            m.then_inc(S("k_selected"), 1)
            for t in range(KT):
                if t == 0:
                    pe.wait_ge(bank_free[0], 1 + B.before(B_TAIL))
                if t % 8 == 0:
                    pe.wait_ge(low_ready[(V_TAIL + t // 8) % RING], W.uses(V_TAIL + t // 8))
                s, a, c0 = (V_TAIL + t // 8) % RING, t % 8 // 2, t % 2 * P
                pe.matmul(acc[0][:, 0, :, :], parts[:, s, a, 0, c0:c0 + P], xs[:, t, :, :],
                          start=t == 0, stop=False, skip_group_check=True)
                m = pe.matmul(acc[0][:, 0, 1, :], parts[:, s, a, 1, c0:c0 + P], xs[:, t, 0, :],
                              start=False, stop=t == KT - 1, skip_group_check=True)
                if t % 8 == 7:
                    m.then_inc(parts_used[s], 1)
            need(pe, 3, "q_in")
            need(pe, 0, "kpad_ready")
            need(pe, 0, "vpad_ready")
            with pe.Fori(0, 4) as i:
                def rkvs(*js):
                    for j in js:
                        rkv_chunk(pe, "pe", i, j)
                pe.matmul(bank[0], sc_("swap"), q_all[:, bass.ds(i * 2, 2), :], start=True, stop=True)\
                  .then_inc(S("q_swapped"), 1)
                rkvs(0, 1)
                need(pe, i, "q_rotated")
                for h in range(4):
                    kp = kpad[:, bass.ds(i // 2 * 2 + h % 2, 1), :]
                    pe.matmul(bank[h][:, 0:128], qg[:, h // 2, 0:128], kp[:, :, 0:128], start=True, stop=True)
                    pe.matmul(bank[h][:, 128:384], qg[:, h // 2, 128:256], kp[:, :, :], start=True, stop=True)\
                      .then_inc(S("swa_scores"), 1)
                rkvs(2, 3, 4, 5, 6)
                need(pe, i, "swa_probs")
                for piece in range(3):
                    for h in range(4):
                        m = pe.transpose(bank[piece][:, h * P:(h + 1) * P], sc[:, h, piece * P:(piece + 1) * P],
                                         ident[:, :])
                m.then_inc(S("probs_turned"), 1)
                rkvs(7, 8)
                need(pe, i, "pt_ready", "vg_ready")
                for e in range(2):
                    for q in range(2):
                        terms = [(0, o, 0) for o in range(2)] if q == 0 else \
                            [(blk, o, 1 + blk) for o in range(2) for blk in range(2)]
                        for n, (blk, o, piece) in enumerate(terms):
                            m = pe.matmul(b2[3][:, e, q * P:(q + 1) * P], vg[:, 2 * blk + o, :],
                                          pt[:, 4 * piece + 2 * e + o, :], start=n == 0, stop=n == len(terms) - 1)
                m.then_inc(S("swa_out"), 1)
                rkvs(9, 10, 11)
                need(pe, i, "swa_done")
            pe.wait_ge(S("rw_cleared"), 8)
            pe.wait_ge(S("rw_tables"), 48)
            need(pe, 0, "lora_act")

            def mem(c, *js):
                for j in js:
                    if not (isinstance(c, int) and j >= 12):
                        mem_chunk(pe, "pe", c, 1 + j // 4, j % 4)

            def units(dst, lhs, rh, name):
                for u in range(UN):
                    m = pe.matmul(dst(u), lhs(u), rh(u), start=True, stop=True)
                m.then_inc(S(name), 1)

            def prepare(n, step):
                if step == 0:
                    need(pe, n, "tz_copied")
                    for h in range(2):
                        rows = slice(64 * h, 64 * h + 64)
                        for u in range(UN):
                            m = pe.matmul(b8[h][:, u, :], daw[rows, u * P:(u + 1) * P], tzc[rows, :],
                                          start=True, stop=True)
                    m.then_inc(S("lora_z"), 1)
                if step == 1:
                    need(pe, n, "kk_sq")
                    pe.matmul(bank[0], rc("same_head"), t2, start=True, stop=True).then_inc(S("kk_sum"), 1)

            def prod_b(n):
                need(pe, n, "B_scaled")
                units(lambda u: two[0][:, u, :], lambda u: Bh[:, u, :], lambda u: rhs[:, u, :], "B_prod")

            def prod_k(n):
                need(pe, n, "K_scaled")
                units(lambda u: two[1][:, u, :], lambda u: Kh[:, u, :], lambda u: rhs[:, u, :], "K_prod")

            def prod_a(n):
                need(pe, n, "Abd_ready", "Arb_ready")
                units(lambda u: two[0][:, u, :], lambda u: Abd[:, u, :], lambda u: Bh[:, u, :], "A_prod")

            def turn_b(n):
                need(pe, n, "Ark_ready")
                for u in range(UN):
                    m = pe.transpose(two[1][:, u, :], Bh[:, u, :], ident[:, :])
                m.then_inc(S("B_turned"), 1)

            def turn_k(n):
                need(pe, n, "A_ready")
                for u in range(UN):
                    m = pe.transpose(two[0][:, u, :], Kh[:, u, :], ident[:, :])
                m.then_inc(S("K_turned"), 1)

            def turn_v(n):
                need(pe, n, "BT_ready")
                units(lambda u: b8[2][:, u, :], lambda u: Pm[:, u, :], lambda u: rc("stack"), "V_turned")

            def solve(c, more):
                need(pe, c, "KT_ready", "Vc_ready", "Y_init")
                for n, b in enumerate(LEVELS):
                    pe.wait_ge(S("Am"), c * 5 + n + 1)
                    if n:
                        pe.wait_ge(S("Y_level"), c * 5 + n)
                        pe.wait_ge(S("X_level"), c * 4 + n)
                    if more and n == 1:
                        need(pe, c + 1, "z_a")
                    if more and n == 2:
                        need(pe, c + 1, "kk_norm")
                    units(lambda u: two[0][:, u, :], lambda u: Am[:, u, :], lambda u: Yi[:, u, :], "P_done")
                    mem_chunk(pe, "pe", c, 1 + n // 4, n % 4, range(0, KC // 2))
                    pe.wait_ge(S("P_ready"), c * 5 + n + 1)
                    units(lambda u: b8[2][:, u, :], lambda u: Xi[:, u, :], lambda u: odd(Pm[:, u, :], b, 1), "Y_more")
                    if n < 4:
                        units(lambda u: b8[3][:, u, :], lambda u: Pm[:, u, :], lambda u: odd(Xi[:, u, :], b, 0),
                              "X_more")
                    if more:
                        prepare(c + 1, n)
                    mem_chunk(pe, "pe", c, 1 + n // 4, n % 4, range(KC // 2, KC))

            def round_(c, more):
                solve(c, more)
                for u in range(UN):
                    pe.matmul(b8[0][:, u, :], Abd[:, u, :], Sc[:, u, :], start=True, stop=False, skip_group_check=True)
                    m = pe.matmul(b8[0][:, u, :], AakT[:, u, :], Vc[:, u, :], start=False, stop=True,
                                  skip_group_check=True)
                m.then_inc(S("R_done"), 1)
                mem(c, 5)
                need(pe, c, "R_ready")
                pe.wait_ge(S("Y_level"), c * 5 + 5)
                units(lambda u: b8[1][:, u, :], lambda u: Yi[:, u, :], lambda u: Rc[:, u, :], "U_done")
                mem(c, 6)
                need(pe, c, "Ubd_ready")
                for u in range(UN):
                    pe.matmul(b8[2][:, u, :], Sbd[:, u, :], rhs[:, u, 64:128], start=True, stop=False,
                              skip_group_check=True)
                    pe.matmul(b8[2][:, u, :], Vbd[:, u, :], ArkT[:, u, :], start=False, stop=False,
                              skip_group_check=True)
                    m = pe.matmul(b8[2][:, u, :], Ubd[:, u, :], ArbT[:, u, :], start=False, stop=True,
                                  skip_group_check=True)
                m.then_inc(S("y_done"), 1)
                for u in range(UN):
                    pe.matmul(b8[3][:, u, :], Bh[:, u, :], Uc[:, u, :], start=True, stop=False, skip_group_check=True)
                    m = pe.matmul(b8[3][:, u, :], Kh[:, u, :], Vc[:, u, :], start=False, stop=True,
                                  skip_group_check=True)
                m.then_inc(S("S_done"), 1)
                mem(c, 7)
                need(pe, c, "y_copied")
                pe.matmul(bank[0], rc("same_head"), cum, start=True, stop=True).then_inc(S("y_sum"), 1)
                need(pe, c, "rkr", "S_sum")
                pe.matmul(bank[3], rc("same_head"), Rc, start=True, stop=True).then_inc(S("bonus_sum"), 1)
                mem(c, 8)
                need(pe, c, "y_sq")
                pe.matmul(bank[1], rc("same_head"), t2, start=True, stop=True).then_inc(S("y_sqsum"), 1)
                if more:
                    mem(c, 9)
                    prod_b(c + 1)
                    mem(c, 10)
                    need(pe, c, "bonus")
                    prod_k(c + 1)
                    mem(c, 11)
                    prod_a(c + 1)
                    mem(c, 12)
                    turn_b(c + 1)
                    mem(c, 13)
                    turn_k(c + 1)
                    mem(c, 14)
                    turn_v(c + 1)
                    mem(c, 15)
                else:
                    mem(c, 9, 10, 11)
            prepare(0, 0)
            mem_chunk(pe, "pe", 0, 0, 0)
            need(pe, 0, "z_a")
            prepare(0, 1)
            mem_chunk(pe, "pe", 0, 0, 1)
            mem_chunk(pe, "pe", 0, 0, 2)
            norm_pe(pe, MEM)
            need(pe, 0, "kk_norm")
            prod_b(0)
            prod_k(0)
            mem_chunk(pe, "pe", 0, 0, 3)
            prod_a(0)
            turn_b(0)
            turn_k(0)
            turn_v(0)
            with pe.Fori(0, TC - 1) as c:
                round_(c, True)
            round_(TC - 1, False)
            pe.wait_ge(S("gup_landed"), 32)
            need(pe, 0, "gup_cleared")
            need(pe, TC - 1, "bonus", "y_var")
            for g in range(4):
                for e in range(2):
                    u = 2 * g + e
                    pe.matmul(b2[g][:, e, :], gup[:, 0, u * P:(u + 1) * P], lora[:, 1, :], start=True, stop=False,
                              skip_group_check=True)
                    m = pe.matmul(b2[g][:, e, :], gup[:, 1, u * P:(u + 1) * P], lora[:, 2, :], start=False, stop=True,
                                  skip_group_check=True)
                m.then_inc(S("gate_done"), 1)

            def mixed(pe, j):
                pe.wait_ge(S("y_split"), (1, 2, 4, 6)[j])
            with pe.Fori(0, 4) as i:
                for u in range(2):
                    products(pe, B_OUT + u, V_OUT + 4 * u, 4, hs, mixed, i, 8, 2, first_tile=YT0, order=(2, 3, 0, 1))
            products(pe, B_XQ, V_XQ, 4, xs, filled(FILL_XA))
            norm_pe(pe, XA)
            with pe.Fori(0, 3) as i:
                for u in range(1, 3):
                    products(pe, B_XQ + u, V_XQ + 4 * u, 4, xs, None, i, 8, 2)
            products(pe, B_XQ + 7, V_XQ + 28, 4, xs)
            pe.wait_ge(S("kv_back"), 32)

            def x_scores(h):
                pe.wait_ge(S("xq_ready"), 2 * h + 2)
                if h >= 2:
                    pe.wait_ge(S("x_exp"), h - 1)
                for q in range(2):
                    for t in range(4):
                        m = pe.matmul(b2[h % 2][:, q, :], QX[:, 4 * h + t, q * P:(q + 1) * P], KX[:, 4 * h + t, :],
                                      start=t == 0, stop=t == 3)
                m.then_inc(S("x_scores"), 1)

            def x_out(h):
                pe.wait_ge(S("x_normed"), h + 1)
                if h:
                    pe.wait_ge(S("o_split"), 2 * h)
                for q in range(2):
                    for t in range(2):
                        m = pe.transpose(b2[2][:, t, q * P:(q + 1) * P], SX[:, 2 * (h % 2) + q, t * P:(t + 1) * P],
                                         ident[:, :])
                m.then_inc(S("x_turned"), 1)
                pe.wait_ge(S("x_probs"), h + 1)
                for g in range(2):
                    for e in range(2):
                        a = h * 512 + (2 * g + e) * P
                        for t in range(2):
                            m = pe.matmul(b2[3 - g][:, e, :], VX[:, t, a:a + P], PX[:, 2 * (h % 2) + t, :],
                                          start=t == 0, stop=t == 1)
                    m.then_inc(S("o_done"), 1)
            x_scores(0)
            x_scores(1)
            for h in range(4):
                x_out(h)
                if h < 2:
                    x_scores(h + 2)

            def attended(pe, j):
                pe.wait_ge(S("o_split"), 2 * (j + 1))
            with pe.Fori(0, 4) as i:
                for u in range(2):
                    products(pe, B_XO + u, V_XO + 4 * u, 4, hs, attended, i, 8, 2, first_tile=YT0)
            ffn_pe(pe, 1, B_UP2, V_UP2, V_DOWN2, F2, FILL_F2)
            with pe.Fori(0, 4) as i:
                for u in range(2):
                    products(pe, B_DOWN2 + u, V_DOWN2 + 12 * u, 11, hs, hidden(1), i, 24, 2)
            norm_pe(pe, FINAL)


def kernel(**inputs):
    import numpy as _np
    import concourse.bacc as _bacc
    from concourse import mybir as _mybir
    from concourse.bass_utils import run_bass_kernel_spmd as _run

    nc = _bacc.Bacc("TRN2", target_bir_lowering=False, num_devices=1)
    f = {k: _np.asarray(v) for k, v in inputs.items()}
    arrays, A = {}, {}

    def dram(name, a):
        arrays[name] = _np.ascontiguousarray(a)
        A[name] = nc.dram_tensor(name, a.shape, _mybir.dt.from_np(a.dtype), kind="ExternalInput").ap()

    def tiles(a):
        return a.reshape(-1, P).T
    mu = f["rw_mu"][0]
    columns_of = {
        "b_out": tiles(f["b_out"][0]), "b_q": tiles(f["b_in_attn"][0, :1024]), "b_kv": tiles(f["b_in_attn"][0, 1024:]),
        "mu": tiles(mu[:3 * C]), "mu_lora": tiles(mu[LORA_COL:LORA_COL + 256]),
        "mu_tail": tiles(mu[TAIL_COL:TAIL_COL + P]), "w0": tiles(f["rw_w0"][0]), "a0": tiles(f["rw_a0"][0]),
        "k_k": tiles(f["rw_k_k"][0]), "k_a": tiles(f["rw_k_a"][0]), "r_k": tiles(f["rw_r_k"][0]),
        "lnx_w": tiles(f["rw_lnx_w"][0]), "lnx_b": tiles(f["rw_lnx_b"][0]),
        "sinks": _np.broadcast_to(f["attn_sinks"][0], (P, 16)), "final_norm": tiles(f["final_norm"]),
    }
    for n in ("f1_norm", "mix_norm", "mem_norm", "xa_norm", "f2_norm"):
        columns_of[n] = tiles(f[n][0])
    dram("params", _np.concatenate([columns_of[n] for n, _ in PARAMS], axis=1))
    dram("swa_consts", swa_consts())
    dram("rw_consts", rw_consts())
    dram("ident", _np.eye(P, dtype=_np.float32))
    dram("x_t", f["x"][0].T)
    dram("mem_t", f["mem"][0].T)
    for n in ("f1_gate", "f1_up", "f1_down", "w_in", "w_out", "w_xq", "w_xkv", "w_xo", "f2_gate", "f2_up", "f2_down",
              "rw_decay_up", "rw_aaa_up", "rw_gate_up"):
        dram(n, f[n][0])
    out = nc.dram_tensor("out_t", (D, T), _mybir.dt.float32, kind="ExternalOutput").ap()
    build(nc, A, out)
    r = _run(nc, [arrays], core_ids=[0])
    return _np.ascontiguousarray(r.results[0]["out_t"].T).reshape(1, T, D)
```

```python
from contextlib import ExitStack

import numpy as np
import concourse.bass as bass
from concourse import mybir

F32 = mybir.dt.float32
F32R = mybir.dt.float32r
ALU = mybir.AluOpType
ACT = mybir.ActivationFunctionType
AX_X = mybir.AxisListType.X

P = 128
D = 2048
T = 256
KT = D // P
D_FF = 5632
FT = D_FF // P
RMS_EPS = 1e-6
GN_EPS = 64e-5
HD = 64
C = 1024
UN = C // P
LORA_COL = 3 * C
GATE_COL = LORA_COL + 128
TAIL_COL = GATE_COL + 32
Q_COL = GATE_COL + 160
KV_COL = Q_COL + 1024
L = 64
TC = T // L
LEVELS = [2, 4, 8, 16, 32]
DECAY = float(np.exp(-0.5))

COLS = 2 * P
KC = 4
CHUNK = KC * COLS
RING = 4
LEAD = 3
STEPS = D_FF // COLS

PARAMS = [("f1_norm", 16), ("mix_norm", 16), ("mem_norm", 16), ("xa_norm", 16), ("f2_norm", 16), ("final_norm", 16),
          ("b_out", 16), ("b_q", 8), ("b_kv", 2), ("mu", 24), ("mu_lora", 2), ("mu_tail", 1), ("w0", 8), ("a0", 8),
          ("k_k", 8), ("k_a", 8), ("r_k", 8), ("lnx_w", 8), ("lnx_b", 8), ("sinks", 16)]
PCOL = {}
for _n, _k in PARAMS:
    PCOL[_n] = sum(k for _, k in PARAMS[:len(PCOL)])
NPAR = sum(k for _, k in PARAMS)

SWA_CONSTS = [("swap", 128), ("select", 512), ("cos", 256), ("sin", 256), ("band", 384)]
RW_CONSTS = [("stack", 64), ("same_head", 128), ("pair", 128), ("level", 640), ("pair_t", 64), ("before_t", 64),
             ("upto_t", 64)]


def columns(spec):
    at, out = 0, {}
    for n, k in spec:
        out[n] = (at, at + k)
        at += k
    return out, at


def swa_consts():
    p = np.arange(P)
    swap = np.zeros((P, P), np.float32)
    swap[p, p ^ 32] = 1.0
    select = np.zeros((P, 4, P), np.float32)
    for g in range(2):
        for e in range(2):
            select[g * HD + np.arange(HD), 2 * g + e, e * HD + np.arange(HD)] = 1.0
    freq = (np.float32(10000.0) ** (-np.arange(0, HD, 2, dtype=np.float32) / np.float32(HD))).astype(np.float32)
    ang = np.arange(T, dtype=np.float32)[None, :] * freq[p % 32][:, None]
    cos, sin = np.cos(ang), np.sin(ang) * np.where(p % HD < 32, -1.0, 1.0)[:, None]
    q = np.arange(P)[:, None]
    k = np.arange(P)[None, :]
    own = np.where(q >= k, 0.0, -1e30)
    prev = np.where(q < k, 0.0, -1e30)
    band = np.concatenate([own, prev, own], axis=1)
    return np.concatenate([swap, select.reshape(P, -1), cos, sin, band], axis=1).astype(np.float32)


def rw_consts():
    p = np.arange(P)
    h, t = p // L, p % L
    stack = (t[:, None] == np.arange(L)[None, :])
    same = h[:, None] == h[None, :]

    def off(b, row, col):
        return (row // (2 * b) == col // (2 * b)) & (row // b % 2 == 1) & (col // b % 2 == 0)
    pair = same & off(1, t[:, None], t[None, :])
    level = [same & off(b, t[:, None], t[None, :]) for b in LEVELS]
    c = np.arange(L)
    pair_t = off(1, c[None, :], t[:, None])
    before_t = t[:, None] < c[None, :]
    upto_t = t[:, None] <= c[None, :]
    return np.concatenate([stack, same, pair] + level + [pair_t, before_t, upto_t], axis=1).astype(np.float32)


class Weights:

    def __init__(self):
        self.real = []

    def add(self, pattern, times=1):
        first = len(self.real)
        self.real += list(pattern) * times
        return first

    def count(self, v):
        return sum(self.real[u] for u in range(v % RING, min(v + 1, len(self.real)), RING))

    def uses(self, v, i=0, per=0):
        n = self.count(v)
        if isinstance(i, int) and i == 0:
            return n
        return i * (self.count(v + per) - n) + n

    def missing(self, v):
        return v >= len(self.real) or not self.real[v]


class Blocks:

    def __init__(self):
        self.pair = []

    def add(self, pairs, times=1):
        first = len(self.pair)
        self.pair += list(pairs) * times
        return first

    def before(self, b, i=0, nb=0):
        n = sum(q == self.pair[b] for q in self.pair[:b])
        if isinstance(i, int) and i == 0:
            return n
        return i * (sum(q == self.pair[b] for q in self.pair[:b + nb]) - n) + n


class Own:

    def __init__(self, sem):
        self.sem, self.n, self.i, self.per = sem, 0, 0, 0

    def __call__(self, eng):
        self.n += 1
        eng.wait_ge(self.sem, self.i * self.per + self.n if self.per else self.n)

    def rounds(self, i, per):
        self.i, self.per, self.start = i, per, self.n

    def end(self, rounds):
        assert self.n == self.start + self.per, (self.n - self.start, self.per)
        self.n, self.per = self.start + rounds * self.per, 0


def build(nc, A, out):
    W, B = Weights(), Blocks()
    full = [True] * 4
    V_UP1, B_UP1 = W.add(full, 2 * STEPS), B.add([0, 1], STEPS)
    V_DOWN1, B_DOWN1 = W.add([True] * 11 + [False], 8), B.add([0, 1], 4)
    V_Q, B_Q = W.add(full, 4), B.add([0, 1], 2)
    V_KV, B_KV = W.add(full), B.add([0])
    V_LORA, B_LORA = W.add(full), B.add([1])
    V_TAIL, B_TAIL = W.add([True, True, False, False]), B.add([0])
    V_RKV, B_RKV = W.add(full, 12), B.add([1, 0], 6)
    V_MEM, B_MEM = W.add(full, 16), B.add([1, 0], 8)
    V_OUT, B_OUT = W.add(full, 8), B.add([1, 0], 4)
    V_XQ, B_XQ = W.add(full, 8), B.add([1, 0], 4)
    V_XO, B_XO = W.add(full, 8), B.add([1, 0], 4)
    V_UP2, B_UP2 = W.add(full, 2 * STEPS), B.add([1, 0], STEPS)
    V_DOWN2, B_DOWN2 = W.add([True] * 11 + [False], 8), B.add([1, 0], 4)
    X1, MIX, MEM, XA, F2, FINAL = range(6)
    FILL_X, FILL_MIX, FILL_MEM, FILL_XA, FILL_F2 = range(5)

    ctx = ExitStack()
    with ctx:
        def sb(name, shape, dt=F32):
            return ctx.enter_context(nc.sbuf_tensor(name, shape, dt))

        sems = {}

        def S(name):
            if name not in sems:
                sems[name] = ctx.enter_context(nc.semaphore(name))
            return sems[name]

        def need(eng, i, *names):
            for n in names:
                eng.wait_ge(S(n), i + 1)

        raw = sb("raw", [P, RING, CHUNK])
        parts = sb("parts", [P, RING, KC, 2, COLS], F32R)
        xs = sb("xs", [P, KT, 2, T], F32R)
        par = sb("par", [P, NPAR])
        low = sb("low", [P, 2, 2, T])
        total = sb("total", [P, 2, T])
        gate = sb("gate", [P, 2, T])
        sig = sb("sig", [P, 2, T])
        up = sb("up", [P, 2, T])
        sq = sb("sq", [P, 2, T])
        sqacc = sb("sqacc", [P, T])
        ones = sb("ones", [P, P])
        ident = sb("unit", [P, P])
        ms = sb("ms", [P, T])
        rstd = sb("rstd", [P, T])
        small = sb("small", [P, 152])
        rcol = sb("rcol", [P, 2])
        HS_AT = KT * T
        M_WORDS = 27632
        at = -(-nc.sbuf_base // 32) * 32
        M = sb("M", [P, M_WORDS])
        hs = nc.alloc_sbuf_tensor_at("hs", [P, FT, 2, T], F32R, offset=at + 4 * HS_AT)

        def view(words, *dims):
            a = cursor[0]
            cursor[0] += words
            assert cursor[0] <= M_WORDS, cursor[0]
            v = M[:, a:a + words]
            if len(dims) == 2:
                v = v.rearrange("p (a b) -> p a b", b=dims[1])
            if len(dims) == 3:
                v = v.rearrange("p (a b c) -> p a b c", b=dims[1], c=dims[2])
            return v

        cursor = [0]
        x = view(HS_AT, KT, T)
        rkv = view(24 * T, 24, T)
        lora = view(3 * T, 3, T)
        q_all = view(UN * T, UN, T)
        WORK = cursor[0]
        swc, nsw = columns(SWA_CONSTS)
        swt = view(nsw)
        k_v = view(2 * T, 2, T)
        krot = view(T)
        ktmp = view(T)
        kpad = view(4 * T, 4, T)
        vpad = view(2 * 512, 2, 512)
        vg = view(512, 4, P)
        qg = view(512, 2, T)
        qtmp = view(512, 2, T)
        sc = view(4 * 384, 4, 384)
        pt = view(12 * P, 12, P)
        rwc, nrw = columns(RW_CONSTS)
        cursor[0] = WORK
        rwt = view(nrw)
        Y_SWA = cursor[0]
        daw = view(C)
        aa = view(512, UN, L)
        kk = view(512, UN, L)
        y_swa = M[:, Y_SWA:Y_SWA + 2048].rearrange("p (a b) -> p a b", b=T)
        Bh = view(1024, UN, P)
        Kh = view(1024, UN, P)
        Abd = view(1024, UN, P)
        rhs = view(1024, UN, P)
        Wx = view(UN * 65, UN, 65)
        Winv = view(512, UN, L)
        cum = view(512, UN, L)
        WL = small[:, 64:72]
        ArkT = view(512, UN, L)
        ArbT = view(512, UN, L)
        AakT = view(1024, UN, P)
        Pm = view(1024, UN, P)
        Ubd = Pm
        X0 = [0]

        def xview(words, *dims):
            a = X0[0]
            X0[0] += words
            assert X0[0] <= HS_AT
            return M[:, a:a + words].rearrange("p (a b) -> p a b", b=dims[1])
        Xi = xview(1024, UN, P)
        Yi = xview(1024, UN, P)
        gup = M[:, X0[0]:X0[0] + 2 * C].rearrange("p (a b) -> p a b", b=C)
        Am = xview(1024, UN, P)
        Araw = xview(1024, UN, P)
        Vbd = view(1024, UN, P)
        Sbd = view(1024, UN, P)
        shifted = M[:, cursor[0] - 1024:cursor[0] - 510].rearrange("p (a b) -> p a b", b=257)
        Sc = view(512, UN, L)
        t1 = sig[:, :, :].rearrange("p a b -> p (a b)").rearrange("p (a b) -> p a b", b=L)
        tzc = small[:, 0:64]
        Vc, Uc, Rc, t2 = (q_all[:, 2 * n:2 * n + 2, :].rearrange("p a b -> p (a b)").rearrange("p (a b) -> p a b", b=L)
                      for n in range(4))
        cursor[0] = HS_AT
        KX = view(KT * T, KT, T)
        VX = view(2 * D, 2, D)
        QX = view(KT * T, KT, T)
        SX = view(1024, 4, T)
        PX = view(1024, 4, T)
        YT0 = FT - KT
        assert cursor[0] <= HS_AT + YT0 * 512
        assert Y_SWA + 2048 <= HS_AT + YT0 * 512

        acc = [ctx.enter_context(nc.psum_tensor(f"acc{p}", [P, 2, 2, T], F32)) for p in range(2)]
        mid = ctx.enter_context(nc.psum_tensor("mid", [P, 4, 512], F32))
        bank = [mid[:, n, :] for n in range(4)]
        b8 = [bk.rearrange("p (u t) -> p u t", t=L) for bk in bank]
        b2 = [bk.rearrange("p (u t) -> p u t", t=T) for bk in bank]
        two = [mid[:, 2 * n:2 * n + 2, :].rearrange("p b (u t) -> p (b u) t", t=P) for n in range(2)]
        dram_x = nc.dram_tensor("spill_x", (D, T), F32, kind="Internal").ap().rearrange("(t p) n -> p t n", p=P)
        dram_k = nc.dram_tensor("spill_k", (D, T), F32, kind="Internal").ap().rearrange("(t p) n -> p t n", p=P)
        dram_v = nc.dram_tensor("spill_v", (T, D), F32, kind="Internal").ap().rearrange("(t p) n -> p t n", p=P)
        dram_q = nc.dram_tensor("spill_q", (C, T), F32, kind="Internal").ap().rearrange("(t p) n -> p t n", p=P)
        out_v = out.rearrange("(t p) n -> p t n", p=P)

        raw_landed = [S(f"raw_landed{s}") for s in range(RING)]
        high_ready = [S(f"high_ready{s}") for s in range(RING)]
        low_ready = [S(f"low_ready{s}") for s in range(RING)]
        parts_used = [S(f"parts_used{s}") for s in range(RING)]
        bank_free = [S(f"bank_free{p}") for p in range(2)]
        low_copied = S("low_copied")
        own = Own(S("dve_step"))
        kv_spilled = [S(f"kv_spilled{p}") for p in range(2)]
        block = ctx.enter_context(nc.Block())

        def mem_block(n, c):
            return n in (1, 2), (c * 2, c * 2 + 8, c * 2 + 9, c * 2 + 1, c * 2 + 2)[n]

        def pc(name, k=0):
            a = PCOL[name] + k
            return par[:, bass.ds(a, 1)] if not isinstance(a, int) else par[:, a:a + 1]

        def plain(eng):
            eng.sem_inc(S("passed"), 1)

        def per_unit(name):
            return par[:, PCOL[name]:PCOL[name] + UN].unsqueeze(2).to_broadcast([P, UN, L])

        def rc(name):
            a, b = rwc[name]
            return rwt[:, a:b]

        def sc_(name):
            a, b = swc[name]
            return swt[:, a:b]

        def load(sp, v, src, i=0, per=0):
            s, n = v % RING, W.uses(v, i, per)
            if W.count(v) > 1:
                sp.wait_ge(low_ready[s], n - 1)
                if not isinstance(i, int):
                    plain(sp)
            sp.dma_start(raw[:, s, :].rearrange("p (t n) -> p t n", n=src.shape[2]), src).then_inc(raw_landed[s], 16)

        def split_high(act, v, i=0, per=0):
            if W.missing(v):
                return
            s, n = v % RING, W.uses(v, i, per)
            act.wait_ge(raw_landed[s], 16 * n)
            if W.count(v) > 1:
                act.wait_ge(parts_used[s], n - 1)
            act.activation(parts[:, s, :, 0, :], raw[:, s, :].rearrange("p (t n) -> p t n", n=COLS), ACT.Copy)\
               .then_inc(high_ready[s], 1)

        def split_low(dve, v, i=0, per=0):
            if W.missing(v):
                return
            s = v % RING
            dve.wait_ge(high_ready[s], W.uses(v, i, per))
            dve.tensor_tensor(parts[:, s, :, 1, :], raw[:, s, :].rearrange("p (t n) -> p t n", n=COLS),
                              parts[:, s, :, 0, :].bitcast(F32), ALU.subtract).then_inc(low_ready[s], 1)

        def ahead(split, eng, v, chunks, i=0, per=0):
            for j in range(chunks):
                split(eng, v + j + LEAD, i, per)

        def chunk_products(pe, b, v, j, chunks, moving, ready=None, i=0, per=0, nb=0, by_token=False, first_tile=0,
                           order=None, tiles=range(KC)):
            p, s = B.pair[b], (v + j) % RING
            if tiles[0] == 0:
                if j == 0:
                    pe.wait_ge(bank_free[p], 1 + B.before(b, i, nb))
                if ready is not None:
                    ready(pe, j)
                pe.wait_ge(low_ready[s], W.uses(v + j, i, per))
            for t in tiles:
                k = j * KC + t
                at = first_tile + (order[j] if order else j) * KC + t
                first, last = k == 0, k == chunks * KC - 1
                for n in range(2):
                    if by_token:
                        pe.matmul(acc[p][:, n, :, :], moving[:, k, 0, n * P:(n + 1) * P], parts[:, s, t, :, :],
                                  start=first, stop=False, skip_group_check=True)
                        m = pe.matmul(acc[p][:, n, 1, :], moving[:, k, 1, n * P:(n + 1) * P], parts[:, s, t, 0, :],
                                      start=False, stop=last, skip_group_check=True)
                    else:
                        pe.matmul(acc[p][:, n, :, :], parts[:, s, t, 0, n * P:(n + 1) * P],
                                  moving[:, at, :, :], start=first, stop=False, skip_group_check=True)
                        m = pe.matmul(acc[p][:, n, 1, :], parts[:, s, t, 1, n * P:(n + 1) * P],
                                      moving[:, at, 0, :], start=False, stop=last, skip_group_check=True)
            if tiles[-1] == KC - 1:
                m.then_inc(parts_used[s], 1)

        def products(pe, b, v, chunks, moving, ready=None, i=0, per=0, nb=0, **kw):
            for j in range(chunks):
                chunk_products(pe, b, v, j, chunks, moving, ready, i, per, nb, **kw)

        def copy_low(act, b, v_last, i=0, per=0):
            p = B.pair[b]
            act.wait_ge(parts_used[v_last % RING], W.uses(v_last, i, per))
            act.activation(low[:, p, :, :], acc[p][:, :, 1, :], ACT.Copy).then_inc(low_copied, 1)

        def add_low(dve, b, i=0, nb=0):
            p = B.pair[b]
            dve.wait_ge(low_copied, b + 1 + i * nb)
            dve.tensor_tensor(total[:, :, :], acc[p][:, :, 0, :], low[:, p, :, :], ALU.add).then_inc(bank_free[p], 1)
            dve.wait_ge(bank_free[p], 2 + B.before(b, i, nb))

        rb = rstd[:, :].unsqueeze(1).to_broadcast([P, 2, T])

        def fill_act(act, norm, gain, blk, src, fill):
            for e in range(2):
                k = 2 * blk + e
                m = act.activation(xs[:, bass.ds(k, 1), 0, :], src[:, bass.ds(k, 1), :], ACT.Copy, scale=pc(gain, k))
            m.then_inc(S("xs_high"), 1)
            if norm not in (X1, MEM):
                square(act, norm, blk, src)

        def square(act, norm, blk, src):
            act.wait_ge(S("sq_added"), 16 * norm + 2 * blk + 1)
            plain(act)
            act.activation(sq[:, :, :], src[:, bass.ds(2 * blk, 2), :], ACT.Square).then_inc(S("sq_ready"), 1)

        def fill_dve(dve, gain, blk, src, fill):
            dve.wait_ge(S("xs_high"), 8 * fill + blk + 1)
            for e in range(2):
                k = 2 * blk + e
                m = dve.scalar_tensor_tensor(xs[:, bass.ds(k, 1), 1, :], src[:, bass.ds(k, 1), :], pc(gain, k),
                                             xs[:, bass.ds(k, 1), 0, :].bitcast(F32), ALU.mult, ALU.subtract)
            m.then_inc(S("xs_ready"), 1)

        def filled(fill):
            def ready(pe, j):
                pe.wait_ge(S("xs_ready"), 8 * fill + 2 * (j + 1))
            return ready

        def sum_squares(pool, norm, blocks=8, beside=None):
            def block_squares(blk):
                if norm == X1:
                    xx = x[:, 2 * blk:2 * blk + 2, :]
                    pool.wait_ge(S(f"x_landed{blk // 2}"), 16)
                    pool.tensor_tensor(sq[:, :, :], xx, xx, ALU.mult).then_inc(S("sq_ready"), 1)
                pool.wait_ge(S("sq_ready"), 8 * norm + blk + 1)
                pool.tensor_tensor(sqacc[:, :], sqacc[:, :], sq[:, 0, :], ALU.add).then_inc(S("sq_added"), 1)
                pool.wait_ge(S("sq_added"), 16 * norm + 2 * blk + 2)
                pool.tensor_tensor(sqacc[:, :], sqacc[:, :], sq[:, 1, :], ALU.add).then_inc(S("sq_added"), 1)
                pool.wait_ge(S("sq_added"), 16 * norm + 2 * blk + 3)
            if norm:
                pool.wait_ge(S("ms_ready"), norm)
            pool.memset(sqacc[:, :], 0.0).then_inc(S("sq_cleared"), 1)
            pool.wait_ge(S("sq_cleared"), norm + 1)
            if beside or norm == X1:
                for blk in range(blocks):
                    block_squares(blk)
                    if beside:
                        beside(blk)
            else:
                with pool.Fori(0, blocks) as blk:
                    block_squares(blk)

        def norm_pe(pe, norm):
            if norm == FINAL:
                pe.wait_ge(S("sq_added"), 16 * norm + 15)
                pe.matmul(bank[0][:, 0:T], ones[:, :], sqacc[:, :], start=True, stop=False)
                pe.wait_ge(S("sq_ready"), 8 * norm + 8)
                pe.matmul(bank[0][:, 0:T], ones[:, :], sq[:, 0, :], start=False, stop=False)
                pe.matmul(bank[0][:, 0:T], ones[:, :], sq[:, 1, :], start=False, stop=True).then_inc(S("ms_ready"), 1)
                return
            pe.wait_ge(S("sq_added"), 16 * norm + 17)
            to = bank[2 if norm == MEM else 0]
            if norm == MEM:
                for e in range(2):
                    pe.matmul(to[:, 256 + e:257 + e], sqacc[:, e * P:(e + 1) * P], ones[:, 0:1],
                              start=True, stop=True)
            pe.matmul(to[:, 0:T], ones[:, :], sqacc[:, :], start=True, stop=True).then_inc(S("ms_ready"), 1)

        def norm_act(act, norm):
            act.wait_ge(S("ms_eps"), norm + 1)
            if norm == MEM:
                act.activation(small[:, 146:148], small[:, 144:146], ACT.Sqrt)
            act.activation(ms[:, :], ms[:, :], ACT.Sqrt).then_inc(S("root_ready"), 1)

        def norm_dve(dve, norm):
            dve.wait_ge(S("ms_ready"), norm + 1)
            to = bank[2 if norm == MEM else 0]
            if norm == MEM:
                dve.tensor_scalar(small[:, 144:146], to[:, 256:258], RMS_EPS, None, ALU.add)
            dve.tensor_scalar(ms[:, :], to[:, 0:T], RMS_EPS, None, ALU.add).then_inc(S("ms_eps"), 1)
            dve.wait_ge(S("root_ready"), norm + 1)
            if norm == MEM:
                dve.reciprocal(rcol[:, :], small[:, 146:148])
            dve.reciprocal(rstd[:, :], ms[:, :]).then_inc(S("dve_step"), 1)
            own(dve)

        def b_step(b):
            base = B_UP1 if b < B_DOWN1 else B_UP2
            return (b - base) // 2 + 1

        def ffn_act(act, ffn, b0, v0, vend, norm):
            def gate_part(b, v, i=0):
                copy_low(act, b, v + 3, i, 8)
                sigmoid(STEPS * ffn + b_step(b) + i)

            def sigmoid(n):
                act.wait_ge(S("gate_ready"), n)
                act.activation(sig[:, :, :], gate[:, :, :], ACT.Sigmoid).then_inc(S("sigmoid_ready"), 1)

            def up_part(b, v, step, i=0):
                n = STEPS * ffn + b_step(b) + i
                copy_low(act, b, v + 3, i, 8)
                act.wait_ge(S("hidden_ready"), n)
                plain(act)
                act.activation(hs[:, bass.ds(step * 2, 2), 0, :], total[:, :, :], ACT.Copy)\
                   .then_inc(S("hidden_high"), 1)
            copy_low(act, b0, v0 + 3)
            ahead(split_high, act, v0 + 4, 2)
            norm_act(act, norm)
            sigmoid(STEPS * ffn + 1)
            ahead(split_high, act, v0 + 6, 2)
            up_part(b0 + 1, v0 + 4, 0)
            ahead(split_high, act, v0 + 8, 4)
            gate_part(b0 + 2, v0 + 8)
            with act.Fori(0, STEPS - 2) as i:
                ahead(split_high, act, v0 + 12, 4, i, 8)
                up_part(b0 + 3, v0 + 12, i + 1, i)
                ahead(split_high, act, v0 + 16, 4, i, 8)
                gate_part(b0 + 4, v0 + 16, i)
            ahead(split_high, act, vend - 4, 4)
            up_part(b0 + 2 * STEPS - 1, vend - 4, STEPS - 1)

        def ffn_dve(dve, ffn, b0, v0, vend, norm):
            def gate_part(b, i=0):
                add_low(dve, b, i, 2)
                scale_gate()

            def scale_gate():
                dve.tensor_tensor(gate[:, :, :], total[:, :, :], rb, ALU.mult).then_inc(S("gate_ready"), 1)

            def up_part(b, step, i=0):
                n = STEPS * ffn + b_step(b) + i
                add_low(dve, b, i, 2)
                dve.tensor_tensor(up[:, :, :], total[:, :, :], rb, ALU.mult).then_inc(S("dve_step"), 1)
                own(dve)
                dve.tensor_tensor(gate[:, :, :], gate[:, :, :], up[:, :, :], ALU.mult).then_inc(S("dve_step"), 1)
                own(dve)
                dve.wait_ge(S("sigmoid_ready"), n)
                dve.tensor_tensor(total[:, :, :], gate[:, :, :], sig[:, :, :], ALU.mult)\
                   .then_inc(S("hidden_ready"), 1)
                dve.wait_ge(S("hidden_high"), n)
                dve.tensor_tensor(hs[:, bass.ds(step * 2, 2), 1, :], total[:, :, :],
                                  hs[:, bass.ds(step * 2, 2), 0, :].bitcast(F32), ALU.subtract)\
                   .then_inc(S("hidden_split"), 1)
            add_low(dve, b0)
            ahead(split_low, dve, v0 + 4, 2)
            norm_dve(dve, norm)
            scale_gate()
            ahead(split_low, dve, v0 + 6, 2)
            up_part(b0 + 1, 0)
            ahead(split_low, dve, v0 + 8, 4)
            gate_part(b0 + 2)
            with dve.Fori(0, STEPS - 2) as i:
                own.rounds(i, 2)
                ahead(split_low, dve, v0 + 12, 4, i, 8)
                up_part(b0 + 3, i + 1, i)
                ahead(split_low, dve, v0 + 16, 4, i, 8)
                gate_part(b0 + 4, i)
            own.end(STEPS - 2)
            ahead(split_low, dve, vend - 4, 4)
            up_part(b0 + 2 * STEPS - 1, STEPS - 1)

        def ffn_pe(pe, ffn, b0, v0, vend, norm, fill):
            products(pe, b0, v0, 4, xs, filled(fill))
            for j in range(4):
                if j == (3 if norm == X1 else 0):
                    norm_pe(pe, norm)
                chunk_products(pe, b0 + 1, v0 + 4, j, 4, xs)
            with pe.Fori(0, STEPS - 1) as i:
                products(pe, b0 + 2, v0 + 8, 4, xs, None, i, 8, 2)
                products(pe, b0 + 3, v0 + 12, 4, xs, None, i, 8, 2)

        def hidden(ffn):
            def ready(pe, j):
                pe.wait_ge(S("hidden_split"), STEPS * ffn + 2 * (j + 1))
            return ready

        def resid_act(act, res, b, v_last, blk, norm, gain, fill, i=0, per=0):
            copy_low(act, b, v_last, i, per)
            act.wait_ge(S("x_updated"), 8 * res + blk + 1)
            plain(act)
            if fill is None:
                act.wait_ge(S("sq_added"), 2 * (8 * norm + blk) + 1)
                plain(act)
                act.activation(sq[:, :, :], x[:, bass.ds(2 * blk, 2), :], ACT.Square).then_inc(S("sq_ready"), 1)
            else:
                fill_act(act, norm, gain, blk, x, fill)

        def resid_dve(dve, res, b, blk, gain, fill, half, bias=None, i=0, nb=0):
            add_low(dve, b, i, nb)
            xx = x[:, bass.ds(2 * blk, 2), :]
            if bias:
                for e in range(2):
                    xe = x[:, bass.ds(2 * blk + e, 1), :]
                    m = dve.scalar_tensor_tensor(xe, total[:, e:e + 1, :], pc(bias, 2 * blk + e), xe, ALU.add, ALU.add)
            else:
                m = dve.scalar_tensor_tensor(xx, total[:, :, :], half, xx, ALU.mult, ALU.add)
            m.then_inc(S("x_updated"), 1)
            dve.wait_ge(S("x_updated"), 8 * res + blk + 1)
            if fill is not None:
                fill_dve(dve, gain, blk, x, fill)

        @block.sync
        def _(sp):
            def cols(name):
                return A[name].rearrange("(t p) n -> p t n", p=P)

            def piece(w, j, c0):
                return w[:, KC * j:KC * (j + 1), c0:c0 + COLS] if isinstance(c0, int) else \
                    w[:, KC * j:KC * (j + 1), bass.ds(c0, COLS)]

            def ffn(v_up, v_down, pre):
                wg, wu, wd = cols(pre + "_gate"), cols(pre + "_up"), cols(pre + "_down")
                for j in range(8):
                    load(sp, v_up + j, piece((wg, wu)[j // 4], j % 4, 0))
                with sp.Fori(0, STEPS - 1) as i:
                    for j in range(8):
                        load(sp, v_up + 8 + j, piece((wg, wu)[j // 4], j % 4, i * COLS + COLS), i, 8)
                with sp.Fori(0, 8) as i:
                    for j in range(11):
                        load(sp, v_down + j, piece(wd, j, i * COLS), i, 12)

            def square(v, name, c0=0, order=(0, 1, 2, 3)):
                w = cols(name)
                with sp.Fori(0, 8) as i:
                    for j in range(4):
                        load(sp, v + j, piece(w, order[j], i * COLS + c0), i, 4)
            ffn(V_UP1, V_DOWN1, "f1")
            win = cols("w_in")
            for b in range(4):
                for j in range(4):
                    load(sp, V_Q + 4 * b + j, piece(win, j, Q_COL + COLS * b))
                if b == 0:
                    sp.wait_ge(S("x_updated"), 8)
                sp.dma_start(dram_x[:, 4 * b:4 * b + 4, :], x[:, 4 * b:4 * b + 4, :]).then_inc(S("x_spilled"), 16)
            for j in range(4):
                load(sp, V_KV + j, piece(win, j, KV_COL))
            for j in range(4):
                load(sp, V_LORA + j, piece(win, j, LORA_COL))
            for j in range(2):
                load(sp, V_TAIL + j, win[:, 8 * j:8 * j + 8, TAIL_COL:TAIL_COL + P])
            with sp.Fori(0, 12) as i:
                for j in range(4):
                    load(sp, V_RKV + j, piece(win, j, i * COLS), i, 4)
            wkv = cols("w_xkv")
            for j in range(4):
                load(sp, V_MEM + j, piece(wkv, j, 0))
            with sp.Fori(0, TC - 1) as c:
                for m in range(1, 5):
                    for j in range(4):
                        load(sp, V_MEM + 4 * m + j, piece(wkv, j, mem_block(m, c)[1] * COLS), c, 16)
            for m in range(1, 4):
                for j in range(4):
                    load(sp, V_MEM + 4 * m + j, piece(wkv, j, mem_block(m, TC - 1)[1] * COLS), TC - 1, 16)
            square(V_OUT, "w_out", 0, (2, 3, 0, 1))
            square(V_XQ, "w_xq")
            square(V_XO, "w_xo")
            ffn(V_UP2, V_DOWN2, "f2")
            for g in (0, 1, 3, 2):
                if g == 3:
                    sp.wait_ge(S("last_out_ready"), 1)
                else:
                    sp.wait_ge(S("out_ready"), g + 1)
                sp.dma_start(out_v[:, 4 * g:4 * g + 4, :], x[:, 4 * g:4 * g + 4, :]).then_inc(S("stored"), 16)
            sp.wait_ge(S("stored"), 64)

        @block.gpsimd
        def _(pool):
            pool.memset(small[:, 140:141], 0.0).then_inc(bank_free[0], 1)
            pool.memset(small[:, 141:142], 0.0).then_inc(bank_free[1], 1)
            pool.memset(small[:, 142:143], 0.0).then_inc(S("sq_added"), 1)
            pool.memset(ones[:, :], 1.0 / D).then_inc(S("ones_ready"), 1)
            sum_squares(pool, X1)
            sum_squares(pool, MIX)
            pool.dma_start(swt, A["swa_consts"]).then_inc(S("swa_tables"), 16)
            pool.memset(vpad[:, :, :], 0.0).then_inc(S("vpad_cleared"), 1)
            pool.memset(shifted[:, :, 0:1], 0.0).then_inc(S("shift_cleared"), 1)
            pool.wait_ge(S("xs_ready"), 8 * FILL_MEM)
            mem_in = A["mem_t"].rearrange("(t p) n -> p t n", p=P)
            pool.wait_ge(S("x_spilled"), 64)
            for g in range(4):
                if g:
                    need(pool, (0, 0, 0, 1)[g], ("", "kv_in", "lora_ready", "lora_ready")[g])
                pool.dma_start(x[:, 4 * g:4 * g + 4, :], mem_in[:, 4 * g:4 * g + 4, :]).then_inc(S("mem_landed"), 16)
            sum_squares(pool, MEM)
            pool.wait_ge(S("swa_probs"), 4)
            pool.dma_start(rwt, A["rw_consts"]).then_inc(S("rw_tables"), 16)
            pool.dma_start(daw[0:64, :], A["rw_decay_up"]).then_inc(S("rw_tables"), 16)
            pool.dma_start(daw[64:128, :], A["rw_aaa_up"]).then_inc(S("rw_tables"), 16)
            pool.wait_ge(S("swa_done"), 4)
            pool.dma_start(dram_q, q_all).then_inc(S("y_spilled"), 16)
            for m in (Bh, Kh, Abd, AakT, Pm):
                pool.memset(m, 0.0).then_inc(S("rw_cleared"), 1)
            for p in range(2):
                pool.memset(small[:, 148 + p:149 + p], 0.0).then_inc(kv_spilled[p], 16)
            pool.wait_ge(S("rw_tables"), 48)
            pool.wait_ge(S("xs_ready"), 8 * FILL_MEM + 4)
            pool.memset(Yi, 0.0).then_inc(S("pool_cleared"), 1)
            pool.wait_ge(S("rkv_ready"), 12)
            pool.memset(Vbd, 0.0)
            pool.memset(Sbd, 0.0)
            pool.memset(Sc, 0.0).then_inc(S("pool_cleared"), 1)

            def masks(c):
                need(pool, c, "A_ready")
                pool.tensor_tensor(Xi, Araw, rc("pair").unsqueeze(1).to_broadcast([P, UN, P]), ALU.mult)\
                    .then_inc(S("X_pairs"), 1)
                need(pool, c, "X_pairs")
                pool.tensor_tensor(Xi, Xi, ident[:, :].unsqueeze(1).to_broadcast([P, UN, P]), ALU.add)
                for n in range(5):
                    if n:
                        pool.wait_ge(S("P_done"), c * 5 + n)
                    a = rwc["level"][0] + n * P
                    pool.tensor_tensor(Am, Araw, rwt[:, a:a + P].unsqueeze(1).to_broadcast([P, UN, P]), ALU.mult)\
                        .then_inc(S("Am"), 1)
            with pool.Fori(0, TC - 1) as c:
                masks(c)
            masks(TC - 1)
            pool.dma_start(y_swa, dram_q).then_inc(S("y_back"), 16)
            pool.wait_ge(S("P_done"), 5 * TC)
            pool.memset(gup[0:96, 1, :], 0.0).then_inc(S("pool_cleared"), 1)
            pool.dma_start(gup[:, 0, :], A["rw_gate_up"][0:128, :]).then_inc(S("gup_landed"), 16)
            pool.dma_start(gup[96:128, 1, :], A["rw_gate_up"][128:160, :]).then_inc(S("gup_landed"), 16)
            need(pool, TC - 1, "U_done")
            pool.dma_start(x[:, 0:8, :], dram_x[:, 0:8, :]).then_inc(S("x_back"), 16)
            need(pool, 3, "gate_done")
            pool.dma_start(x[:, 8:16, :], dram_x[:, 8:16, :]).then_inc(S("x_back"), 16)
            need(pool, 5, "y_split")
            for p in range(2):
                pool.wait_ge(kv_spilled[p], 16 * 9)

            def kv_piece(g):
                k, v = slice(2 * g, 2 * g + 2), slice(COLS * g, COLS * (g + 1))
                pool.dma_start(KX[:, k, :], dram_k[:, k, :]).then_inc(S("kv_back"), 16)
                pool.dma_start(VX[:, :, v], dram_v[:, :, v]).then_inc(S("kv_back"), 16)
            sum_squares(pool, XA, 8, kv_piece)
            sum_squares(pool, F2)

            def final_gain(blk):
                pool.wait_ge(S("sq_ready"), 8 * FINAL + blk + 1)
                xx, a = x[:, 2 * blk:2 * blk + 2, :], PCOL["final_norm"] + 2 * blk
                pool.tensor_tensor(xx, xx, par[:, a:a + 2].unsqueeze(2).to_broadcast([P, 2, T]), ALU.mult)\
                    .then_inc(S("x_gained"), 1)
            sum_squares(pool, FINAL, 7, final_gain)
            final_gain(7)
            pool.wait_ge(S("x_gained"), 8)
            pool.wait_ge(S("out_ready"), 1)
            pool.tensor_tensor(x[:, 12:16, :], x[:, 12:16, :], rstd[:, :].unsqueeze(1).to_broadcast([P, 4, T]),
                               ALU.mult).then_inc(S("last_out_ready"), 1)


        def rkv_chunk(eng, kind, i, j, n0=0):
            n = n0 + j // 4
            v, b = V_RKV + 4 * n0 + j, B_RKV + n
            if kind == "pe":
                chunk_products(eng, b, v - j % 4, j % 4, 4, xs, None, i, 8, 2)
            elif kind == "act":
                split_high(eng, v + LEAD, i, 8)
                if j % 4 == 3:
                    copy_low(eng, b, v, i, 8)
            else:
                split_low(eng, v + LEAD, i, 8)
                if j % 4 == 3:
                    add_low(eng, b, i, 2)
                    shift_in(eng)
                    for e in range(2):
                        k = i * 4 + 2 * n + e
                        m = eng.scalar_tensor_tensor(rkv[:, bass.ds(k, 1), :], up[:, e:e + 1, :], pc("mu", k),
                                                     shifted[:, e:e + 1, 1:257], ALU.mult, ALU.add)
                    m.then_inc(S("rkv_ready"), 1)

        def shift_in(dve):
            dve.tensor_tensor(shifted[:, :, 1:257], total[:, :, :], rb, ALU.mult).then_inc(S("dve_step"), 1)
            own(dve)
            dve.tensor_tensor(up[:, :, :], shifted[:, :, 0:256], shifted[:, :, 1:257], ALU.subtract)\
               .then_inc(S("dve_step"), 1)
            own(dve)

        def mem_chunk(eng, kind, c, m, j, tiles=range(KC)):
            v, b, by_token = V_MEM + 4 * m, B_MEM + m, mem_block(m, c)[0]
            odd_one = m % 2
            if kind == "pe":
                chunk_products(eng, b, v, j, 4, xs, filled(FILL_MEM) if m == 0 else None, c, 16, 4,
                               by_token=by_token, tiles=tiles)
            elif kind == "act":
                split_high(eng, v + j + LEAD, c, 16)
                if j == 3:
                    copy_low(eng, b, v + 3, c, 16)
            else:
                split_low(eng, v + j + LEAD, c, 16)
                if j == 3:
                    add_low(eng, b, c, 4)
                    eng.wait_ge(kv_spilled[odd_one], c * 32 + 16 * (m // 2 + 1))
                    by = rcol[:, :].unsqueeze(2).to_broadcast([P, 2, T]) if by_token else rb
                    eng.tensor_tensor((gate, up)[odd_one][:, :, :], total[:, :, :], by, ALU.mult)\
                       .then_inc(S("kv_out"), 1)

        def mem_store(act, c, m):
            by_token, col = mem_block(m, c)
            act.wait_ge(S("kv_out"), c * 4 + m + 1)
            if by_token:
                dst = dram_v[:, :, bass.ds((col - 8) * COLS, COLS)]
            else:
                dst = dram_k[:, bass.ds(col * 2, 2), :]
            act.dma_start(dst, (gate, up)[m % 2][:, :, :]).then_inc(kv_spilled[m % 2], 16)

        XSCALE = float(D // 4) ** -0.5
        xmax, xneg, xsum, xrec = (small[:, 112 + 4 * n:116 + 4 * n] for n in range(4))

        mx, negm, es, sums, rden = (small[:, 72 + 8 * n:80 + 8 * n] for n in range(5))

        def halves(eng, dst, src, name, mask=None, scale=None):
            for h in range(2):
                rows, co = slice(h * HD, h * HD + HD), slice(h * L, h * L + L)
                if mask is not None:
                    m = eng.tensor_tensor(dst[rows, :, co], src[rows, :, :],
                                          mask[rows, :].unsqueeze(1).to_broadcast([HD, UN, L]), ALU.mult)
                elif scale is not None:
                    m = eng.tensor_tensor(dst[rows, :, co], src[rows, :, :], scale[rows, :, :], ALU.mult)
                elif eng is nc.scalar:
                    m = eng.activation(dst[rows, :, co], src[rows, :, :], ACT.Copy)
                else:
                    m = eng.tensor_copy(dst[rows, :, co], src[rows, :, :])
            if name:
                m.then_inc(S(name), 1)

        def bcast(table):
            return table.unsqueeze(1).to_broadcast([P, UN, L])

        def odd(m, b, e):
            return m.rearrange("p (n two b) -> p n two b", two=2, b=b)[:, :, e, :]

        @block.scalar
        def _(act):
            act.dma_start(par[:, :], A["params"]).then_inc(S("par_landed"), 16)
            need(act, 0, "ones_ready")
            act.activation(small[:, 150:151], ones[:, 0:1], ACT.Square)
            xin = A["x_t"].rearrange("(t p) n -> p t n", p=P)
            for g in range(4):
                act.dma_start(x[:, 4 * g:4 * g + 4, :], xin[:, 4 * g:4 * g + 4, :]).then_inc(S(f"x_landed{g}"), 16)
            act.dma_start(ident[:, :], A["ident"]).then_inc(S("ident_landed"), 16)
            act.wait_ge(S("par_landed"), 16)
            for g in range(4):
                act.wait_ge(S(f"x_landed{g}"), 16)
                fill_act(act, X1, "f1_norm", 2 * g, x, FILL_X)
                fill_act(act, X1, "f1_norm", 2 * g + 1, x, FILL_X)
                split_high(act, V_UP1 + g)
            ahead(split_high, act, V_UP1 + 1, 3)
            ffn_act(act, 0, B_UP1, V_UP1, V_DOWN1, X1)
            with act.Fori(0, 4) as i:
                for u in range(2):
                    ahead(split_high, act, V_DOWN1 + 12 * u, 12, i, 24)
                    resid_act(act, 0, B_DOWN1 + u, V_DOWN1 + 12 * u + 10, 2 * i + u, MIX, "mix_norm", FILL_MIX, i, 24)
            ahead(split_high, act, V_Q, 4)
            norm_act(act, MIX)
            copy_low(act, B_Q, V_Q + 3)
            for b in range(1, 4):
                ahead(split_high, act, V_Q + 4 * b, 4)
                copy_low(act, B_Q + b, V_Q + 4 * b + 3)
            ahead(split_high, act, V_KV, 4)
            copy_low(act, B_KV, V_KV + 3)
            ahead(split_high, act, V_LORA, 4)
            copy_low(act, B_LORA, V_LORA + 3)
            need(act, 0, "v_turned", "vpad_cleared")
            for g in range(2):
                vp = vpad[:, g, :].rearrange("p (b e n) -> p b e n", b=2, e=2)
                for e in range(2):
                    m = act.activation(vp[:, :, e, e * HD:(e + 1) * HD],
                                       bank[1].rearrange("p (b n) -> p b n", n=P)[:, 0:2, g * HD:(g + 1) * HD],
                                       ACT.Copy)
            m.then_inc(S("vpad_ready"), 1)
            need(act, 0, "k_selected")
            act.activation(kpad, mid[:, 2:4, :].rearrange("p b (u t) -> p (b u) t", t=T), ACT.Copy)\
               .then_inc(S("kpad_ready"), 1)
            ahead(split_high, act, V_TAIL, 4)
            copy_low(act, B_TAIL, V_TAIL + 1)
            need(act, 1, "lora_ready")
            act.activation(lora[0:64, 0, :], lora[0:64, 0, :], ACT.Tanh)
            act.activation(lora[:, 1:3, :], lora[:, 1:3, :], ACT.Sigmoid).then_inc(S("lora_act"), 1)
            act.wait_ge(S("mem_landed"), 64)
            with act.Fori(0, 4) as i:
                for j in range(2):
                    rkv_chunk(act, "act", i, j)
                square(act, MEM, i * 2, x)
                rkv_chunk(act, "act", i, 2)
                need(act, i, "sinks_less_max")
                act.activation(es, es, ACT.Exp).then_inc(S("sink_exp"), 1)
                for h in range(4):
                    act.activation(sc[:, h, 0:128], sc[:, h, 0:128], ACT.Exp, bias=negm[:, h:h + 1],
                                   accum_out=sums[:, h:h + 1])
                    m = act.activation(sc[:, h, 128:384], sc[:, h, 128:384], ACT.Exp, bias=negm[:, 4 + h:5 + h],
                                       accum_out=sums[:, 4 + h:5 + h])
                m.then_inc(S("swa_exp"), 1)
                for j in range(3, 6):
                    rkv_chunk(act, "act", i, j)
                square(act, MEM, i * 2 + 1, x)
                need(act, i, "probs_turned")
                act.activation(pt, mid[:, 0:3, :].rearrange("p b (u t) -> p (b u) t", t=P), ACT.Copy)\
                   .then_inc(S("pt_ready"), 1)
                for j in range(6, 8):
                    rkv_chunk(act, "act", i, j)

            def prepare(n, step):
                if step == 0:
                    ts = bass.ds(n * L, L)
                    if not isinstance(n, int):
                        plain(act)
                    act.activation(tzc, lora[:, 0, ts], ACT.Copy).then_inc(S("tz_copied"), 1)
                    need(act, n, "kk_raw")
                    act.activation(t2, kk, ACT.Square).then_inc(S("kk_sq"), 1)
                if step == 1:
                    need(act, n, "z_decay")
                    act.activation(t1, t1, ACT.Sigmoid).then_inc(S("decay_sig"), 1)
                    need(act, n, "z_a")
                    act.activation(aa, aa, ACT.Sigmoid).then_inc(S("a_ready"), 1)
                    need(act, n, "kk_sum")
                    act.activation(t2, b8[0], ACT.Sqrt).then_inc(S("kk_norm"), 1)
                if step == 2:
                    need(act, n, "cum_ready")
                    act.activation(Wx[:, :, 1:65], cum, ACT.Exp, scale=-DECAY)
                    act.activation(Winv, cum, ACT.Exp, scale=DECAY).then_inc(S("W_ready"), 1)

            def turn(n, *parts):
                for part in parts:
                    dst, src = ((Araw, two[0]), (Bh, two[1]), (Kh, two[0]), (Vc, b8[2]))[part]
                    need(act, n, ("A_prod", "B_turned", "K_turned", "V_turned")[part])
                    act.activation(dst, src, ACT.Copy).then_inc(S(("A_ready", "BT_ready", "KT_ready", "Vc_ready")[part]), 1)

            def scaled_blocks(n, *parts):
                ts = bass.ds(n * L, L)
                if 0 in parts:
                    need(act, n, "a_scaled")
                    halves(act, Abd, rhs[:, :, 0:64], None)
                if 1 in parts:
                    halves(act, Pm, rkv[:, 16:24, ts], "Abd_ready")

            def solve(c, more):
                for n in range(5):
                    act.wait_ge(S("P_done"), c * 5 + n + 1)
                    act.activation(Pm, two[0], ACT.Copy).then_inc(S("P_ready"), 1)
                    if more and n < 3:
                        prepare(c + 1, n)
                    mem(c, n)

            def mem(c, *js):
                for j in js:
                    if isinstance(c, int) and j >= 12:
                        continue
                    mem_chunk(act, "act", c, 1 + j // 4, j % 4)
                    if j % 4 == 1:
                        mem_store(act, c, j // 4)
            def values(*js):
                for j in js:
                    rkv_chunk(act, "act", 0, j, 8)

            def mem_split(g):
                last = V_RKV + 44 + g
                act.wait_ge(parts_used[last % RING], W.uses(last))
                for e in range(2):
                    fill_act(act, MEM, "mem_norm", 2 * g + e, x, FILL_MEM)
            values(0, 1)
            act.wait_ge(S("rw_tables"), 48)
            act.wait_ge(S("y_spilled"), 16)
            values(2)
            prepare(0, 0)
            values(3, 4)
            prepare(0, 1)
            values(5)
            prepare(0, 2)
            values(6, 7)
            act.wait_ge(S("rw_cleared"), 5)
            scaled_blocks(0, 0)
            values(8, 9, 10, 11, 12)
            for g in range(3):
                mem_split(g)
                values(13 + g)
            mem_split(3)
            mem_chunk(act, "act", 0, 0, 0)
            act.wait_ge(S("rkv_ready"), 12)
            scaled_blocks(0, 1)
            norm_act(act, MEM)
            mem_chunk(act, "act", 0, 0, 1)
            turn(0, 0)
            mem_chunk(act, "act", 0, 0, 2)
            turn(0, 1, 2)
            mem_chunk(act, "act", 0, 0, 3)
            turn(0, 3)

            def round_(c, more):
                solve(c, more)
                need(act, c, "R_done")
                act.activation(Rc, b8[0], ACT.Copy).then_inc(S("R_ready"), 1)
                mem(c, 5)
                need(act, c, "U_done")
                act.activation(Uc, b8[1], ACT.Copy).then_inc(S("U_ready"), 1)
                mem(c, 6)
                need(act, c, "y_done")
                act.activation(cum, b8[2], ACT.Copy).then_inc(S("y_copied"), 1)
                mem(c, 7)
                need(act, c, "S_new")
                halves(act, Sbd, Sc, None)
                need(act, c, "y_centred")
                act.activation(t2, t1, ACT.Square).then_inc(S("y_sq"), 1)
                mem(c, 8)
                need(act, c, "y_var")
                act.activation(t2, t2, ACT.Sqrt).then_inc(S("y_root"), 1)
                if more:
                    scaled_blocks(c + 1, 0, 1)
                    mem(c, 9, 10)
                    for part in range(4):
                        turn(c + 1, part)
                        mem(c, 11 + part)
                    mem(c, 15)
                else:
                    mem(c, 9, 10)
            with act.Fori(0, TC - 1) as c:
                round_(c, True)
            round_(TC - 1, False)
            act.wait_ge(S("y_back"), 16)
            for g in range(2):
                act.activation(hs[:, YT0 + 8 + 4 * g:YT0 + 12 + 4 * g, 0, :], y_swa[:, 4 * g:4 * g + 4, :], ACT.Copy)\
                   .then_inc(S("y_high"), 1)
            mem(TC - 1, 11)
            for g in range(4):
                act.wait_ge(S("y_gated"), g + 1)
                act.activation(hs[:, YT0 + 2 * g:YT0 + 2 * g + 2, 0, :], rkv[:, 2 * g:2 * g + 2, :], ACT.Copy)\
                   .then_inc(S("y_high"), 1)
            mem_store(act, TC - 1, 3)
            with act.Fori(0, 4) as i:
                for u in range(2):
                    ahead(split_high, act, V_OUT + 4 * u, 4, i, 8)
                    resid_act(act, 1, B_OUT + u, V_OUT + 4 * u + 3, 2 * i + u, XA, "xa_norm", FILL_XA, i, 8)
            ahead(split_high, act, V_XQ, 4)
            norm_act(act, XA)
            copy_low(act, B_XQ, V_XQ + 3)
            with act.Fori(0, 3) as i:
                for u in range(1, 3):
                    ahead(split_high, act, V_XQ + 4 * u, 4, i, 8)
                    copy_low(act, B_XQ + u, V_XQ + 4 * u + 3, i, 8)
            ahead(split_high, act, V_XQ + 28, 4)
            copy_low(act, B_XQ + 7, V_XQ + 31)

            def x_exp(h):
                act.wait_ge(S("x_negmax"), h + 1)
                for q in range(2):
                    k = 2 * (h % 2) + q
                    m = act.activation(SX[:, k, :], b2[h % 2][:, q, :], ACT.Exp, scale=XSCALE,
                                       bias=xneg[:, k:k + 1], accum_out=xsum[:, k:k + 1])
                m.then_inc(S("x_exp"), 1)

            def x_out(h):
                act.wait_ge(S("x_turned"), h + 1)
                act.activation(PX[:, 2 * (h % 2):2 * (h % 2) + 2, :], b2[2], ACT.Copy).then_inc(S("x_probs"), 1)
                for g in range(2):
                    act.wait_ge(S("o_done"), 2 * h + g + 1)
                    a = YT0 + 4 * h + 2 * g
                    act.activation(hs[:, a:a + 2, 0, :], b2[3 - g], ACT.Copy).then_inc(S("o_high"), 1)
            x_exp(0)
            for h in range(4):
                if h < 3:
                    x_exp(h + 1)
                x_out(h)
            with act.Fori(0, 4) as i:
                for u in range(2):
                    ahead(split_high, act, V_XO + 4 * u, 4, i, 8)
                    resid_act(act, 2, B_XO + u, V_XO + 4 * u + 3, 2 * i + u, F2, "f2_norm", FILL_F2, i, 8)
            ahead(split_high, act, V_UP2, 4)
            ffn_act(act, 1, B_UP2, V_UP2, V_DOWN2, F2)
            with act.Fori(0, 3) as i:
                for u in range(2):
                    ahead(split_high, act, V_DOWN2 + 12 * u, 12, i, 24)
                    resid_act(act, 3, B_DOWN2 + u, V_DOWN2 + 12 * u + 10, 2 * i + u, FINAL, None, None, i, 24)
            for u in range(6, 8):
                ahead(split_high, act, V_DOWN2 + 12 * u, 12)
                if u == 7:
                    act.activation(small[:, 150:151], ones[:, 0:1], ACT.Sqrt)
                resid_act(act, 3, B_DOWN2 + u, V_DOWN2 + 12 * u + 10, u, FINAL, None, None)
            norm_act(act, FINAL)

        @block.vector
        def _(dve):
            dve.wait_ge(S("par_landed"), 16)
            for b in range(8):
                dve.wait_ge(S(f"x_landed{b // 2}"), 16)
                fill_dve(dve, "f1_norm", b, x, FILL_X)
                if b % 2:
                    split_low(dve, V_UP1 + b // 2)
            ahead(split_low, dve, V_UP1 + 1, 3)
            ffn_dve(dve, 0, B_UP1, V_UP1, V_DOWN1, X1)
            with dve.Fori(0, 4) as i:
                for u in range(2):
                    ahead(split_low, dve, V_DOWN1 + 12 * u, 12, i, 24)
                    resid_dve(dve, 0, B_DOWN1 + u, 2 * i + u, "mix_norm", FILL_MIX, 0.5, None, i, 2)
            ahead(split_low, dve, V_Q, 4)
            norm_dve(dve, MIX)

            def scaled(b, dst, bias, k, name):
                add_low(dve, b)
                dve.tensor_tensor(dst, total[:, :, :], rb, ALU.mult).then_inc(S("dve_step"), 1)
                own(dve)
                a = PCOL[bias] + k
                dve.tensor_tensor(dst, dst, par[:, a:a + 2].unsqueeze(2).to_broadcast([P, 2, T]), ALU.add)\
                   .then_inc(S(name), 1)
            scaled(B_Q, q_all[:, 0:2, :], "b_q", 0, "q_in")
            for b in range(1, 4):
                ahead(split_low, dve, V_Q + 4 * b, 4)
                scaled(B_Q + b, q_all[:, 2 * b:2 * b + 2, :], "b_q", 2 * b, "q_in")
            ahead(split_low, dve, V_KV, 4)
            scaled(B_KV, k_v, "b_kv", 0, "kv_in")
            ahead(split_low, dve, V_LORA, 4)
            dve.wait_ge(S("swa_tables"), 16)
            need(dve, 0, "k_swapped", "kv_in")
            dve.tensor_tensor(ktmp, bank[0][:, 0:T], sc_("sin"), ALU.mult)
            dve.tensor_tensor(krot, k_v[:, 0, :], sc_("cos"), ALU.mult).then_inc(S("dve_step"), 1)
            own(dve)
            dve.tensor_tensor(krot, krot, ktmp, ALU.add).then_inc(S("k_rotated"), 1)

            def lora_part(b, dst, ntiles, mu):
                add_low(dve, b)
                need(dve, 0, "shift_cleared")
                shift_in(dve)
                for e in range(ntiles):
                    m = dve.scalar_tensor_tensor(dst[:, e, :], up[:, e, :], pc(mu, e), shifted[:, e, 1:257],
                                                 ALU.mult, ALU.add)
                m.then_inc(S("lora_ready"), 1)
            lora_part(B_LORA, lora[:, 0:2, :], 2, "mu_lora")
            ahead(split_low, dve, V_TAIL, 4)
            lora_part(B_TAIL, lora[:, 2:3, :], 1, "mu_tail")
            need(dve, 0, "vpad_ready")
            with dve.Fori(0, 4) as i:
                own.rounds(i, 11)
                qi = q_all[:, bass.ds(i * 2, 2), :]

                def rkvs(*js):
                    for j in js:
                        rkv_chunk(dve, "dve", i, j)
                cosb = sc_("cos").unsqueeze(1).to_broadcast([P, 2, T])
                sinb = sc_("sin").unsqueeze(1).to_broadcast([P, 2, T])
                need(dve, i, "q_swapped")
                dve.tensor_tensor(qtmp, b2[0], sinb, ALU.mult)
                dve.tensor_tensor(qg, qi, cosb, ALU.mult).then_inc(S("dve_step"), 1)
                own(dve)
                dve.tensor_tensor(qg, qg, qtmp, ALU.add).then_inc(S("q_rotated"), 1)
                dve.tensor_scalar(vg, vpad[:, bass.ds(i // 2, 1), :].rearrange("p a (b n) -> p (a b) n", n=P), 1.0, None,
                                  ALU.mult)\
                   .then_inc(S("vg_ready"), 1)
                rkvs(0, 1)
                for h in range(4):
                    dve.wait_ge(S("swa_scores"), i * 4 + h + 1)
                    m = dve.scalar_tensor_tensor(sc[:, h, :], bank[h][:, 0:384], HD ** -0.5, sc_("band"),
                                                 ALU.mult, ALU.add)
                m.then_inc(S("dve_step"), 1)
                own(dve)
                dve.reduce_max(mx[:, 0:4], sc[:, :, 0:128], AX_X)
                dve.reduce_max(mx[:, 4:8], sc[:, :, 128:384], AX_X).then_inc(S("dve_step"), 1)
                own(dve)
                sink = par[:, bass.ds(i * 4 + PCOL["sinks"], 4)].unsqueeze(1).to_broadcast([P, 2, 4])

                def pair4(s):
                    return s.rearrange("p (a b) -> p a b", b=4)
                dve.tensor_tensor(pair4(mx), pair4(mx), sink, ALU.max).then_inc(S("dve_step"), 1)
                own(dve)
                dve.tensor_scalar(negm, mx, -1.0, None, ALU.mult).then_inc(S("dve_step"), 1)
                own(dve)
                dve.tensor_tensor(pair4(es), sink, pair4(negm), ALU.add).then_inc(S("sinks_less_max"), 1)
                rkvs(2)
                need(dve, i, "sink_exp", "swa_exp")
                dve.tensor_tensor(sums, sums, es, ALU.add).then_inc(S("dve_step"), 1)
                own(dve)
                dve.reciprocal(rden, sums).then_inc(S("dve_step"), 1)
                own(dve)
                dve.tensor_tensor(sc[:, :, 0:128], sc[:, :, 0:128], rden[:, 0:4].unsqueeze(2).to_broadcast([P, 4, 128]),
                                  ALU.mult)
                dve.tensor_tensor(sc[:, :, 128:384], sc[:, :, 128:384],
                                  rden[:, 4:8].unsqueeze(2).to_broadcast([P, 4, 256]), ALU.mult)\
                   .then_inc(S("swa_probs"), 1)
                rkvs(3, 4, 5, 6)
                need(dve, i, "swa_out")
                dve.tensor_scalar(qi, b2[3], 1.0, None, ALU.mult).then_inc(S("swa_done"), 1)
                rkvs(7)
            own.end(4)
            def mem(c, *js):
                for j in js:
                    if not (isinstance(c, int) and j >= 12):
                        mem_chunk(dve, "dve", c, 1 + j // 4, j % 4)

            def prepare(n, step):
                ts = bass.ds(n * L, L)
                kv_ = rkv[:, 8:16, ts]
                if step == 0:
                    dve.tensor_tensor(kk, kv_, per_unit("k_k"), ALU.mult).then_inc(S("kk_raw"), 1)
                    need(dve, n, "lora_z")
                    dve.tensor_tensor(t1, b8[0], per_unit("w0"), ALU.add).then_inc(S("z_decay"), 1)
                    dve.tensor_tensor(aa, b8[1], per_unit("a0"), ALU.add).then_inc(S("z_a"), 1)
                if step == 1:
                    need(dve, n, "decay_sig")
                    for u in range(UN):
                        m = dve.tensor_tensor_scan(cum[:, u, :], t1[:, u, :], t1[:, u, :], 0.0, ALU.add, ALU.max)
                    m.then_inc(S("cum_ready"), 1)
                if step == 2:
                    need(dve, n, "kk_norm")
                    dve.tensor_scalar(t2, t2, 1e-12, None, ALU.max).then_inc(S("dve_step"), 1)
                    own(dve)
                    dve.reciprocal(t2, t2).then_inc(S("dve_step"), 1)
                    own(dve)
                if step == 3:
                    dve.tensor_tensor(kk, kk, t2, ALU.mult)
                    need(dve, n, "a_ready")
                    dve.scalar_tensor_tensor(t1, aa, -1.0, per_unit("k_a"), ALU.add, ALU.mult)\
                       .then_inc(S("dve_step"), 1)
                    own(dve)
                    dve.scalar_tensor_tensor(kv_, t1, 1.0, kv_, ALU.add, ALU.mult).then_inc(S("dve_step"), 1)
                    own(dve)
                if step == 4:
                    dve.tensor_tensor(aa, kk, aa, ALU.mult).then_inc(S("dve_step"), 1)
                    own(dve)

            def scale_a(n):
                ts = bass.ds(n * L, L)
                need(dve, n, "W_ready")
                dve.scalar_tensor_tensor(rhs[:, :, 0:64], kk, -1.0, Wx[:, :, 0:64], ALU.mult, ALU.mult)\
                   .then_inc(S("a_scaled"), 1)
                dve.tensor_tensor(rhs[:, :, 64:128], rkv[:, 0:8, ts], Wx[:, :, 1:65], ALU.mult)
                dve.tensor_copy(WL, Wx[:, :, 64])

            def scale_b(n):
                ts = bass.ds(n * L, L)
                halves(dve, Bh, aa, "B_scaled", scale=Winv)
                halves(dve, Kh, rkv[:, 8:16, ts], "K_scaled", scale=Winv)

            def take_b(n):
                need(dve, n, "B_prod")
                halves(dve, Yi, two[0][:, :, 0:64], "dve_step", mask=rc("pair_t"))
                dve.tensor_tensor(ArbT, two[0][:, :, 64:128], bcast(rc("upto_t")), ALU.mult)\
                   .then_inc(S("Arb_ready"), 1)
                own(dve)
                dve.tensor_tensor(Yi, Yi, ident[:, :].unsqueeze(1).to_broadcast([P, UN, P]), ALU.add)\
                   .then_inc(S("Y_init"), 1)

            def take_k(n):
                need(dve, n, "K_prod")
                halves(dve, AakT, two[1][:, :, 0:64], None, mask=rc("before_t"))
                dve.tensor_tensor(ArkT, two[1][:, :, 64:128], bcast(rc("upto_t")), ALU.mult)\
                   .then_inc(S("Ark_ready"), 1)

            def take_v(n):
                need(dve, n, "Vc_ready")
                halves(dve, Vbd, Vc, None)

            def solve(c, more):
                for n, b in enumerate(LEVELS):
                    dve.wait_ge(S("Y_more"), c * 5 + n + 1)
                    yo = Yi.rearrange("p u (n two b) -> p (u n) two b", two=2, b=b)[:, :, 1, :]
                    dve.tensor_tensor(yo, yo, bank[2].rearrange("p (n b) -> p n b", b=b), ALU.add)\
                       .then_inc(S("Y_level"), 1)
                    if n < 4:
                        dve.wait_ge(S("X_more"), c * 4 + n + 1)
                        xo = Xi.rearrange("p u (n two b) -> p (u n) two b", two=2, b=b)[:, :, 0, :]
                        dve.tensor_tensor(xo, xo, bank[3].rearrange("p (n b) -> p n b", b=b), ALU.add)\
                           .then_inc(S("X_level"), 1)
                    if more:
                        prepare(c + 1, n)
                    mem(c, n)

            def round_(c, more):
                ts = bass.ds(c * L, L)
                rv, kv_, vv = rkv[:, 0:8, ts], rkv[:, 8:16, ts], rkv[:, 16:24, ts]
                solve(c, more)
                mem(c, 5)
                need(dve, c, "U_ready")
                halves(dve, Ubd, Uc, "Ubd_ready")
                dve.tensor_tensor(Rc, rv, kv_, ALU.mult).then_inc(S("dve_step"), 1)
                own(dve)
                dve.tensor_tensor(Rc, Rc, per_unit("r_k"), ALU.mult).then_inc(S("rkr"), 1)
                mem(c, 6)
                need(dve, c, "S_done")
                dve.tensor_tensor(Sc, Sc, b8[3], ALU.add).then_inc(S("S_sum"), 1)
                need(dve, c, "S_sum")
                dve.tensor_tensor(Sc, Sc, WL.unsqueeze(2).to_broadcast([P, UN, L]), ALU.mult).then_inc(S("S_new"), 1)
                mem(c, 7)
                need(dve, c, "y_sum", "y_copied")
                dve.scalar_tensor_tensor(t1, b8[0], -1.0 / HD, cum, ALU.mult, ALU.add).then_inc(S("y_centred"), 1)
                if more:
                    scale_a(c + 1)
                mem(c, 8)
                need(dve, c, "y_sqsum")
                dve.tensor_scalar(t2, b8[1], 1.0 / HD, GN_EPS, ALU.mult, ALU.add).then_inc(S("y_var"), 1)
                need(dve, c, "bonus_sum")
                dve.tensor_tensor(Rc, b8[3], vv, ALU.mult).then_inc(S("bonus"), 1)
                if more:
                    scale_b(c + 1)
                    mem(c, 9)
                    take_b(c + 1)
                    mem(c, 10)
                    take_k(c + 1)
                    mem(c, 11, 12)
                else:
                    mem(c, 9)
                need(dve, c, "y_root")
                dve.reciprocal(t2, t2).then_inc(S("dve_step"), 1)
                own(dve)
                if more:
                    mem(c, 13)
                dve.tensor_tensor(t1, t1, t2, ALU.mult).then_inc(S("dve_step"), 1)
                own(dve)
                dve.tensor_tensor(t1, t1, per_unit("lnx_w"), ALU.mult).then_inc(S("dve_step"), 1)
                own(dve)
                if more:
                    take_v(c + 1)
                    mem(c, 14)
                dve.tensor_tensor(t1, t1, per_unit("lnx_b"), ALU.add).then_inc(S("dve_step"), 1)
                own(dve)
                dve.tensor_tensor(rv, t1, Rc, ALU.add).then_inc(S("chunk_done"), 1)
                if more:
                    mem(c, 15)
                else:
                    mem(c, 10)
                need(dve, c, "chunk_done")
            def values(*js):
                for j in js:
                    rkv_chunk(dve, "dve", 0, j, 8)

            def mem_split(g):
                for e in range(2):
                    fill_dve(dve, "mem_norm", 2 * g + e, x, FILL_MEM)
            values(0, 1, 2)
            dve.wait_ge(S("rkv_ready"), 8)
            dve.wait_ge(S("rw_tables"), 48)
            prepare(0, 0)
            values(3, 4)
            dve.memset(Wx[:, :, 0:1], 1.0).then_inc(S("rw_cleared"), 1)
            prepare(0, 1)
            values(5)
            prepare(0, 2)
            values(6)
            prepare(0, 3)
            dve.wait_ge(S("rw_cleared"), 6)
            scale_a(0)
            prepare(0, 4)
            values(7)
            scale_b(0)
            values(8, 9, 10, 11)
            take_k(0)
            values(12)
            mem_split(0)
            values(13)
            mem_split(1)
            values(14)
            mem_split(2)
            need(dve, 0, "pool_cleared")
            take_b(0)
            values(15)
            mem_split(3)
            norm_dve(dve, MEM)
            for j in range(4):
                mem_chunk(dve, "dve", 0, 0, j)
            need(dve, 1, "pool_cleared")
            take_v(0)
            with dve.Fori(0, TC - 1) as c:
                own.rounds(c, 11)
                round_(c, True)
            own.end(TC - 1)
            round_(TC - 1, False)
            for g in range(4):
                need(dve, g, "gate_done")
                dve.tensor_tensor(rkv[:, 2 * g:2 * g + 2, :], rkv[:, 2 * g:2 * g + 2, :], b2[g], ALU.mult)\
                   .then_inc(S("y_gated"), 1)
            for g in range(2):
                need(dve, g, "y_high")
                t = slice(YT0 + 8 + 4 * g, YT0 + 12 + 4 * g)
                dve.tensor_tensor(hs[:, t, 1, :], y_swa[:, 4 * g:4 * g + 4, :], hs[:, t, 0, :].bitcast(F32),
                                  ALU.subtract).then_inc(S("y_split"), 1)
            mem(TC - 1, 11)
            for g in range(4):
                need(dve, 2 + g, "y_high")
                t = slice(YT0 + 2 * g, YT0 + 2 * g + 2)
                dve.tensor_tensor(hs[:, t, 1, :], rkv[:, 2 * g:2 * g + 2, :], hs[:, t, 0, :].bitcast(F32),
                                  ALU.subtract).then_inc(S("y_split"), 1)
            dve.wait_ge(S("x_back"), 32)
            with dve.Fori(0, 4) as i:
                for u in range(2):
                    ahead(split_low, dve, V_OUT + 4 * u, 4, i, 8)
                    resid_dve(dve, 1, B_OUT + u, 2 * i + u, "xa_norm", FILL_XA, 1.0, "b_out", i, 2)
            ahead(split_low, dve, V_XQ, 4)
            norm_dve(dve, XA)

            def x_query(b, blk, i=0):
                add_low(dve, b, i, 2)
                dve.tensor_tensor(QX[:, bass.ds(2 * blk, 2), :], total[:, :, :], rb, ALU.mult).then_inc(S("xq_ready"), 1)
            x_query(B_XQ, 0)
            with dve.Fori(0, 3) as i:
                for u in range(1, 3):
                    ahead(split_low, dve, V_XQ + 4 * u, 4, i, 8)
                    x_query(B_XQ + u, 2 * i + u, i)
            ahead(split_low, dve, V_XQ + 28, 4)
            x_query(B_XQ + 7, 7)

            def x_max(h):
                k = 2 * (h % 2)
                dve.wait_ge(S("x_scores"), h + 1)
                dve.reduce_max(xmax[:, k:k + 2], b2[h % 2], AX_X).then_inc(S("dve_step"), 1)
                own(dve)
                dve.tensor_scalar(xneg[:, k:k + 2], xmax[:, k:k + 2], -XSCALE, None, ALU.mult)\
                   .then_inc(S("x_negmax"), 1)

            def x_norm(h):
                k = 2 * (h % 2)
                dve.wait_ge(S("x_exp"), h + 1)
                dve.reciprocal(xrec[:, k:k + 2], xsum[:, k:k + 2]).then_inc(S("dve_step"), 1)
                own(dve)
                dve.tensor_tensor(SX[:, k:k + 2, :], SX[:, k:k + 2, :],
                                  xrec[:, k:k + 2].unsqueeze(2).to_broadcast([P, 2, T]), ALU.mult)\
                   .then_inc(S("x_normed"), 1)

            def x_out(h):
                for g in range(2):
                    need(dve, 2 * h + g, "o_high")
                    a = YT0 + 4 * h + 2 * g
                    dve.tensor_tensor(hs[:, a:a + 2, 1, :], b2[3 - g], hs[:, a:a + 2, 0, :].bitcast(F32),
                                      ALU.subtract).then_inc(S("o_split"), 1)
            x_max(0)
            x_norm(0)
            for h in range(4):
                if h < 3:
                    x_max(h + 1)
                    x_norm(h + 1)
                x_out(h)
            with dve.Fori(0, 4) as i:
                for u in range(2):
                    ahead(split_low, dve, V_XO + 4 * u, 4, i, 8)
                    resid_dve(dve, 2, B_XO + u, 2 * i + u, "f2_norm", FILL_F2, 1.0, None, i, 2)
            ahead(split_low, dve, V_UP2, 4)
            ffn_dve(dve, 1, B_UP2, V_UP2, V_DOWN2, F2)
            with dve.Fori(0, 3) as i:
                for u in range(2):
                    ahead(split_low, dve, V_DOWN2 + 12 * u, 12, i, 24)
                    resid_dve(dve, 3, B_DOWN2 + u, 2 * i + u, None, None, 0.5, None, i, 2)
            for u in range(6, 8):
                ahead(split_low, dve, V_DOWN2 + 12 * u, 12)
                resid_dve(dve, 3, B_DOWN2 + u, u, None, None, 0.5)
            norm_dve(dve, FINAL)
            dve.wait_ge(S("x_gained"), 6)
            for g in range(3):
                dve.tensor_tensor(x[:, 4 * g:4 * g + 4, :], x[:, 4 * g:4 * g + 4, :],
                                  rstd[:, :].unsqueeze(1).to_broadcast([P, 4, T]), ALU.mult).then_inc(S("out_ready"), 1)

        @block.tensor
        def _(pe):
            need(pe, 0, "ones_ready")
            ffn_pe(pe, 0, B_UP1, V_UP1, V_DOWN1, X1, FILL_X)
            pe.wait_ge(S("ident_landed"), 16)
            with pe.Fori(0, 4) as i:
                for u in range(2):
                    products(pe, B_DOWN1 + u, V_DOWN1 + 12 * u, 11, hs, hidden(0), i, 24, 2)
            products(pe, B_Q, V_Q, 4, xs, filled(FILL_MIX))
            norm_pe(pe, MIX)
            for b in range(1, 4):
                products(pe, B_Q + b, V_Q + 4 * b, 4, xs)
            products(pe, B_KV, V_KV, 4, xs)
            products(pe, B_LORA, V_LORA, 4, xs)
            pe.wait_ge(S("swa_tables"), 16)
            need(pe, 0, "kv_in")
            pe.matmul(bank[0][:, 0:T], sc_("swap"), k_v[:, 0, :], start=True, stop=True).then_inc(S("k_swapped"), 1)
            for e in range(2):
                m = pe.transpose(bank[1][:, e * P:(e + 1) * P], k_v[:, 1, e * P:(e + 1) * P], ident[:, :])
            m.then_inc(S("v_turned"), 1)
            for t in range(KT):
                if t == 0:
                    pe.wait_ge(bank_free[0], 1 + B.before(B_TAIL))
                if t % 8 == 0:
                    pe.wait_ge(low_ready[(V_TAIL + t // 8) % RING], W.uses(V_TAIL + t // 8))
                s, a, c0 = (V_TAIL + t // 8) % RING, t % 8 // 2, t % 2 * P
                pe.matmul(acc[0][:, 0, :, :], parts[:, s, a, 0, c0:c0 + P], xs[:, t, :, :],
                          start=t == 0, stop=False, skip_group_check=True)
                m = pe.matmul(acc[0][:, 0, 1, :], parts[:, s, a, 1, c0:c0 + P], xs[:, t, 0, :],
                              start=False, stop=t == KT - 1, skip_group_check=True)
                if t % 8 == 7:
                    m.then_inc(parts_used[s], 1)
            need(pe, 0, "k_rotated")
            for n in range(4):
                m = pe.matmul(b2[2 + n // 2][:, n % 2, :], sc_("select")[:, n * P:(n + 1) * P], krot,
                              start=True, stop=True)
            m.then_inc(S("k_selected"), 1)
            need(pe, 3, "q_in")
            need(pe, 0, "kpad_ready")
            need(pe, 0, "vpad_ready")
            with pe.Fori(0, 4) as i:
                def rkvs(*js):
                    for j in js:
                        rkv_chunk(pe, "pe", i, j)
                pe.matmul(bank[0], sc_("swap"), q_all[:, bass.ds(i * 2, 2), :], start=True, stop=True)\
                  .then_inc(S("q_swapped"), 1)
                rkvs(0, 1)
                need(pe, i, "q_rotated")
                for h in range(4):
                    kp = kpad[:, bass.ds(i // 2 * 2 + h % 2, 1), :]
                    pe.matmul(bank[h][:, 0:128], qg[:, h // 2, 0:128], kp[:, :, 0:128], start=True, stop=True)
                    pe.matmul(bank[h][:, 128:384], qg[:, h // 2, 128:256], kp[:, :, :], start=True, stop=True)\
                      .then_inc(S("swa_scores"), 1)
                rkvs(2, 3, 4, 5)
                need(pe, i, "swa_probs")
                for piece in range(3):
                    for h in range(4):
                        m = pe.transpose(bank[piece][:, h * P:(h + 1) * P], sc[:, h, piece * P:(piece + 1) * P],
                                         ident[:, :])
                m.then_inc(S("probs_turned"), 1)
                rkvs(6)
                need(pe, i, "pt_ready", "vg_ready")
                for e in range(2):
                    for q in range(2):
                        terms = [(0, o, 0) for o in range(2)] if q == 0 else \
                            [(blk, o, 1 + blk) for o in range(2) for blk in range(2)]
                        for n, (blk, o, piece) in enumerate(terms):
                            m = pe.matmul(b2[3][:, e, q * P:(q + 1) * P], vg[:, 2 * blk + o, :],
                                          pt[:, 4 * piece + 2 * e + o, :], start=n == 0, stop=n == len(terms) - 1)
                m.then_inc(S("swa_out"), 1)
                rkvs(7)
                need(pe, i, "swa_done")

            def mem(c, *js):
                for j in js:
                    if not (isinstance(c, int) and j >= 12):
                        mem_chunk(pe, "pe", c, 1 + j // 4, j % 4)

            def units(dst, lhs, rh, name):
                for u in range(UN):
                    m = pe.matmul(dst(u), lhs(u), rh(u), start=True, stop=True)
                m.then_inc(S(name), 1)

            def prepare(n, step):
                if step == 0:
                    need(pe, n, "tz_copied")
                    for h in range(2):
                        rows = slice(64 * h, 64 * h + 64)
                        for u in range(UN):
                            m = pe.matmul(b8[h][:, u, :], daw[rows, u * P:(u + 1) * P], tzc[rows, :],
                                          start=True, stop=True)
                    m.then_inc(S("lora_z"), 1)
                if step == 1:
                    need(pe, n, "kk_sq")
                    pe.matmul(bank[0], rc("same_head"), t2, start=True, stop=True).then_inc(S("kk_sum"), 1)

            def prod_b(n):
                need(pe, n, "B_scaled")
                units(lambda u: two[0][:, u, :], lambda u: Bh[:, u, :], lambda u: rhs[:, u, :], "B_prod")

            def prod_k(n):
                need(pe, n, "K_scaled")
                units(lambda u: two[1][:, u, :], lambda u: Kh[:, u, :], lambda u: rhs[:, u, :], "K_prod")

            def prod_a(n):
                need(pe, n, "Abd_ready", "Arb_ready")
                units(lambda u: two[0][:, u, :], lambda u: Abd[:, u, :], lambda u: Bh[:, u, :], "A_prod")

            def turn_b(n):
                need(pe, n, "Ark_ready")
                for u in range(UN):
                    m = pe.transpose(two[1][:, u, :], Bh[:, u, :], ident[:, :])
                m.then_inc(S("B_turned"), 1)

            def turn_k(n):
                need(pe, n, "A_ready")
                for u in range(UN):
                    m = pe.transpose(two[0][:, u, :], Kh[:, u, :], ident[:, :])
                m.then_inc(S("K_turned"), 1)

            def turn_v(n):
                need(pe, n, "BT_ready")
                units(lambda u: b8[2][:, u, :], lambda u: Pm[:, u, :], lambda u: rc("stack"), "V_turned")

            def solve(c, more):
                need(pe, c, "KT_ready", "Vc_ready", "Y_init")
                for n, b in enumerate(LEVELS):
                    pe.wait_ge(S("Am"), c * 5 + n + 1)
                    if n:
                        pe.wait_ge(S("Y_level"), c * 5 + n)
                        pe.wait_ge(S("X_level"), c * 4 + n)
                    if more and n == 1:
                        need(pe, c + 1, "z_a")
                    if more and n == 2:
                        need(pe, c + 1, "kk_norm")
                    units(lambda u: two[0][:, u, :], lambda u: Am[:, u, :], lambda u: Yi[:, u, :], "P_done")
                    mem_chunk(pe, "pe", c, 1 + n // 4, n % 4, range(0, KC // 2))
                    pe.wait_ge(S("P_ready"), c * 5 + n + 1)
                    units(lambda u: b8[2][:, u, :], lambda u: Xi[:, u, :], lambda u: odd(Pm[:, u, :], b, 1), "Y_more")
                    if n < 4:
                        units(lambda u: b8[3][:, u, :], lambda u: Pm[:, u, :], lambda u: odd(Xi[:, u, :], b, 0),
                              "X_more")
                    if more:
                        prepare(c + 1, n)
                    mem_chunk(pe, "pe", c, 1 + n // 4, n % 4, range(KC // 2, KC))

            def gate_products():
                pe.wait_ge(S("gup_landed"), 32)
                need(pe, 2, "pool_cleared")
                need(pe, TC - 1, "bonus", "y_var")
                for g in range(4):
                    for e in range(2):
                        u = 2 * g + e
                        pe.matmul(b2[g][:, e, :], gup[:, 0, u * P:(u + 1) * P], lora[:, 1, :], start=True, stop=False,
                                  skip_group_check=True)
                        m = pe.matmul(b2[g][:, e, :], gup[:, 1, u * P:(u + 1) * P], lora[:, 2, :], start=False, stop=True,
                                      skip_group_check=True)
                    m.then_inc(S("gate_done"), 1)

            def round_(c, more):
                solve(c, more)
                for u in range(UN):
                    pe.matmul(b8[0][:, u, :], Abd[:, u, :], Sc[:, u, :], start=True, stop=False, skip_group_check=True)
                    m = pe.matmul(b8[0][:, u, :], AakT[:, u, :], Vc[:, u, :], start=False, stop=True,
                                  skip_group_check=True)
                m.then_inc(S("R_done"), 1)
                mem(c, 5)
                need(pe, c, "R_ready")
                pe.wait_ge(S("Y_level"), c * 5 + 5)
                units(lambda u: b8[1][:, u, :], lambda u: Yi[:, u, :], lambda u: Rc[:, u, :], "U_done")
                mem(c, 6)
                need(pe, c, "Ubd_ready")
                for u in range(UN):
                    pe.matmul(b8[2][:, u, :], Sbd[:, u, :], rhs[:, u, 64:128], start=True, stop=False,
                              skip_group_check=True)
                    pe.matmul(b8[2][:, u, :], Vbd[:, u, :], ArkT[:, u, :], start=False, stop=False,
                              skip_group_check=True)
                    m = pe.matmul(b8[2][:, u, :], Ubd[:, u, :], ArbT[:, u, :], start=False, stop=True,
                                  skip_group_check=True)
                m.then_inc(S("y_done"), 1)
                for u in range(UN):
                    pe.matmul(b8[3][:, u, :], Bh[:, u, :], Uc[:, u, :], start=True, stop=False, skip_group_check=True)
                    m = pe.matmul(b8[3][:, u, :], Kh[:, u, :], Vc[:, u, :], start=False, stop=True,
                                  skip_group_check=True)
                m.then_inc(S("S_done"), 1)
                mem(c, 7)
                need(pe, c, "y_copied")
                pe.matmul(bank[0], rc("same_head"), cum, start=True, stop=True).then_inc(S("y_sum"), 1)
                need(pe, c, "rkr", "S_sum")
                pe.matmul(bank[3], rc("same_head"), Rc, start=True, stop=True).then_inc(S("bonus_sum"), 1)
                mem(c, 8)
                need(pe, c, "y_sq")
                pe.matmul(bank[1], rc("same_head"), t2, start=True, stop=True).then_inc(S("y_sqsum"), 1)
                if not more:
                    gate_products()
                if more:
                    mem(c, 9)
                    prod_b(c + 1)
                    mem(c, 10)
                    need(pe, c, "bonus")
                    prod_k(c + 1)
                    mem(c, 11)
                    prod_a(c + 1)
                    mem(c, 12)
                    turn_b(c + 1)
                    mem(c, 13)
                    turn_k(c + 1)
                    mem(c, 14)
                    turn_v(c + 1)
                    mem(c, 15)
                else:
                    mem(c, 9, 10, 11)
            def values(*js):
                for j in js:
                    rkv_chunk(pe, "pe", 0, j, 8)
            values(0, 1, 2, 3)
            pe.wait_ge(S("rw_tables"), 48)
            need(pe, 0, "lora_act")
            prepare(0, 0)
            values(4, 5)
            need(pe, 0, "z_a")
            prepare(0, 1)
            values(6, 7, 8, 9, 10, 11)
            need(pe, 0, "kk_norm")
            pe.wait_ge(S("rw_cleared"), 6)
            prod_k(0)
            prod_b(0)
            values(12, 13, 14)
            need(pe, 0, "Ark_ready")
            norm_pe(pe, MEM)
            values(15)
            mem_chunk(pe, "pe", 0, 0, 0)
            mem_chunk(pe, "pe", 0, 0, 1)
            mem_chunk(pe, "pe", 0, 0, 2)
            prod_a(0)
            pe.wait_ge(S("ms_eps"), MEM + 1)
            turn_b(0)
            turn_k(0)
            mem_chunk(pe, "pe", 0, 0, 3)
            turn_v(0)
            need(pe, 1, "pool_cleared")
            with pe.Fori(0, TC - 1) as c:
                round_(c, True)
            round_(TC - 1, False)
            def mixed(pe, j):
                pe.wait_ge(S("y_split"), (1, 2, 4, 6)[j])
            with pe.Fori(0, 4) as i:
                for u in range(2):
                    products(pe, B_OUT + u, V_OUT + 4 * u, 4, hs, mixed, i, 8, 2, first_tile=YT0, order=(2, 3, 0, 1))
            products(pe, B_XQ, V_XQ, 4, xs, filled(FILL_XA))
            norm_pe(pe, XA)
            with pe.Fori(0, 3) as i:
                for u in range(1, 3):
                    products(pe, B_XQ + u, V_XQ + 4 * u, 4, xs, None, i, 8, 2)
            products(pe, B_XQ + 7, V_XQ + 28, 4, xs)
            pe.wait_ge(S("kv_back"), 256)

            def x_scores(h):
                pe.wait_ge(S("xq_ready"), 2 * h + 2)
                if h >= 2:
                    pe.wait_ge(S("x_exp"), h - 1)
                for q in range(2):
                    for t in range(4):
                        m = pe.matmul(b2[h % 2][:, q, :], QX[:, 4 * h + t, q * P:(q + 1) * P], KX[:, 4 * h + t, :],
                                      start=t == 0, stop=t == 3)
                m.then_inc(S("x_scores"), 1)

            def x_turn(h):
                pe.wait_ge(S("x_normed"), h + 1)
                if h:
                    pe.wait_ge(S("o_split"), 2 * h)
                for q in range(2):
                    for t in range(2):
                        m = pe.transpose(b2[2][:, t, q * P:(q + 1) * P], SX[:, 2 * (h % 2) + q, t * P:(t + 1) * P],
                                         ident[:, :])
                m.then_inc(S("x_turned"), 1)

            def x_out(h):
                pe.wait_ge(S("x_probs"), h + 1)
                for g in range(2):
                    for e in range(2):
                        a = h * 512 + (2 * g + e) * P
                        for t in range(2):
                            m = pe.matmul(b2[3 - g][:, e, :], VX[:, t, a:a + P], PX[:, 2 * (h % 2) + t, :],
                                          start=t == 0, stop=t == 1)
                    m.then_inc(S("o_done"), 1)

            def attended(pe, j):
                pe.wait_ge(S("o_split"), 2 * (j + 1))

            def xo_chunk(j):
                chunk_products(pe, B_XO, V_XO, j, 4, hs, attended, first_tile=YT0)
            x_scores(0)
            x_scores(1)
            x_turn(0)
            x_scores(2)
            x_out(0)
            x_scores(3)
            for h in range(1, 4):
                x_turn(h)
                xo_chunk(h - 1)
                x_out(h)
            xo_chunk(3)
            products(pe, B_XO + 1, V_XO + 4, 4, hs, None, first_tile=YT0)
            with pe.Fori(0, 3) as i:
                for u in range(2, 4):
                    products(pe, B_XO + u, V_XO + 4 * u, 4, hs, None, i, 8, 2, first_tile=YT0)
            ffn_pe(pe, 1, B_UP2, V_UP2, V_DOWN2, F2, FILL_F2)
            with pe.Fori(0, 4) as i:
                for u in range(2):
                    products(pe, B_DOWN2 + u, V_DOWN2 + 12 * u, 11, hs, hidden(1), i, 24, 2)
            norm_pe(pe, FINAL)


def kernel(**inputs):
    import numpy as _np
    import concourse.bacc as _bacc
    from concourse import mybir as _mybir
    from concourse.bass_utils import run_bass_kernel_spmd as _run

    nc = _bacc.Bacc("TRN2", target_bir_lowering=False, num_devices=1)
    f = {k: _np.asarray(v) for k, v in inputs.items()}
    arrays, A = {}, {}

    def dram(name, a):
        arrays[name] = _np.ascontiguousarray(a)
        A[name] = nc.dram_tensor(name, a.shape, _mybir.dt.from_np(a.dtype), kind="ExternalInput").ap()

    def tiles(a):
        return a.reshape(-1, P).T
    mu = f["rw_mu"][0]
    columns_of = {
        "b_out": tiles(f["b_out"][0]), "b_q": tiles(f["b_in_attn"][0, :1024]), "b_kv": tiles(f["b_in_attn"][0, 1024:]),
        "mu": tiles(mu[:3 * C]), "mu_lora": tiles(mu[LORA_COL:LORA_COL + 256]),
        "mu_tail": tiles(mu[TAIL_COL:TAIL_COL + P]), "w0": tiles(f["rw_w0"][0]), "a0": tiles(f["rw_a0"][0]),
        "k_k": tiles(f["rw_k_k"][0]), "k_a": tiles(f["rw_k_a"][0]), "r_k": tiles(f["rw_r_k"][0]),
        "lnx_w": tiles(f["rw_lnx_w"][0]), "lnx_b": tiles(f["rw_lnx_b"][0]),
        "sinks": _np.broadcast_to(f["attn_sinks"][0], (P, 16)), "final_norm": tiles(f["final_norm"]),
    }
    for n in ("f1_norm", "mix_norm", "mem_norm", "xa_norm", "f2_norm"):
        columns_of[n] = tiles(f[n][0])
    dram("params", _np.concatenate([columns_of[n] for n, _ in PARAMS], axis=1))
    dram("swa_consts", swa_consts())
    dram("rw_consts", rw_consts())
    dram("ident", _np.eye(P, dtype=_np.float32))
    dram("x_t", f["x"][0].T)
    dram("mem_t", f["mem"][0].T)
    for n in ("f1_gate", "f1_up", "f1_down", "w_in", "w_out", "w_xq", "w_xkv", "w_xo", "f2_gate", "f2_up", "f2_down",
              "rw_decay_up", "rw_aaa_up", "rw_gate_up"):
        dram(n, f[n][0])
    out = nc.dram_tensor("out_t", (D, T), _mybir.dt.float32, kind="ExternalOutput").ap()
    build(nc, A, out)
    r = _run(nc, [arrays], core_ids=[0])
    return _np.ascontiguousarray(r.results[0]["out_t"].T).reshape(1, T, D)
```
